# Optimizing a Trainium2 kernel written in Bass

```python
import jax, jax.numpy as jnp
from jax import lax
import numpy as np

D_MODEL = 1024
BATCH = 1
SEQ = 256
DEPTH = 1

MIX_WIDTH = D_MODEL
GMLP_WIDTH = MIX_WIDTH // 2
RWKV_WIDTH = MIX_WIDTH - GMLP_WIDTH
HEAD_DIM = 64
GMLP_HEADS = GMLP_WIDTH // HEAD_DIM
RWKV_HEADS = RWKV_WIDTH // HEAD_DIM
CHUNK = 128
DECAY_LORA = 32
ICLR_LORA = 32
GATE_LORA = 96
RWKV_PROJ = 3 * RWKV_WIDTH + DECAY_LORA + ICLR_LORA + GATE_LORA
IN_WIDTH = 2 * GMLP_WIDTH + RWKV_PROJ
N_GROUPS = 4
EXPERTS_PER_GROUP = 8
N_EXPERTS = N_GROUPS * EXPERTS_PER_GROUP
TOP_K = 2
EXPERT_HIDDEN = 512
MOE_BLOCK = 128
RMS_EPS = 1e-6
LN_EPS = 1e-5
GN_EPS = 64e-5


def _rmsnorm(x, g):
    x32 = x.astype(jnp.float32)
    y = x32 * lax.rsqrt(jnp.mean(x32 * x32, axis=-1, keepdims=True) + RMS_EPS)
    return y.astype(x.dtype) * g

def _modulate(h, shift, scale):
    return h * (1 + scale[:, None, :]) + shift[:, None, :]

def _token_shift(z):
    return jnp.pad(z, ((0, 0), (1, 0), (0, 0)))[:, :-1]

def _gmlp_mixer(zu, zv, ln_w, ln_b, ws, bs):
    B, S, _ = zu.shape
    u = jax.nn.gelu(zu)
    v = jax.nn.gelu(zv)
    v32 = v.astype(jnp.float32)
    m = jnp.mean(v32, axis=-1, keepdims=True)
    var = jnp.mean(jnp.square(v32 - m), axis=-1, keepdims=True)
    v = ((v32 - m) * lax.rsqrt(var + LN_EPS)).astype(zu.dtype) * ln_w + ln_b
    vc = v.reshape(B, S // CHUNK, CHUNK, GMLP_HEADS, HEAD_DIM)
    w_causal = jnp.tril(ws)
    mixed = jnp.einsum('hts,bcshd->bcthd', w_causal, vc) + bs.T[None, None, :, :, None]
    return u * mixed.reshape(B, S, GMLP_WIDTH)

def _wkv7_scan(r, w, k, v, a, b):
    Bn, S, H, N = r.shape
    seq = tuple(jnp.moveaxis(t, 1, 0) for t in (r, w, k, v, a, b))

    def step(state, inp):
        r_t, w_t, k_t, v_t, a_t, b_t = inp
        sa = jnp.einsum('bhvk,bhk->bhv', state, a_t)
        state = (state * w_t[:, :, None, :] + sa[..., None] * b_t[:, :, None, :]
                 + v_t[..., None] * k_t[:, :, None, :])
        return state, jnp.einsum('bhvk,bhk->bhv', state, r_t)

    s0 = jnp.zeros((Bn, H, N, N), jnp.float32)
    _, y = lax.scan(step, s0, seq)
    return jnp.moveaxis(y, 0, 1)

def _rwkv7_mixer(z, mu, w0, w2, a0, a2, g2, k_k, k_a, r_k, gn_w, gn_b):
    B, S, _ = z.shape
    f32 = jnp.float32
    z = z + (_token_shift(z) - z) * mu
    W = RWKV_WIDTH
    r, k, v, xw, xa, xg = jnp.split(
        z, [W, 2 * W, 3 * W, 3 * W + DECAY_LORA, 3 * W + DECAY_LORA + ICLR_LORA], axis=-1)
    w_log = -jax.nn.softplus(-(w0 + jnp.tanh(xw) @ w2).astype(f32)) - 0.5
    decay = jnp.exp(-jnp.exp(w_log))
    a = jax.nn.sigmoid(a0 + xa @ a2)
    g = jax.nn.sigmoid(xg) @ g2
    hv = lambda t: t.reshape(B, S, RWKV_HEADS, HEAD_DIM)
    kk = hv(k * k_k).astype(f32)
    kk = kk / jnp.maximum(jnp.sqrt(jnp.sum(kk * kk, axis=-1, keepdims=True)), 1e-12)
    k = k * (1 + (a - 1) * k_a)
    r4, k4, v4, a4 = hv(r), hv(k), hv(v), hv(a)
    y = _wkv7_scan(r4.astype(f32), hv(decay), k4.astype(f32), v4.astype(f32),
                   -kk, kk * a4.astype(f32))
    m = jnp.mean(y, axis=-1, keepdims=True)
    var = jnp.mean(jnp.square(y - m), axis=-1, keepdims=True)
    y = ((y - m) * lax.rsqrt(var + GN_EPS)).reshape(B, S, W).astype(z.dtype) * gn_w + gn_b
    bonus = jnp.sum(r4 * k4 * r_k, axis=-1, keepdims=True) * v4
    return (y + bonus.reshape(B, S, W)) * g

def _hier_moe(h, rg_w, rg_b, re_w, re_b, w_gate, w_up, w_down):
    B, S, D = h.shape
    N = B * S
    f32 = jnp.float32
    ht = h.reshape(N, D)
    group_prob = jax.nn.softmax((ht @ rg_w + rg_b).astype(f32), axis=-1)
    g_p, g_idx = lax.top_k(group_prob, 1)
    exp_logits = (ht @ re_w + re_b).astype(f32).reshape(N, N_GROUPS, EXPERTS_PER_GROUP)
    sel = jnp.take_along_axis(exp_logits, g_idx[:, :, None], axis=1)[:, 0]
    e_p, e_idx = lax.top_k(jax.nn.softmax(sel, axis=-1), TOP_K)
    e_p = e_p / jnp.sum(e_p, axis=-1, keepdims=True)
    weights = g_p * e_p
    expert = g_idx * EXPERTS_PER_GROUP + e_idx
    A = N * TOP_K
    flat_e = expert.reshape(A)
    flat_w = weights.reshape(A)
    flat_tok = jnp.repeat(jnp.arange(N, dtype=jnp.int32), TOP_K)
    order = jnp.argsort(flat_e)
    se, stok, sw = flat_e[order], flat_tok[order], flat_w[order]
    counts = jnp.bincount(flat_e, length=N_EXPERTS)
    padded = (counts + MOE_BLOCK - 1) // MOE_BLOCK * MOE_BLOCK
    pad_end = jnp.cumsum(padded)
    pad_start = pad_end - padded
    start = jnp.cumsum(counts) - counts
    dest = pad_start[se] + jnp.arange(A) - start[se]
    n_blocks = -(-A // MOE_BLOCK) + N_EXPERTS
    P = n_blocks * MOE_BLOCK
    tok_buf = jnp.full((P,), N, jnp.int32).at[dest].set(stok)
    w_buf = jnp.zeros((P,), f32).at[dest].set(sw)
    block_e = jnp.minimum(
        jnp.searchsorted(pad_end, jnp.arange(n_blocks) * MOE_BLOCK, side='right'), N_EXPERTS - 1)
    x_pad = jnp.concatenate([ht, jnp.zeros((1, D), ht.dtype)], axis=0)
    xb = x_pad[tok_buf].reshape(n_blocks, MOE_BLOCK, D)

    def expert_block(args):
        xbk, e = args
        return (jax.nn.silu(xbk @ w_gate[e]) * (xbk @ w_up[e])) @ w_down[e]

    yb = lax.map(expert_block, (xb, block_e)).reshape(P, D)
    y = jnp.zeros((N + 1, D), yb.dtype).at[tok_buf].add(yb * w_buf[:, None].astype(yb.dtype))
    return y[:N].reshape(B, S, D)

def first_inputs(seed: int = 0) -> dict:
    key = jax.random.key(seed)
    ks = jax.random.split(key, 40)
    L, D = DEPTH, D_MODEL
    nrm = lambda k, shape, s: jax.random.normal(k, shape, jnp.float32) * s
    uni = lambda k, shape, lo, hi: jax.random.uniform(k, shape, jnp.float32, lo, hi)
    return {
        "x": nrm(ks[0], (BATCH, SEQ, D), 1.0),
        "c": nrm(ks[1], (BATCH, D), 1.0),
        "ada_w": nrm(ks[2], (L, D, 6 * D), 0.3 * D ** -0.5),
        "ada_b": nrm(ks[3], (L, 6 * D), 0.01),
        "norm1_g": 1.0 + nrm(ks[4], (L, D), 0.05),
        "w_in": nrm(ks[5], (L, D, IN_WIDTH), D ** -0.5),
        "gmlp_ln_w": 1.0 + nrm(ks[6], (L, GMLP_WIDTH), 0.05),
        "gmlp_ln_b": nrm(ks[7], (L, GMLP_WIDTH), 0.02),
        "gmlp_ws": nrm(ks[8], (L, GMLP_HEADS, CHUNK, CHUNK), CHUNK ** -0.5),
        "gmlp_bs": 1.0 + nrm(ks[9], (L, GMLP_HEADS, CHUNK), 0.1),
        "rwkv_mu": uni(ks[10], (L, RWKV_PROJ), 0.0, 1.0),
        "rwkv_w0": uni(ks[11], (L, RWKV_WIDTH), -6.0, 0.0),
        "rwkv_w2": nrm(ks[12], (L, DECAY_LORA, RWKV_WIDTH), 0.1),
        "rwkv_a0": nrm(ks[13], (L, RWKV_WIDTH), 0.5),
        "rwkv_a2": nrm(ks[14], (L, ICLR_LORA, RWKV_WIDTH), ICLR_LORA ** -0.5),
        "rwkv_g2": nrm(ks[15], (L, GATE_LORA, RWKV_WIDTH), GATE_LORA ** -0.5),
        "rwkv_k_k": 0.85 + nrm(ks[16], (L, RWKV_WIDTH), 0.05),
        "rwkv_k_a": 1.0 + nrm(ks[17], (L, RWKV_WIDTH), 0.05),
        "rwkv_r_k": nrm(ks[18], (L, RWKV_HEADS, HEAD_DIM), 0.1),
        "rwkv_gn_w": 1.0 + nrm(ks[19], (L, RWKV_WIDTH), 0.05),
        "rwkv_gn_b": nrm(ks[20], (L, RWKV_WIDTH), 0.02),
        "w_out": nrm(ks[21], (L, MIX_WIDTH, D), MIX_WIDTH ** -0.5),
        "norm2_g": 1.0 + nrm(ks[22], (L, D), 0.05),
        "router_group_w": nrm(ks[23], (L, D, N_GROUPS), D ** -0.5),
        "router_group_b": nrm(ks[24], (L, N_GROUPS), 0.01),
        "router_expert_w": nrm(ks[25], (L, D, N_EXPERTS), D ** -0.5),
        "router_expert_b": nrm(ks[26], (L, N_EXPERTS), 0.01),
        "moe_w_gate": nrm(ks[27], (L, N_EXPERTS, D, EXPERT_HIDDEN), D ** -0.5),
        "moe_w_up": nrm(ks[28], (L, N_EXPERTS, D, EXPERT_HIDDEN), D ** -0.5),
        "moe_w_down": nrm(ks[29], (L, N_EXPERTS, EXPERT_HIDDEN, D), EXPERT_HIDDEN ** -0.5),
        "final_norm_g": 1.0 + nrm(ks[30], (D,), 0.05),
    }

def first_block(x, c, ada_w, ada_b, norm1_g, w_in, gmlp_ln_w, gmlp_ln_b, gmlp_ws, gmlp_bs,
              rwkv_mu, rwkv_w0, rwkv_w2, rwkv_a0, rwkv_a2, rwkv_g2, rwkv_k_k, rwkv_k_a,
              rwkv_r_k, rwkv_gn_w, rwkv_gn_b, w_out, norm2_g, router_group_w, router_group_b,
              router_expert_w, router_expert_b, moe_w_gate, moe_w_up, moe_w_down,
              final_norm_g):
    for l in range(DEPTH):
        mod = c @ ada_w[l] + ada_b[l]
        shift1, scale1, gate1, shift2, scale2, gate2 = jnp.split(mod, 6, axis=-1)
        h = _modulate(_rmsnorm(x, norm1_g[l]), shift1, scale1)
        z = h @ w_in[l]
        zu, zv, zr = jnp.split(z, [GMLP_WIDTH, 2 * GMLP_WIDTH], axis=-1)
        y_a = _gmlp_mixer(zu, zv, gmlp_ln_w[l], gmlp_ln_b[l], gmlp_ws[l], gmlp_bs[l])
        y_b = _rwkv7_mixer(zr, rwkv_mu[l], rwkv_w0[l], rwkv_w2[l], rwkv_a0[l], rwkv_a2[l],
                           rwkv_g2[l], rwkv_k_k[l], rwkv_k_a[l], rwkv_r_k[l],
                           rwkv_gn_w[l], rwkv_gn_b[l])
        y = jnp.concatenate([y_a, y_b], axis=-1) @ w_out[l]
        x = x + gate1[:, None, :] * y
        h = _modulate(_rmsnorm(x, norm2_g[l]), shift2, scale2)
        y = _hier_moe(h, router_group_w[l], router_group_b[l], router_expert_w[l],
                      router_expert_b[l], moe_w_gate[l], moe_w_up[l], moe_w_down[l])
        x = x + gate2[:, None, :] * y
    return _rmsnorm(x, final_norm_g)


DEPTH_2 = 2

N_HEADS = 16
HEAD_DIM_2 = D_MODEL // N_HEADS
D_FF = ((8 * D_MODEL // 3 + 127) // 128) * 128
CONV_WIDTH = 3
Q_BLOCK = 128
N_MIXERS = 2
N_MOD = 6
N_SB_LAYERS = (DEPTH_2 + 1) // 2
N_FOX_LAYERS = DEPTH_2 // 2


def rmsnorm(x, g):
    xf = x.astype(jnp.float32)
    y = xf * lax.rsqrt(jnp.mean(xf * xf, axis=-1, keepdims=True) + RMS_EPS)
    return (y * g.astype(jnp.float32)).astype(x.dtype)

def modulate(h, shift, scale):
    return h * (1.0 + scale[:, None, :]) + shift[:, None, :]

def split_heads(t):
    b, s, _ = t.shape
    return t.reshape(b, s, N_HEADS, HEAD_DIM_2).transpose(0, 2, 1, 3)

def merge_heads(t):
    b, h, s, d = t.shape
    return t.transpose(0, 2, 1, 3).reshape(b, s, h * d)

def stick_breaking_attention(q, k, v):
    s_len = q.shape[2]
    scale = HEAD_DIM_2 ** -0.5
    outs = []
    for blk in range(s_len // Q_BLOCK):
        q0 = blk * Q_BLOCK
        k_end = q0 + Q_BLOCK
        qb, kb, vb = q[:, :, q0:k_end], k[:, :, :k_end], v[:, :, :k_end]
        z = jnp.einsum('bhqd,bhkd->bhqk', qb, kb).astype(jnp.float32) * scale
        t_idx = q0 + jnp.arange(Q_BLOCK)[:, None]
        s_idx = jnp.arange(k_end)[None, :]
        strict = s_idx < t_idx
        log_beta = jax.nn.log_sigmoid(z)
        log_1mb = jnp.where(strict, jax.nn.log_sigmoid(-z), 0.0)
        after = lax.cumsum(log_1mb, axis=3, reverse=True) - log_1mb
        a = jnp.where(strict, jnp.exp(log_beta + after), 0.0)
        outs.append(jnp.einsum('bhqk,bhkd->bhqd', a.astype(vb.dtype), vb))
    return jnp.concatenate(outs, axis=2)

def forgetting_attention(q, k, v, log_f):
    s_len = q.shape[2]
    scale = HEAD_DIM_2 ** -0.5
    cum = lax.cumsum(log_f, axis=2)
    outs = []
    for blk in range(s_len // Q_BLOCK):
        q0 = blk * Q_BLOCK
        k_end = q0 + Q_BLOCK
        qb, kb, vb = q[:, :, q0:k_end], k[:, :, :k_end], v[:, :, :k_end]
        z = jnp.einsum('bhqd,bhkd->bhqk', qb, kb).astype(jnp.float32) * scale
        decay = cum[:, :, q0:k_end, None] - cum[:, :, None, :k_end]
        t_idx = q0 + jnp.arange(Q_BLOCK)[:, None]
        s_idx = jnp.arange(k_end)[None, :]
        logits = jnp.where(s_idx <= t_idx, z + decay, -jnp.inf)
        p = jax.nn.softmax(logits, axis=-1)
        outs.append(jnp.einsum('bhqk,bhkd->bhqd', p.astype(vb.dtype), vb))
    return jnp.concatenate(outs, axis=2)

def causal_depthwise_conv(h, w, b):
    s_len = h.shape[1]
    hp = jnp.pad(h, ((0, 0), (CONV_WIDTH - 1, 0), (0, 0)))
    out = b[None, None, :]
    for kk in range(CONV_WIDTH):
        out = out + w[kk][None, None, :] * hp[:, kk:kk + s_len]
    return out

def second_inputs(seed: int = 0) -> dict:
    key = jax.random.key(seed)
    ks = jax.random.split(key, 20)
    f32 = jnp.float32
    d, f, h = D_MODEL, D_FF, N_HEADS

    def nrm(k, shape, s):
        return jax.random.normal(k, shape, f32) * s

    return {
        "x": nrm(ks[0], (BATCH, SEQ, d), 1.0),
        "c": nrm(ks[1], (BATCH, d), 1.0),
        "w_mod": nrm(ks[2], (DEPTH_2, d, N_MOD * d), 0.5 * d ** -0.5),
        "b_mod": nrm(ks[3], (DEPTH_2, N_MOD * d), 0.02),
        "g_mix_pre": 1.0 + nrm(ks[4], (DEPTH_2, d), 0.05),
        "g_mix_post": 1.0 + nrm(ks[5], (DEPTH_2, d), 0.05),
        "w_qkv": nrm(ks[6], (DEPTH_2, d, 3 * d), d ** -0.5),
        "w_o": nrm(ks[7], (DEPTH_2, d, d), d ** -0.5),
        "w_fg": nrm(ks[8], (N_FOX_LAYERS, d, h), d ** -0.5),
        "b_fg": 3.0 + nrm(ks[9], (N_FOX_LAYERS, h), 0.5),
        "g_ffn_pre": 1.0 + nrm(ks[10], (DEPTH_2, d), 0.05),
        "g_ffn_post": 1.0 + nrm(ks[11], (DEPTH_2, d), 0.05),
        "w_ffn_gate": nrm(ks[12], (DEPTH_2, d, f), d ** -0.5),
        "w_ffn_up": nrm(ks[13], (DEPTH_2, d, f), d ** -0.5),
        "w_conv": nrm(ks[14], (DEPTH_2, CONV_WIDTH, f), CONV_WIDTH ** -0.5),
        "b_conv": nrm(ks[15], (DEPTH_2, f), 0.02),
        "w_ffn_down": nrm(ks[16], (DEPTH_2, f, d), f ** -0.5),
    }

def second_block(x, c, w_mod, b_mod, g_mix_pre, g_mix_post, w_qkv, w_o, w_fg, b_fg,
              g_ffn_pre, g_ffn_post, w_ffn_gate, w_ffn_up, w_conv, b_conv, w_ffn_down):
    c_act = jax.nn.silu(c)
    for i in range(DEPTH_2):
        mod = jnp.einsum('bd,dm->bm', c_act, w_mod[i]) + b_mod[i]
        sh_a, sc_a, gt_a, sh_f, sc_f, gt_f = jnp.split(mod, N_MOD, axis=-1)

        h = modulate(rmsnorm(x, g_mix_pre[i]), sh_a, sc_a)
        qkv = jnp.einsum('bsd,de->bse', h, w_qkv[i])
        q, k, v = (split_heads(t) for t in jnp.split(qkv, 3, axis=-1))
        if i % N_MIXERS == 0:
            o = stick_breaking_attention(q, k, v)
        else:
            j = i // N_MIXERS
            f_logit = jnp.einsum('bsd,dh->bhs', h, w_fg[j]) + b_fg[j][None, :, None]
            log_f = jax.nn.log_sigmoid(f_logit.astype(jnp.float32))
            o = forgetting_attention(q, k, v, log_f)
        o = jnp.einsum('bse,ed->bsd', merge_heads(o), w_o[i])
        x = x + gt_a[:, None, :] * rmsnorm(o, g_mix_post[i])

        h = modulate(rmsnorm(x, g_ffn_pre[i]), sh_f, sc_f)
        gate = jnp.einsum('bsd,df->bsf', h, w_ffn_gate[i])
        up = jnp.einsum('bsd,df->bsf', h, w_ffn_up[i])
        gate = causal_depthwise_conv(gate, w_conv[i], b_conv[i])
        y = jnp.einsum('bsf,fd->bsd', jax.nn.silu(gate) * up, w_ffn_down[i])
        x = x + gt_f[:, None, :] * rmsnorm(y, g_ffn_post[i])
    return x


def setup_inputs(seed=0):
    out = dict(first_inputs(seed))
    for name, value in second_inputs(seed + 1).items():
        if name != "x":
            out[name + "_2"] = value
    return out


def reference(
    x, c, ada_w, ada_b, norm1_g, w_in, gmlp_ln_w, gmlp_ln_b, gmlp_ws, gmlp_bs, rwkv_mu, rwkv_w0,
    rwkv_w2, rwkv_a0, rwkv_a2, rwkv_g2, rwkv_k_k, rwkv_k_a, rwkv_r_k, rwkv_gn_w, rwkv_gn_b,
    w_out, norm2_g, router_group_w, router_group_b, router_expert_w, router_expert_b,
    moe_w_gate, moe_w_up, moe_w_down, final_norm_g, c_2, w_mod_2, b_mod_2, g_mix_pre_2,
    g_mix_post_2, w_qkv_2, w_o_2, w_fg_2, b_fg_2, g_ffn_pre_2, g_ffn_post_2, w_ffn_gate_2,
    w_ffn_up_2, w_conv_2, b_conv_2, w_ffn_down_2,
):
    x = first_block(
        x, c, ada_w, ada_b, norm1_g, w_in, gmlp_ln_w, gmlp_ln_b, gmlp_ws, gmlp_bs, rwkv_mu,
        rwkv_w0, rwkv_w2, rwkv_a0, rwkv_a2, rwkv_g2, rwkv_k_k, rwkv_k_a, rwkv_r_k, rwkv_gn_w,
        rwkv_gn_b, w_out, norm2_g, router_group_w, router_group_b, router_expert_w,
        router_expert_b, moe_w_gate, moe_w_up, moe_w_down, final_norm_g,
    )
    return second_block(
        x, c_2, w_mod_2, b_mod_2, g_mix_pre_2, g_mix_post_2, w_qkv_2, w_o_2, w_fg_2, b_fg_2,
        g_ffn_pre_2, g_ffn_post_2, w_ffn_gate_2, w_ffn_up_2, w_conv_2, b_conv_2, w_ffn_down_2,
    )


_drawn_inputs = setup_inputs


def setup_inputs(seed=0):
    import zlib

    import numpy as np

    out = dict(_drawn_inputs(seed))
    spreads = {}
    factors = {'ada_b': 3.933,
     'norm1_g': 2.835,
     'gmlp_ln_w': 6.356,
     'gmlp_ln_b': 8.0,
     'gmlp_bs': 2.789,
     'rwkv_w2': 5.931,
     'rwkv_k_k': 39.128,
     'rwkv_k_a': 4.669,
     'rwkv_gn_w': 6.802,
     'rwkv_gn_b': 47.864,
     'norm2_g': 3.02,
     'router_group_b': 8.0,
     'router_expert_b': 8.0,
     'g_mix_post_2': 2.745,
     'g_ffn_post_2': 2.895,
     'b_conv_2': 7.998}
    for name, (base, spread) in spreads.items():
        noise = np.random.default_rng([zlib.crc32(name.encode()), seed]).standard_normal(out[name].shape)
        drawn = base * np.exp(spread * noise) if base else spread * noise
        out[name] = __import__('jax').numpy.asarray(drawn.astype(out[name].dtype))
    for name, factor in factors.items():
        out[name] = (out[name] * factor).astype(out[name].dtype)
    return out
```

```python
from contextlib import ExitStack

import numpy as np

import concourse.bass as bass
from concourse import mybir

F32 = mybir.dt.float32
I32 = mybir.dt.int32
U32 = mybir.dt.uint32
ALU = mybir.AluOpType
ACT = mybir.ActivationFunctionType
AX = mybir.AxisListType

P = 128
D = 1024
TOK = 256
NT = TOK // P
DC = D // P
HALF = 512
NM = HALF // P
HD = 64
NHR = HALF // HD
CH = 64
NE, HID = 32, 512
NG, EPG = 4, 8
WIN = 64
SLOTS = 2 * TOK
NHA = 16
FF = 2816
NFT = FF // P
RING = 6
SLOTF = 4096
RMS_EPS, LN_EPS, GN_EPS = 1e-6, 1e-5, 64e-5
DECAY = float(np.exp(-0.5))
NEG = -1e30

COLS = {}
_n = 0
for _name, _w in [("c1", 8), ("ada_b", 48), ("norm1_g", 8), ("mu_rkv", 12), ("mu_wa", 1), ("mu_g", 1),
                  ("w0", 4), ("a0", 4), ("k_k", 4), ("k_a", 4), ("r_k", 4), ("gn_w", 4), ("gn_b", 4),
                  ("norm2_g", 8), ("c2", 8), ("b_mod0", 48), ("b_mod1", 48), ("g_mix_pre", 16),
                  ("g_mix_post", 16), ("g_ffn_pre", 16), ("g_ffn_post", 16), ("w_conv", 132),
                  ("b_conv", 44), ("b_fg", 1)]:
    COLS[_name] = (_n, _w)
    _n += _w
NCOL = _n


class Sems:

    def __init__(self, nc, ctx):
        self.nc, self.ctx, self.made = nc, ctx, {}

    def __call__(self, name):
        if name not in self.made:
            self.made[name] = self.ctx.enter_context(self.nc.semaphore(name))
        return self.made[name]


class Chain:

    def __init__(self, eng, named, name):
        self.eng, self.named, self.sem, self.n, self.told = eng, named, named(name), 0, {}

    def __call__(self, ins):
        self.n += 1
        ins.then_inc(self.sem, 1)
        self.eng.wait_ge(self.sem, self.n)

    def to(self, ins, name):
        self.told[name] = self.told.get(name, 0) + 1
        ins.then_inc(self.named(name), 1)
        self.eng.wait_ge(self.named(name), self.told[name])


class Stream:

    def __init__(self):
        self.n = 0

    def take(self):
        n = self.n
        self.n += 1
        return n % RING, n // RING + 1, n


def build_program(nc, a):
    with ExitStack() as ctx:
        S = Sems(nc, ctx)

        def sb(name, shape, dt=F32):
            return ctx.enter_context(nc.sbuf_tensor(name, shape, dt))

        psum = ctx.enter_context(nc.psum_tensor("psum", [P, 8, 512], F32))
        bank = [psum[:, i, :] for i in range(8)]
        ring = sb("ring", [P, RING, SLOTF])
        AR = 23040
        arena = sb("arena", [P, AR])

        def at(off, *shape):
            n = int(np.prod(shape))
            assert off + n <= AR
            v = arena[:, off:off + n]
            if len(shape) == 1:
                return v
            names = "abcd"[:len(shape)]
            return v.rearrange(f"p ({' '.join(names)}) -> p {' '.join(names)}",
                               **{k: s for k, s in zip(names, shape)})

        x = sb("x", [P, NT, D])
        cols = sb("cols", [P, NCOL])
        ident = sb("ident", [P, P])
        ones = sb("ones", [P, P])
        bones = sb("bones", [P, P])
        upper = sb("upper", [P, P])
        upper_inc = sb("upper_inc", [P, P])
        mask_ar = sb("mask_ar", [P, 2, P])
        level = sb("level", [P, 6, P])
        keep1 = sb("keep1", [NHA, TOK])
        keep = sb("keep", [P, TOK])
        modc = sb("modc", [P, 3, 48])
        small = sb("small", [P, 96])
        omm = small[:, 0:14]
        omka = small[:, 14:18]
        stat = small[:, 18:34]
        negone = small[:, 34:35]
        onecol = small[:, 35:36]
        gneps = small[:, 36:37]
        powh = small[:, 38:40]
        fcol = small[:, 40:48]
        dend = small[:, 48:64].rearrange("p (m c) -> p m c", m=NM)
        silc = small[:, 64:72]
        spare = small[:, 72:80]
        mtab = sb("mtab", [1, 3 * NE + 1], I32)

        def col(name, i=0, n=1):
            o = COLS[name][0] + i
            return cols[:, o:o + n]

        hT = at(0, DC, TOK)
        xn = at(2048, NT, D)
        gv = at(2048, NT, HALF)
        wsT = at(3072, NHR, P)
        rT, kT, vT = at(4096, NM, TOK), at(5120, NM, TOK), at(6144, NM, TOK)
        xwa, xg = at(7168, TOK), at(7424, TOK)
        sw, cum = at(7680, NM, TOK), at(8704, NM, TOK)
        aT, eL = at(9728, NM, TOK), at(10752, NM, TOK)
        kkn, tmp1, tmp2 = at(11776, NM, TOK), at(12800, NM, TOK), at(13824, NM, TOK)
        tokv, tokb, tokk = at(0, NT, HALF), at(1024, NT, HALF), at(2048, NT, HALF)
        gram = at(3072, 16, 512)
        Xi = at(11264, 8, P)
        XT = at(12288, 16, P)
        Pm = at(14336, 2, 4, P)
        Pb = at(15360, 512)
        arT = at(15872, 2, NM, TOK)
        bkT = at(17920, 2, NM, TOK)
        lora = at(15872, 512)
        g2s = at(16384, 512)
        lnw, lnb = at(17920, 512), at(18432, 512)
        bsb = at(18944, NM, P)
        U = at(17920, NT, 512)
        Mst = at(18944, NM, P)
        DCm = at(19456, NM, P)
        gT, bonus, yaT = at(19968, NM, TOK), at(20992, NM, TOK), at(22016, NM, TOK)
        ybT = at(3072, NM, TOK)
        yv, yd, ysq = at(4096, NM, TOK), at(5120, NM, TOK), at(6144, NM, TOK)

        h2 = at(0, NT, D)
        h2T = at(2048, DC, TOK)
        perm = at(4096, NT, SLOTS)
        pw = at(5120, NT, SLOTS)
        pwT = at(6144, 4, TOK)
        xsT = at(7168, DC, SLOTS + WIN)
        ysT = at(11776, DC, SLOTS + WIN)
        actT = at(16384, 2, P)
        sg = at(16640, 4 * WIN)
        xw = at(17920, DC, WIN)
        ym = at(18432, 512)
        actm = at(18944, 4 * WIN)
        gate2b = at(16896, D)
        sc2b, sh2b = at(17920, D), at(18944, D)
        gate1b = at(19968, D)
        fgb = at(20992, D)
        rt = at(22016, 1024)
        iota = at(11776, SLOTS)
        diag = at(12288, DC, P)
        rw = at(13312, DC, 36)
        rb = at(13600, 36)
        ys = at(0, 4, D)

        hTd = at(0, DC, TOK)
        QT, KT, Vd = at(2048, DC, TOK), at(4096, DC, TOK), at(6144, NT, D)
        oT = at(8192, DC, TOK)
        yt = at(10240, NT, D)
        gmixb, gffnb = at(12288, D), at(13312, D)
        diagd = at(14336, DC, P)
        t1 = at(15360, 2, 2, 384)
        sp_ = at(16896, 2, 2, 384)
        pr = at(18432, 2, 2, 384)
        cumf = at(19968, TOK)
        ncumf = at(20224, TOK)
        wfg = at(20480, DC, NHA)
        neg_lower = at(20608, P)
        neg_ones = at(20736, P)
        neg_ge = at(20864, P)
        neg_gt = at(20992, P)
        actF = at(15360, 2, 2, TOK)
        cv = at(16896, 2, TOK)
        sv = at(17920, 2, TOK)

        st_sp = Stream()
        st_pe = Stream()

        def w_cols(w, c0, n=512):
            return w[:, c0:c0 + n].rearrange("(c p) n -> p c n", p=P)

        block = ctx.enter_context(nc.Block())

        @block.sync
        def _(sp):
            def load(src, n):
                s, _, i = st_sp.take()
                if i >= RING:
                    sp.wait_ge(S("slot_freed"), i - RING + 1)
                sp.dma_start(ring[:, s, 0:n].rearrange("p (c n) -> p c n", c=src.shape[1]), src)\
                    .then_inc(S(f"slot{s}_loaded"), 16)

            sp.dma_start(cols[:, :], a["cols"]).then_inc(S("cols_in"), 16)
            sp.dma_start(x[:, :, :], a["x"].rearrange("(t p) d -> p t d", p=P)).then_inc(S("x_in"), 16)
            for i in range(4):
                load(w_cols(a["ada_w"], 512 * i), 4096)
            sp.dma_start(lora[0:64, :], a["lora"]).then_inc(S("lora_in"), 16)
            sp.dma_start(g2s[0:96, :], a["g2"]).then_inc(S("lora_in"), 16)
            sp.dma_start(lnw, a["ln_w"].partition_broadcast(P)).then_inc(S("ln_in"), 16)
            sp.dma_start(lnb, a["ln_b"].partition_broadcast(P)).then_inc(S("ln_in"), 16)
            for half in range(2):
                sp.dma_start(bsb[64 * half:64 * half + 64, :, :],
                             a["bs"][half].partition_broadcast(64)).then_inc(S("ln_in"), 16)
            for i in range(3):
                load(w_cols(a["w_in"], D + 512 * i), 4096)
            load(w_cols(a["w_in"], D + 3 * HALF, 160), 1280)
            load(w_cols(a["w_in"], HALF), 4096)
            load(w_cols(a["w_in"], 0), 4096)
            sp.wait_ge(S("turned"), 4)
            sp.dma_start(wsT, a["ws"]).then_inc(S("ws_in"), 16)
            for i in range(4, 12):
                load(w_cols(a["ada_w"], 512 * i), 4096)
            for i in range(12):
                load(w_cols(a["w_mod0"], 512 * i), 4096)
            for i in range(2):
                load(w_cols(a["w_out"], 512 * i), 4096)
            sp.wait_ge(S("x1_ready"), 2)
            sp.dma_start(fgb, a["final_g"].partition_broadcast(P)).then_inc(S("router_in"), 16)
            sp.dma_start(rw, a["router_w"].rearrange("(c p) n -> p c n", p=P)).then_inc(S("router_in"), 16)
            sp.dma_start(rb, a["router_b"].partition_broadcast(P)).then_inc(S("router_in"), 16)
            moe_n0 = st_sp.n
            with sp.Fori(0, NE // 2, 1) as i:
                for e in range(2):
                    for k, w in enumerate(("moe_gate", "moe_up", "moe_down")):
                        n = moe_n0 + 3 * e + k
                        s = n % RING
                        sp.wait_ge(S("slot_freed"), i * RING + (n - RING + 1))
                        src = a[w][bass.ds(i * 2 + e, 1), :, :].rearrange("o (c p) n -> p (o c) n", p=P)
                        sp.dma_start(ring[:, s, :].rearrange("p (c n) -> p c n", c=src.shape[1]), src)\
                            .then_inc(S(f"slot{s}_loaded"), 16)
            st_sp.n += 3 * NE
            for layer in range(2):
                for i in range(6):
                    load(w_cols(a[f"w_qkv{layer}"], 512 * i), 4096)
                if layer == 0:
                    sp.wait_ge(S("x2_ready"), 2)
                    sp.dma_start(wfg, a["w_fg"].rearrange("(c p) n -> p c n", p=P)).then_inc(S("fg_in"), 16)
                    for i in range(12):
                        load(w_cols(a["w_mod1"], 512 * i), 4096)
                for i in range(2):
                    load(w_cols(a[f"w_o{layer}"], 512 * i), 4096)
                n0 = st_sp.n
                wg, wu, wd = (a[f"w_ffn_{k}{layer}"] for k in ("gate", "up", "down"))

                def ffn_group(g, w, n, i):
                    wide = bass.ds(g * 512, w)
                    for k, src in enumerate((wg[:, wide].rearrange("(c p) n -> p c n", p=P),
                                             wu[:, wide].rearrange("(c p) n -> p c n", p=P),
                                             wd[wide, :].rearrange("(c p) n -> p c n", p=P))):
                        s = (n + k) % RING
                        sp.wait_ge(S("slot_freed"), i * RING + (n + k - RING + 1))
                        sp.dma_start(ring[:, s, 0:8 * w].rearrange("p (c n) -> p c n", c=src.shape[1]), src)\
                            .then_inc(S(f"slot{s}_loaded"), 16)

                ffn_group(0, 512, n0, 0)
                with sp.Fori(0, 2, 1) as i:
                    for k in range(2):
                        ffn_group(i * 2 + (1 + k), 512, n0 + 3 + 3 * k, i)
                ffn_group(5, 256, n0 + 15, 0)
                st_sp.n += 18
            sp.wait_ge(S("out_ready"), 2)
            sp.dma_start(a["out"].rearrange("(t p) d -> p t d", p=P), x[:, :, :]).then_inc(S("out_stored"), 16)
            sp.wait_ge(S("out_stored"), 16)

        @block.gpsimd
        def _(pool):
            g = Chain(pool, S, "pool_step")
            nc.gpsimd.memset(small[:, 34:35], -1.0)
            nc.gpsimd.memset(onecol, 1.0)
            nc.gpsimd.memset(gneps, GN_EPS)
            g(nc.gpsimd.memset(powh, -0.5))
            nc.gpsimd.memset(ones[:, :], 1.0).then_inc(S("consts"), 1)
            g(nc.gpsimd.memset(ident[:, :], 0.0))
            nc.gpsimd.affine_select(out=ident[:, :], in_=ident[:, :], compare_op=ALU.not_equal, fill=1.0, base=0,
                                    pattern=[[-1, P]], channel_multiplier=1).then_inc(S("consts"), 1)

            def rsqrt_of(n):
                pool.wait_ge(S("ms_ready"), n)
                nc.gpsimd.tensor_tensor(stat[:, 2:4], stat[:, 0:2], powh, ALU.pow).then_inc(S("rstd_ready"), 1)

            rsqrt_of(1)
            pool.wait_ge(S("consts"), 2)
            g(nc.gpsimd.affine_select(out=bones[:, 0:64], in_=ones[:, 0:64], compare_op=ALU.is_ge, fill=0.0, base=63,
                                      pattern=[[0, 64]], channel_multiplier=-1))
            nc.gpsimd.affine_select(out=bones[:, 64:128], in_=ones[:, 64:128], compare_op=ALU.is_ge, fill=0.0,
                                    base=-64, pattern=[[0, 64]], channel_multiplier=1).then_inc(S("bones_made"), 1)
            for t_, cmp in ((upper[:, :], ALU.is_gt), (upper_inc[:, :], ALU.is_ge)):
                nc.gpsimd.affine_select(out=t_, in_=ones[:, :], compare_op=cmp, fill=0.0, base=0,
                                        pattern=[[1, P]], channel_multiplier=-1).then_inc(S("upper_made"), 1)
            pool.wait_ge(S("bones_made"), 1)
            pool.wait_ge(S("upper_made"), 2)
            nc.gpsimd.tensor_tensor(mask_ar[:, 0, :], bones[:, :], upper[:, :], ALU.mult).then_inc(S("masks_made"), 1)
            nc.gpsimd.tensor_tensor(mask_ar[:, 1, :], bones[:, :], upper_inc[:, :], ALU.mult).then_inc(S("masks_made"), 1)
            nc.gpsimd.memset(keep[:, :], 1.0).then_inc(S("keep_set"), 1)
            pool.wait_ge(S("keep_set"), 1)
            nc.gpsimd.memset(keep[:, :].rearrange("p (c t) -> p c t", t=CH)[:, :, 0:1], 0.0)\
                .then_inc(S("masks_made"), 1)
            g(nc.gpsimd.memset(keep1[:, :], 1.0))
            g(nc.gpsimd.memset(level[:, :, :], 0.0))
            for l in range(6):
                b = 1 << l
                v = level[:, l, :].rearrange("p (q u b) -> p q u b", u=2, b=b)[:, :, 0, :]
                n = P // (2 * b)
                g(nc.gpsimd.memset(v, 1.0))
                g(nc.gpsimd.affine_select(out=v, in_=v, compare_op=ALU.is_ge, fill=0.0, base=-b,
                                          pattern=[[-2 * b, n], [0, b]], channel_multiplier=1))
                g(nc.gpsimd.affine_select(out=v, in_=v, compare_op=ALU.is_ge, fill=0.0, base=2 * b - 1,
                                          pattern=[[2 * b, n], [0, b]], channel_multiplier=-1))
            pool.nop().then_inc(S("levels_made"), 1)
            pool.wait_ge(S("ws_in"), 16)
            nc.gpsimd.affine_select(out=wsT, in_=wsT, compare_op=ALU.is_ge, fill=0.0, base=0,
                                    pattern=[[0, NHR], [1, P]], channel_multiplier=-1).then_inc(S("ws_masked"), 1)
            rsqrt_of(2)
            rsqrt_of(3)
            pool.wait_ge(S("x1_ready"), 2)
            nc.gpsimd.iota(iota, pattern=[[1, SLOTS]], base=0, channel_multiplier=0,
                           allow_small_or_imprecise_dtypes=True).then_inc(S("iota_made"), 1)
            g(nc.gpsimd.memset(xsT[:, :, SLOTS:SLOTS + WIN], 0.0))
            pool.nop().then_inc(S("iota_made"), 1)
            rsqrt_of(4)
            pool.wait_ge(S("x2_ready"), 2)
            g(nc.gpsimd.memset(neg_lower, -1.0))
            nc.gpsimd.memset(neg_ones, -1.0)
            nc.gpsimd.memset(neg_ge, NEG)
            g(nc.gpsimd.memset(neg_gt, NEG))
            nc.gpsimd.affine_select(out=neg_lower, in_=neg_lower, compare_op=ALU.is_ge, fill=0.0, base=0,
                                    pattern=[[-1, P]], channel_multiplier=1).then_inc(S("neg_made"), 1)
            nc.gpsimd.affine_select(out=neg_ge, in_=neg_ge, compare_op=ALU.is_ge, fill=0.0, base=0,
                                    pattern=[[-1, P]], channel_multiplier=1).then_inc(S("neg_made"), 1)
            nc.gpsimd.affine_select(out=neg_gt, in_=neg_gt, compare_op=ALU.is_gt, fill=0.0, base=0,
                                    pattern=[[1, P]], channel_multiplier=-1).then_inc(S("neg_made"), 1)
            for n in range(8):
                rsqrt_of(5 + n)

        @block.tensor
        def _(pe):
            mm = nc.tensor.matmul

            def take():
                s, use, n = st_pe.take()
                pe.wait_ge(S(f"slot{s}_loaded"), 16 * use)
                fresh[0] = n > 0 and not ahead[0]
                ahead[0] = False
                return ring[:, s, :]

            fresh = [False]
            ahead = [False]

            def opened(ins):
                if fresh[0]:
                    fresh[0] = False
                    ins.then_inc(S("slot_freed"), 1)

            def mod_slot(j, vec, o):
                w = take()[:, 0:4096].rearrange("p (c n) -> p c n", c=DC)
                for q in range(4):
                    for c in range(DC):
                        last = mm(bank[0][:, o + 4 * j + q:o + 4 * j + q + 1], w[:, c, q * P:(q + 1) * P],
                                  vec[:, c:c + 1], start=(c == 0), stop=(c == DC - 1))
                        opened(last)
                if j in (3, 11):
                    last.then_inc(S("mod_done"), 1)

            def turn(src, n):
                pe.wait_ge(S("xn_ready"), 2 * n)
                for u in range(4):
                    if n > 1:
                        pe.wait_ge(S("banks14_free"), n - 1)
                    for cc in range(2):
                        for t in range(NT):
                            last = nc.tensor.transpose(bank[1 + u][:, (2 * cc + t) * P:(2 * cc + t + 1) * P],
                                                       src[:, t, (2 * u + cc) * P:(2 * u + cc + 1) * P], ident[:, :])
                    last.then_inc(S("turned"), 1)

            pe.wait_ge(S("cols_in"), 16)
            pe.wait_ge(S("consts"), 2)
            for j in range(4):
                mod_slot(j, col("c1", 0, 8), 0)
            turn(xn, 1)
            pe.wait_ge(S("h_ready_v"), 4)
            pe.wait_ge(S("h_ready_s"), 4)
            unit = 0
            UB = [1, 2, 3, 4, 5, 6]
            for q in range(3):
                w = take()[:, 0:4096].rearrange("p (c n) -> p c n", c=DC)
                for half in range(2):
                    if unit >= 6:
                        pe.wait_ge(S("unit_free"), unit - 5)
                    b = bank[UB[unit % 6]]
                    for mi in range(2):
                        m = 2 * half + mi
                        for c in range(DC):
                            last = mm(b[:, mi * TOK:(mi + 1) * TOK], w[:, c, m * P:(m + 1) * P], hT[:, c, :],
                                      start=(c == 0), stop=(c == DC - 1))
                            opened(last)
                    last.then_inc(S("unit_ready"), 1)
                    unit += 1
            w = take()[:, 0:1280].rearrange("p (c n) -> p c n", c=DC)
            pe.wait_ge(S("unit_free"), unit - 5)
            b = bank[UB[unit % 6]]
            for c in range(DC):
                opened(mm(b[0:64, 0:TOK], w[:, c, 0:64], hT[:, c, :], start=(c == 0), stop=(c == DC - 1)))
            for c in range(DC):
                last = mm(b[0:96, TOK:2 * TOK], w[:, c, 64:160], hT[:, c, :], start=(c == 0), stop=(c == DC - 1))
            last.then_inc(S("unit_ready"), 1)
            unit += 1
            w = take()[:, 0:4096].rearrange("p (c n) -> p c n", c=DC)
            for t in range(NT):
                pe.wait_ge(S("unit_free"), unit - 5)
                b = bank[UB[unit % 6]]
                for c in range(DC):
                    last = mm(b[:, :], hT[:, c, t * P:(t + 1) * P], w[:, c, :], start=(c == 0), stop=(c == DC - 1))
                    opened(last)
                last.then_inc(S("unit_ready"), 1)
                unit += 1
            w = take()[:, 0:4096].rearrange("p (c n) -> p c n", c=DC)
            for half in range(2):
                pe.wait_ge(S("unit_free"), unit - 5)
                b = bank[UB[unit % 6]]
                for mi in range(2):
                    m = 2 * half + mi
                    for c in range(DC):
                        last = mm(b[:, mi * TOK:(mi + 1) * TOK], w[:, c, m * P:(m + 1) * P], hT[:, c, :],
                                  start=(c == 0), stop=(c == DC - 1))
                        opened(last)
                last.then_inc(S("unit_ready"), 1)
                unit += 1

            mods = iter([(4 + j, "c1") for j in range(8)] + [(j, "c2") for j in range(12)])

            def fill(n=1):
                for _ in range(n):
                    j, v = next(mods, (None, None))
                    if j is None:
                        return
                    if v == "c2" and j == 0:
                        pe.wait_ge(S("silu_c"), 1)
                    if (v, j) in (("c1", 4), ("c2", 0)):
                        pe.wait_ge(S("mod_copied"), 1 if v == "c1" else 2)
                    if v == "c1":
                        mod_slot(j, col("c1", 0, 8), 0)
                    else:
                        mod_slot(j, silc, 64)

            pe.wait_ge(S("unit_free"), 7)
            pe.wait_ge(S("gelu_done"), 4)
            pe.wait_ge(S("lora_in"), 32)
            pe.wait_ge(S("lowrank_ready"), 2)
            for half in range(2):
                for mi in range(2):
                    m = 2 * half + mi
                    ms = slice(m * P, (m + 1) * P)
                    o = slice(mi * TOK, (mi + 1) * TOK)
                    mm(bank[1 + half][:, o], lora[0:32, ms], xwa[0:32, :], start=True, stop=True)
                for mi in range(2):
                    m = 2 * half + mi
                    ms = slice(m * P, (m + 1) * P)
                    o = slice(mi * TOK, (mi + 1) * TOK)
                    mm(bank[3 + half][:, o], lora[32:64, ms], xwa[32:64, :], start=True, stop=True)
                for mi in range(2):
                    m = 2 * half + mi
                    ms = slice(m * P, (m + 1) * P)
                    o = slice(mi * TOK, (mi + 1) * TOK)
                    last = mm(bank[5 + half][:, o], g2s[0:96, ms], xg[0:96, :], start=True, stop=True)
                last.then_inc(S("lora_done"), 1)
            fill(2)
            pe.wait_ge(S("bones_made"), 1)
            pe.wait_ge(S("kk_sq"), 1)
            pe.wait_ge(S("sw_ready"), 4)
            for half in range(2):
                mm(bank[7][:, 0:512] if half else bank[1][:, 0:512], bones[:, :],
                   tmp1[:, 2 * half:2 * half + 2, :], start=True, stop=True).then_inc(S("kk_sums"), 1)
            fill(2)
            pe.wait_ge(S("ws_masked"), 1)
            pe.wait_ge(S("gv_ready"), 2)
            pe.wait_ge(S("a_ready"), 4)
            for m in range(NM):
                for hh in range(2):
                    for t in range(NT):
                        last = mm(bank[3 + m // 2][64 * hh:64 * hh + 64, ((m % 2) * 2 + t) * P:((m % 2) * 2 + t + 1) * P],
                                  gv[:, t, (2 * m + hh) * HD:(2 * m + hh + 1) * HD], wsT[:, 2 * m + hh, :],
                                  start=True, stop=True)
                if m % 2:
                    last.then_inc(S("mixed"), 1)
            fill(2)
            pe.wait_ge(S("bonus_in"), 1)
            pe.wait_ge(S("g_ready"), 2)
            for half in range(2):
                mm(bank[5 + half][:, 0:512], bones[:, :], tmp2[:, 2 * half:2 * half + 2, :],
                   start=True, stop=True).then_inc(S("bonus_sums"), 1)
            fill(1)
            pe.wait_ge(S("bk_ready"), 1)
            for q in range(3):
                for t in range(NT):
                    b = bank[1 + 2 * q + t]
                    if q == 1 and t == 0:
                        pe.wait_ge(S("ya_ready"), 1)
                    if q == 2 and t == 0:
                        pe.wait_ge(S("bonus_ready"), 2)
                    for m in range(NM):
                        src = vT if q == 0 else bkT[:, q - 1]
                        last = nc.tensor.transpose(b[:, m * P:(m + 1) * P], src[:, m, t * P:(t + 1) * P], ident[:, :])
                    last.then_inc(S("tok_turned"), 1)
            fill(1)
            pe.wait_ge(S("tok_copied"), 4)
            pe.wait_ge(S("tokb_copied"), 2)
            for i in range(16):
                T, h = i // 8, i % 8
                m, pb = h // 2, 64 * (h % 2)
                if i >= 6:
                    pe.wait_ge(S("gram_copied"), i - 5)
                b = bank[[1, 3, 2, 4, 7, 5][i % 6]]
                for q in range(2):
                    last = mm(b[:, q * 256:(q + 1) * 256].rearrange("p (w t) -> p w t", w=2),
                              bkT[pb:pb + 64, q, m, T * P:(T + 1) * P],
                              arT[pb:pb + 64, :, m, T * P:(T + 1) * P], start=True, stop=True)
                last.then_inc(S("gram_done"), 1)
                if i % 8 == 7:
                    fill(1)
            pe.wait_ge(S("gram_copied"), 16)

            def inverse(T):
                for l in range(6):
                    for g in range(2):
                        n = T * 12 + l * 2 + g
                        pe.wait_ge(S("levels_made"), 1)
                        if l == 0 and T > 0:
                            pe.wait_ge(S("xt_ready"), T * 12 - 1 + g)
                        if l > 0:
                            pe.wait_ge(S("x_ready"), T * 10 + (l - 1) * 2 + g + 1)
                            pe.wait_ge(S("xt_ready"), T * 12 + (l - 1) * 2 + g + 1)
                        for j in range(4):
                            i = T * 8 + 4 * g + j
                            last = mm(bank[1 + 3 * g][:, j * P:(j + 1) * P], gram[:, i, 0:P],
                                      Xi[:, 4 * g + j, :] if l else ident[:, :], start=True, stop=True)
                        last.then_inc(S("ax_done"), 1)
                    for g in range(2):
                        n = T * 12 + l * 2 + g
                        pe.wait_ge(S("p_ready"), n + 1)
                        if 0 < l < 5:
                            for j in range(4):
                                last = mm(bank[2 + 3 * g][:, j * P:(j + 1) * P], XT[:, T * 8 + 4 * g + j, :],
                                          Pm[:, g, j, :], start=True, stop=True)
                            last.then_inc(S("xp_done"), 1)
                        for j in range(4):
                            o = bank[3 + 3 * g][:, j * P:(j + 1) * P]
                            old = XT[:, T * 8 + 4 * g + j, :] if l else ident[:, :]
                            mm(o, Pm[:, g, j, :], old, start=True, stop=False)
                            last = mm(o, ident[:, :], old, start=False, stop=True)
                        last.then_inc(S("xt_done"), 1)
                    fill(1 if T == 0 or l % 2 else 0)

            def v_terms(T):
                for h in range(8):
                    last = mm(bank[7][:, h * HD:(h + 1) * HD], gram[:, T * 8 + h, 256:384],
                              tokv[:, T, h * HD:(h + 1) * HD], start=(h == 0), stop=False, skip_group_check=True)
                last.then_inc(S("pv_done"), 1)

            def chunk(c):
                T, pb = c // 2, 64 * (c % 2)
                ps = slice(pb, pb + 64)
                if c > 0:
                    pe.wait_ge(S("state_ready"), c)
                    for m in range(NM):
                        last = mm(bank[7][ps, m * P:(m + 1) * P], arT[:, 0, m, c * CH:(c + 1) * CH],
                                  Mst[:, m, :], start=False, stop=False, skip_group_check=True)
                    last.then_inc(S("p_state"), 1)
                pe.wait_ge(S("pb_ready"), c + 1)
                pe.wait_ge(S("xt_ready"), 12 * (T + 1))
                for h in range(8):
                    last = mm(bank[1][ps, h * HD:(h + 1) * HD], XT[:, T * 8 + h, ps], Pb[:, h * HD:(h + 1) * HD],
                              start=True, stop=True)
                last.then_inc(S("u_done"), 1)
                if c < 3:
                    pe.wait_ge(S("u_ready"), c + 1)
                    for m in range(NM):
                        fs = slice(m * P, (m + 1) * P)
                        mm(bank[2][:, fs], tokb[ps, T, fs], U[ps, T, fs], start=True, stop=False)
                        last = mm(bank[2][:, fs], tokk[ps, T, fs], tokv[ps, T, fs], start=False, stop=True)
                    last.then_inc(S("ds_done"), 1)

            def y_v(T):
                b = bank[5 + T]
                for hh in range(2):
                    for m in range(NM):
                        h = 2 * m + hh
                        mm(b[64 * hh:64 * hh + 64, m * P:(m + 1) * P], tokv[:, T, h * HD:(h + 1) * HD],
                           gram[:, T * 8 + h, 384:512], start=(m == 0), stop=False, skip_group_check=True)

            def y_state(c):
                T = c // 2
                for m in range(NM):
                    o = m * P + (c % 2) * CH
                    last = mm(bank[5 + T][:, o:o + CH], Mst[:, m, :], arT[:, 1, m, c * CH:(c + 1) * CH],
                              start=False, stop=False, skip_group_check=True)
                last.then_inc(S("y_state"), 1)

            def y_u(T):
                pe.wait_ge(S("u_ready"), 2 * T + 2)
                for hh in range(2):
                    for m in range(NM):
                        h = 2 * m + hh
                        last = mm(bank[5 + T][64 * hh:64 * hh + 64, m * P:(m + 1) * P], U[:, T, h * HD:(h + 1) * HD],
                                  gram[:, T * 8 + h, 128:256], start=False, stop=True, skip_group_check=True)
                last.then_inc(S("y_done"), 1)

            inverse(0)
            inverse(1)
            pe.wait_ge(S("xt_ready"), 24)
            v_terms(0)
            y_v(0)
            y_v(1)
            chunk(0)
            fill(1)
            pe.wait_ge(S("state_ready"), 1)
            y_state(1)
            chunk(1)
            y_u(0)
            fill(1)
            pe.wait_ge(S("pb_ready"), 2)
            v_terms(1)
            pe.wait_ge(S("state_ready"), 2)
            y_state(2)
            chunk(2)
            fill(1)
            pe.wait_ge(S("state_ready"), 3)
            y_state(3)
            chunk(3)
            y_u(1)
            while st_pe.n < 30:
                fill(1)
            pe.wait_ge(S("yv_ready"), 2)
            for half in range(2):
                mm(bank[1 + half][:, :], bones[:, :], yv[:, 2 * half:2 * half + 2, :], start=True, stop=True)\
                    .then_inc(S("gn_mean"), 1)
            pe.wait_ge(S("ysq_ready"), 2)
            for half in range(2):
                mm(bank[3 + half][:, :], bones[:, :], ysq[:, 2 * half:2 * half + 2, :], start=True, stop=True)\
                    .then_inc(S("gn_var"), 1)
            pe.wait_ge(S("yb_ready"), 1)
            for n in range(2):
                w = take()[:, 0:4096].rearrange("p (c n) -> p c n", c=DC)
                for t in range(NT):
                    for c in range(DC):
                        src = yaT[:, c] if c < 4 else ybT[:, c - 4]
                        last = mm(bank[[1, 5][t] + n][:, :], src[:, t * P:(t + 1) * P], w[:, c, :],
                                  start=(c == 0), stop=(c == DC - 1))
                        opened(last)
            last.then_inc(S("mix_done"), 1)
            def rows(src, n, b0, freed=None):
                pe.wait_ge(S("diag_ready"), n)
                if freed:
                    pe.wait_ge(S(freed[0]), freed[1])
                for k in range(2):
                    mm(bank[b0 + k][:, :], ones[:, :], src[:, 4 * k:4 * k + 4, :], start=True, stop=True)\
                        .then_inc(S("rows_done"), 1)

            rows(diag, 1, 3)
            rows(diag, 2, 3, ("rows_copied", 2))
            rows(diag, 3, 1, ("x1_ready", 2))
            rows(diag, 4, 5)

            pe.wait_ge(S("h2_ready"), 2)
            for u in range(4):
                if u == 0:
                    pe.wait_ge(S("rows_copied"), 8)
                for cc in range(2):
                    for t in range(NT):
                        last = nc.tensor.transpose(bank[1 + u][:, (2 * cc + t) * P:(2 * cc + t + 1) * P],
                                                   h2[:, t, (2 * u + cc) * P:(2 * u + cc + 1) * P], ident[:, :])
                last.then_inc(S("turned"), 1)
            pe.wait_ge(S("h2T_ready"), 4)
            pe.wait_ge(S("router_in"), 48)
            for t in range(NT):
                for c in range(DC):
                    last = mm(bank[5][:, t * 64:t * 64 + 36], h2T[:, c, t * P:(t + 1) * P], rw[:, c, :],
                              start=(c == 0), stop=(c == DC - 1))
            last.then_inc(S("logits_done"), 1)
            pe.wait_ge(S("onehot_ready"), 2)
            oh = rt[:, 768:832].rearrange("p (t e) -> p t e", t=NT)
            mm(bank[6][:, 0:NE], upper[:, :], oh[:, 0], start=True, stop=True)
            mm(bank[6][:, NE:2 * NE], ones[:, :], oh[:, 0], start=True, stop=False)
            mm(bank[6][:, NE:2 * NE], upper[:, :], oh[:, 1], start=False, stop=True)
            mm(bank[6][:, 2 * NE:3 * NE], ones[:, :], oh[:, 0], start=True, stop=False)
            mm(bank[6][:, 2 * NE:3 * NE], ones[:, :], oh[:, 1], start=False, stop=True).then_inc(S("pos_done"), 1)
            pe.wait_ge(S("perm_ready"), 2)
            for c in range(DC):
                b = [1, 2, 3, 4][c % 4]
                if c >= 4:
                    pe.wait_ge(S("xs_copied"), c - 3)
                for t in range(NT):
                    last = mm(bank[b][:, :], h2[:, t, c * P:(c + 1) * P], perm[:, t, :], start=(t == 0), stop=(t == 1))
                last.then_inc(S("xs_done"), 1)
            pe.wait_ge(S("pw_ready"), 2)
            for s in range(4):
                for t in range(NT):
                    last = nc.tensor.transpose(bank[5 + s // 2][:, ((s % 2) * 2 + t) * P:((s % 2) * 2 + t + 1) * P],
                                               pw[:, t, s * P:(s + 1) * P], ident[:, :])
                if s % 2:
                    last.then_inc(S("pwt_done"), 1)
            pe.wait_ge(S("xs_copied"), 8)

            moe_n0 = st_pe.n
            for name in ("up_done", "down_done", "act_turned", "y_turned"):
                pe.nop().then_inc(S(name), 1)
            pe.wait_ge(S("pwt_copied"), 2)
            pe.wait_ge(S("mtab_ready"), 1)

            def window(slots, done, frees):
                def product(b, lhsT, w, n, first, last):
                    for half in range(2):
                        o = slice(64 * half, 64 * half + 64)
                        ins = mm(bank[b][o, 0:n], lhsT, w[:, half * n:(half + 1) * n], start=first, stop=last,
                                 tile_position=(0, 64 * half))
                    return ins

                for k, (name, free_sem) in enumerate((("gate_done", "silu_done"), ("up_done", "act_done"))):
                    w = slots(k, DC)
                    if k == 0:
                        pe.wait_ge(S("xw_ready"), done)
                    pe.wait_ge(S(free_sem), done)
                    for c in range(DC):
                        last = product(1 + k, xw[:, c, :], w[:, c, :], 256, c == 0, c == DC - 1)
                        if frees and c == 0:
                            last.then_inc(S("slot_freed"), 1)
                    last.then_inc(S(name), 1)
                pe.wait_ge(S("act_done"), done + 1)
                pe.wait_ge(S("actT_ready"), done)
                for j in range(2):
                    last = nc.tensor.transpose(bank[4][:, j * P:(j + 1) * P], actm[:, j * P:(j + 1) * P], ident[:, :])
                last.then_inc(S("act_turned"), 1)
                w = slots(2, 4)
                pe.wait_ge(S("actT_ready"), done + 1)
                pe.wait_ge(S("ym_ready"), done)
                for k in range(4):
                    last = product(3, actT[:, k % 2, 64 * (k // 2):64 * (k // 2) + 64], w[:, k, :], 512, k == 0, k == 3)
                    if frees and k == 0:
                        last.then_inc(S("slot_freed"), 1)
                last.then_inc(S("down_done"), 1)
                pe.wait_ge(S("ym_ready"), done + 1)
                pe.wait_ge(S("ys_copied"), done)
                for j in range(4):
                    last = nc.tensor.transpose(bank[5][:, j * P:(j + 1) * P], ym[:, j * P:(j + 1) * P], ident[:, :])
                last.then_inc(S("y_turned"), 1)

            with pe.Fori(0, NE // 2, 1) as i:
                for e in range(2):
                    extra = pe.value_load(mtab[0:1, bass.ds(i * 2 + (NE + e), 1)], min_val=0, max_val=3)
                    before = pe.value_load(mtab[0:1, bass.ds(i * 2 + (2 * NE + e), 1)], min_val=1, max_val=4 * NE)

                    def slots(k, chunks):
                        n = moe_n0 + 3 * e + k
                        pe.wait_ge(S(f"slot{n % RING}_loaded"), i * 16 + 16 * (n // RING + 1))
                        return ring[:, n % RING, :].rearrange("p (c n) -> p c n", c=chunks)

                    with pe.If(extra > 0):
                        with pe.Fori(0, extra, 1) as w:
                            window(slots, before + w, False)
                    window(slots, before + extra, True)
            st_pe.n += 3 * NE

            total = pe.value_load(mtab[0:1, 3 * NE:3 * NE + 1], min_val=1, max_val=4 * NE)
            pe.wait_ge(S("ys_copied"), total)
            for s in range(4):
                for k in range(2):
                    u = 2 * s + k
                    if u >= 6:
                        pe.wait_ge(S(f"yst_copied{k}"), s - 2)
                    for c in range(4):
                        last = nc.tensor.transpose(bank[1 + u % 6][:, c * P:(c + 1) * P],
                                                   ysT[:, 4 * k + c, s * P:(s + 1) * P], ident[:, :])
                    last.then_inc(S("ys_turned"), 1)
            pe.wait_ge(S("yst_copied0"), 4)
            pe.wait_ge(S("yst_copied1"), 4)
            for t in range(NT):
                for n in range(2):
                    for s in range(4):
                        last = mm(bank[1 + 2 * t + n][:, :], pwT[:, s, t * P:(t + 1) * P], ys[:, s, n * 512:(n + 1) * 512],
                                  start=(s == 0), stop=(s == 3))
                last.then_inc(S("moe_done"), 1)

            turns = [1]

            def turn_again():
                turns[0] += 1
                n = turns[0]
                pe.wait_ge(S("xn_ready"), 2 * n)
                for u in range(4):
                    for cc in range(2):
                        for t in range(NT):
                            last = nc.tensor.transpose(bank[1 + u][:, (2 * cc + t) * P:(2 * cc + t + 1) * P],
                                                       yt[:, t, (2 * u + cc) * P:(2 * u + cc + 1) * P], ident[:, :])
                    last.then_inc(S("turned"), 1)
                pe.wait_ge(S("h_ready_v"), 4 * n)
                pe.wait_ge(S("h_ready_s"), 4 * n)

            for layer in range(2):
                pe.wait_ge(S("neg_made"), 3)
                rows(diagd, 5 + 2 * layer, 5)
                rows(diagd, 6 + 2 * layer, 5, ("rows_copied", 10 + 4 * layer))
                turn_again()
                pe.wait_ge(S("rows_copied"), 12 + 4 * layer)
                L8 = 4 * layer
                for q in range(4):
                    w = take()[:, 0:4096].rearrange("p (c n) -> p c n", c=DC)
                    for half in range(2):
                        u = 2 * q + half
                        if u >= 6:
                            pe.wait_ge(S("q_copied"), L8 + u - 5)
                        for mi in range(2):
                            m = 2 * half + mi
                            for c in range(DC):
                                last = mm(bank[1 + u % 6][:, mi * TOK:(mi + 1) * TOK], w[:, c, m * P:(m + 1) * P],
                                          hTd[:, c, :], start=(c == 0), stop=(c == DC - 1))
                                opened(last)
                        last.then_inc(S("qk_done"), 1)
                for n in range(2):
                    w = take()[:, 0:4096].rearrange("p (c n) -> p c n", c=DC)
                    for t in range(NT):
                        u = 8 + 2 * n + t
                        if u < 10:
                            pe.wait_ge(S("q_copied"), L8 + u - 5)
                        else:
                            pe.wait_ge(S("k_copied"), L8 + u - 9)
                        for c in range(DC):
                            last = mm(bank[1 + u % 6][:, :], hTd[:, c, t * P:(t + 1) * P], w[:, c, :],
                                      start=(c == 0), stop=(c == DC - 1))
                            opened(last)
                        last.then_inc(S("v_done"), 1)
                if layer == 1:
                    pe.wait_ge(S("fg_in"), 16)
                    for c in range(DC):
                        last = mm(bank[7][0:NHA, 0:TOK], wfg[:, c, :], hTd[:, c, :], start=(c == 0), stop=(c == DC - 1))
                    last.then_inc(S("fg_done"), 1)
                pe.wait_ge(S("q_copied"), L8 + 4)
                pe.wait_ge(S("k_copied"), L8 + 4)
                pe.wait_ge(S("v_copied"), L8 + 4)
                if layer == 1:
                    pe.wait_ge(S("cum_ready"), 1)
                A8 = 8 * layer

                def scores(m):
                    if m >= 2:
                        pe.wait_ge(S("prob_ready"), A8 + m - 1)
                    for hh in range(2):
                        h, pb = 2 * m + hh, 64 * hh
                        z = bank[1 + 2 * (m % 2) + hh]
                        hs = slice(pb, pb + 64)
                        if layer == 0:
                            mm(z[:, 0:256], KT[hs, m, 0:P], QT[hs, m, :], start=True, stop=False, skip_group_check=True)
                            mm(z[:, 256:384], KT[hs, m, P:TOK], QT[hs, m, P:TOK], start=False, stop=False,
                               skip_group_check=True)
                            mm(z[:, 0:128], ident[:, :], neg_ge, start=False, stop=False, skip_group_check=True)
                            last = mm(z[:, 256:384], ident[:, :], neg_ge, start=False, stop=True, skip_group_check=True)
                        else:
                            mm(z[:, 0:128], QT[hs, m, 0:P], KT[hs, m, 0:P], start=True, stop=False, skip_group_check=True)
                            mm(z[:, 128:384], QT[hs, m, P:TOK], KT[hs, m, :], start=False, stop=False,
                               skip_group_check=True)
                            one = ident[0:NHA, h:h + 1]
                            mm(z[:, 0:128], cumf[0:NHA, 0:P], one.broadcast_to([NHA, P]), start=False, stop=False,
                               skip_group_check=True)
                            mm(z[:, 128:384], cumf[0:NHA, P:TOK], one.broadcast_to([NHA, TOK]), start=False, stop=False,
                               skip_group_check=True)
                            mm(z[:, 0:128], one.broadcast_to([NHA, P]), ncumf[0:NHA, 0:P], start=False, stop=False,
                               skip_group_check=True)
                            mm(z[:, 128:384], one.broadcast_to([NHA, P]), ncumf[0:NHA, :], start=False, stop=False,
                               skip_group_check=True)
                            mm(z[:, 0:128], ident[:, :], neg_gt, start=False, stop=False, skip_group_check=True)
                            last = mm(z[:, 256:384], ident[:, :], neg_gt, start=False, stop=True, skip_group_check=True)
                    last.then_inc(S("z_done"), 1)

                def middle(m):
                    if layer == 0:
                        pe.wait_ge(S("sp_ready"), m + 1)
                        for hh in range(2):
                            z = bank[1 + 2 * (m % 2) + hh]
                            s_ = sp_[:, m % 2, hh, :]
                            mm(z[:, 0:384], neg_lower, s_, start=False, stop=False, skip_group_check=True)
                            last = mm(z[:, 128:256], neg_ones, s_[:, 256:384], start=False, stop=True,
                                      skip_group_check=True)
                        last.then_inc(S("sums_done"), 1)
                    else:
                        pe.wait_ge(S("prob_ready"), A8 + m + 1)
                        if m >= 1:
                            pe.wait_ge(S("pt_copied"), m)
                        for hh in range(2):
                            for k in range(3):
                                last = nc.tensor.transpose(bank[7 if hh else 0][:, k * P:(k + 1) * P],
                                                           pr[:, m % 2, hh, k * P:(k + 1) * P], ident[:, :])
                        last.then_inc(S("pt_done"), 1)

                def output(m):
                    if layer == 0:
                        pe.wait_ge(S("prob_ready"), A8 + m + 1)
                    else:
                        pe.wait_ge(S("pt_copied"), m + 1)
                    if m >= 2:
                        pe.wait_ge(S("o_copied"), A8 + m - 1)
                    pt = (t1 if layer else pr)[:, m % 2]
                    for hh in range(2):
                        h = 2 * m + hh
                        o = bank[5 + m % 2][64 * hh:64 * hh + 64, 0:TOK]
                        mm(o, Vd[:, 0, h * HD:(h + 1) * HD], pt[:, hh, 0:256], start=True, stop=False,
                           skip_group_check=True)
                        last = mm(o[:, P:TOK], Vd[:, 1, h * HD:(h + 1) * HD], pt[:, hh, 256:384], start=False, stop=True,
                                  skip_group_check=True)
                    last.then_inc(S("o_done"), 1)

                mods1 = iter(range(12))
                for m in range(8 + 2):
                    if m < 8:
                        scores(m)
                    if 1 <= m <= 8:
                        middle(m - 1)
                    if m >= 2:
                        output(m - 2)
                    if layer == 0:
                        for _ in range(2 if m % 5 == 0 else 1):
                            j = next(mods1, None)
                            if j is not None:
                                pe.wait_ge(S("mod_copied"), 3)
                                mod_slot(j, silc, 128)
                pe.wait_ge(S("o_copied"), A8 + 8)
                pe.wait_ge(S("prob_ready"), A8 + 8)
                for n in range(2):
                    w = take()[:, 0:4096].rearrange("p (c n) -> p c n", c=DC)
                    for t in range(NT):
                        for c in range(DC):
                            last = mm(bank[1 + 2 * t + n][:, :], oT[:, c, t * P:(t + 1) * P], w[:, c, :],
                                      start=(c == 0), stop=(c == DC - 1))
                            opened(last)
                        last.then_inc(S("proj_done"), 1)
                turn_again()

                n0 = st_pe.n
                F0 = NFT * layer

                def group_slots(n, i, w):
                    out = []
                    for k in range(3):
                        s = (n + k) % RING
                        out.append((S(f"slot{s}_loaded"), i * 16 + 16 * ((n + k) // RING + 1),
                                    ring[:, s, 0:8 * w].rearrange("p (c n) -> p c n", c=(DC, DC, w // P)[k])))
                    return out

                def gate_up(sl, j, f):
                    b = bank[5 + j % 2]
                    if j == 0:
                        pe.wait_ge(*sl[0][0:2])
                        pe.wait_ge(*sl[1][0:2])
                    if not isinstance(f, int) or f >= 2:
                        pe.wait_ge(S("act_f"), f - 1)
                    for k in range(2):
                        for c in range(DC):
                            last = mm(b[:, k * TOK:(k + 1) * TOK], sl[k][2][:, c, j * P:(j + 1) * P], hTd[:, c, :],
                                      start=(c == 0), stop=(c == DC - 1))
                            opened(last)
                    last.then_inc(S("gu_done"), 1)

                def down(sl, j, f, first=False, last_of=None, final=False):
                    if j == 0:
                        pe.wait_ge(*sl[2][0:2])
                    pe.wait_ge(S("act_f"), f + 1)
                    i = 0
                    for t in range(NT):
                        for n in range(2):
                            ins = mm(bank[1 + 2 * t + n][:, :], actF[:, 0, j % 2, t * P:(t + 1) * P],
                                     sl[2][2][:, j, n * 512:(n + 1) * 512], start=first, stop=final, skip_group_check=True)
                            if last_of and i in (0, 1, 3):
                                ins.then_inc(S("slot_freed"), 1)
                            i += 1

                fresh[0] = True
                g0 = group_slots(n0, 0, 512)
                gate_up(g0, 0, F0 + 0)
                gate_up(g0, 1, F0 + 1)
                down(g0, 0, F0 + 0, first=True)
                gate_up(g0, 2, F0 + 2)
                down(g0, 1, F0 + 1)
                gate_up(g0, 3, F0 + 3)
                down(g0, 2, F0 + 2)

                def middle_group(prev, n, i, f):
                    cur = group_slots(n, i, 512)
                    gate_up(cur, 0, f)
                    down(prev, 3, f - 1, last_of=True)
                    gate_up(cur, 1, f + 1)
                    down(cur, 0, f)
                    gate_up(cur, 2, f + 2)
                    down(cur, 1, f + 1)
                    gate_up(cur, 3, f + 3)
                    down(cur, 2, f + 2)
                    return cur

                with pe.Fori(0, 2, 1) as i:
                    prev = [(None, None, ring[:, (n0 + k) % RING, :].rearrange("p (c n) -> p c n", c=(DC, DC, 4)[k]))
                            for k in range(3)]
                    prev = middle_group(prev, n0 + 3, i, i * 8 + (F0 + 4))
                    middle_group(prev, n0 + 6, i, i * 8 + (F0 + 8))
                prev = [(None, None, ring[:, (n0 + 12 + k) % RING, :].rearrange("p (c n) -> p c n", c=(DC, DC, 4)[k]))
                        for k in range(3)]
                g5 = group_slots(n0 + 15, 0, 256)
                gate_up(g5, 0, F0 + 20)
                down(prev, 3, F0 + 19, last_of=True)
                gate_up(g5, 1, F0 + 21)
                down(g5, 0, F0 + 20)
                down(g5, 1, F0 + 21, last_of=True, final=True)
                st_pe.n += 18
                ahead[0] = True
                pe.wait_ge(S("slot_freed"), st_pe.n)
                pe.nop().then_inc(S("ffn_done"), 1)

        @block.vector
        def _(dve):
            V = nc.vector
            d = Chain(dve, S, "vector_step")

            def mean_square(src, dst=None):
                for t in range(NT):
                    d(V.tensor_tensor_reduce(out=dst[:, t, :], in0=src[:, t, :], in1=src[:, t, :], scale=1.0 / D,
                                             scalar=RMS_EPS, op0=ALU.mult, op1=ALU.add, accum_out=stat[:, t:t + 1]))
                d.to(V.tensor_copy(stat[:, 0:2], stat[:, 0:2]), "ms_ready")

            def scaled(dst, n):
                dve.wait_ge(S("rstd_ready"), n)
                for t in range(NT):
                    d.to(V.tensor_scalar(dst[:, t, :], x[:, t, :], stat[:, 2 + t:3 + t], None, ALU.mult), "xn_ready")

            def gain(lm, sc0, g):
                d(V.scalar_tensor_tensor(out=fcol, in0=modc[:, lm, sc0:sc0 + 8], scalar=1.0, in1=g,
                                         op0=ALU.add, op1=ALU.mult))

            def evac_h(dst, lm, sh0, n):
                for c in (0, 1, 4, 5):
                    dve.wait_ge(S("turned"), n + c // 2 + 1)
                    o = (c % 2) * TOK
                    d.to(V.tensor_scalar(dst[:, c, :], bank[1 + c // 2][:, o:o + TOK], fcol[:, c:c + 1],
                                    modc[:, lm, sh0 + c:sh0 + c + 1], ALU.mult, ALU.add), "h_ready_v")

            dve.wait_ge(S("x_in"), 16)
            mean_square(x, xn)
            scaled(xn, 1)
            dve.wait_ge(S("cols_in"), 16)
            d(V.tensor_scalar(small[:, 0:14], cols[:, COLS["mu_rkv"][0]:COLS["mu_rkv"][0] + 14], -1.0, 1.0,
                              ALU.mult, ALU.add))
            d(V.tensor_scalar(omka, col("k_a", 0, 4), -1.0, 1.0, ALU.mult, ALU.add))
            dve.wait_ge(S("mod_done"), 1)
            d.to(V.tensor_tensor(modc[:, 0, 0:16], bank[0][:, 0:16], col("ada_b", 0, 16), ALU.add), "mod_copied")
            dve.wait_ge(S("mod_copied"), 1)
            gain(0, 8, col("norm1_g", 0, 8))
            d.to(V.tensor_copy(stat[:, 15:16], fcol[:, 0:1]), "fcol_ready")
            evac_h(hT, 0, 0, 0)

            UB = [1, 2, 3, 4, 5, 6]
            for u in range(7):
                b = bank[UB[u % 6]]
                dve.wait_ge(S("shift_ready"), 2 * u + 2)
                for mi in range(2):
                    if u < 6:
                        m = 2 * (u % 2) + mi
                        dst, mu = (rT, kT, vT)[u // 2][:, m, :], col("mu_rkv", (u // 2) * 4 + m)
                        rows_ = P
                    else:
                        dst, rows_ = (xwa, xg)[mi], (64, 96)[mi]
                        mu = col(("mu_wa", "mu_g")[mi])
                    o = mi * TOK
                    ins = V.scalar_tensor_tensor(out=dst[0:rows_, 1:TOK], in0=b[0:rows_, o:o + TOK - 1],
                                                 scalar=mu[0:rows_, :], in1=dst[0:rows_, 1:TOK],
                                                 op0=ALU.mult, op1=ALU.add)
                    if mi == 0:
                        d(ins)
                    else:
                        d.to(ins, "unit_free")
            dve.wait_ge(S("unit_free"), 7)
            for m in range(NM):
                d(V.tensor_scalar(kkn[:, m, :], kT[:, m, :], col("k_k", m), None, ALU.mult))
            d.to(V.tensor_tensor(tmp1, kkn, kkn, ALU.mult), "kk_sq")
            dve.wait_ge(S("masks_made"), 3)
            dve.wait_ge(S("sw_ready"), 4)
            for m in range(NM):
                d(V.tensor_tensor_scan(out=cum[:, m, :], data0=keep[:, :], data1=sw[:, m, :], initial=0.0,
                                       op0=ALU.mult, op1=ALU.add))
            d.to(V.tensor_tensor(sw, cum, sw, ALU.subtract), "cum_done")
            dve.wait_ge(S("a_ready"), 4)
            for m in range(NM):
                d(V.tensor_scalar(tmp2[:, m, :], aT[:, m, :], col("k_a", m), omka[:, m:m + 1], ALU.mult, ALU.add))
            d(V.tensor_tensor(kT, kT, tmp2, ALU.mult))
            dve.wait_ge(S("gelu_done"), 4)
            d(V.tensor_scalar(stat[:, 6:8], stat[:, 4:6], 1.0 / HALF, None, ALU.mult))
            for t in range(NT):
                d(V.tensor_scalar(gv[:, t, :], gv[:, t, :], stat[:, 6 + t:7 + t], None, ALU.subtract))
                d(V.tensor_tensor_reduce(out=tmp2[:, 0:2, :].rearrange("p a b -> p (a b)"), in0=gv[:, t, :],
                                         in1=gv[:, t, :], scale=1.0 / HALF, scalar=LN_EPS, op0=ALU.mult, op1=ALU.add,
                                         accum_out=stat[:, t:t + 1]))
            d.to(V.tensor_copy(stat[:, 0:2], stat[:, 0:2]), "ms_ready")
            dve.wait_ge(S("kk_norm"), 2)
            d(V.tensor_scalar(tmp1, tmp1, 1e-12, None, ALU.max))
            d(V.reciprocal(tmp1, tmp1))
            d(V.tensor_tensor(kkn, kkn, tmp1, ALU.mult))
            dve.wait_ge(S("ln_in"), 64)
            dve.wait_ge(S("rstd_ready"), 2)
            for t in range(NT):
                d(V.scalar_tensor_tensor(out=gv[:, t, :], in0=gv[:, t, :], scalar=stat[:, 2 + t:3 + t], in1=lnw,
                                         op0=ALU.mult, op1=ALU.mult))
                d.to(V.tensor_tensor(gv[:, t, :], gv[:, t, :], lnb, ALU.add), "gv_ready")
            for m in range(NM):
                ins = V.scalar_tensor_tensor(out=tmp2[:, m, :], in0=rT[:, m, :], scalar=col("r_k", m), in1=kT[:, m, :],
                                             op0=ALU.mult, op1=ALU.mult)
                d(ins) if m < NM - 1 else d.to(ins, "bonus_in")
            dve.wait_ge(S("exps_done"), 3)
            d(V.tensor_copy(dend, eL.rearrange("p m (c t) -> p m c t", t=CH)[:, :, :, CH - 1:CH].squeeze(3)))
            for k in range(2):
                dve.wait_ge(S("mixed"), k + 1)
                v = bank[3 + k].rearrange("p (m t s) -> p m t s", m=2, t=NT)
                for mi in range(2):
                    m = 2 * k + mi
                    d(V.tensor_tensor(tmp1[:, m, :].rearrange("p (t s) -> p t s", t=NT), v[:, mi],
                                      bsb[:, m:m + 1, :].broadcast_to([P, NT, P]), ALU.add))
            d.to(V.tensor_tensor(yaT, yaT, tmp1, ALU.mult), "ya_ready")
            d(V.tensor_tensor(tmp1, kkn, aT, ALU.mult))
            d(V.scalar_tensor_tensor(out=arT[:, 0], in0=kkn, scalar=-1.0, in1=sw, op0=ALU.mult, op1=ALU.mult))
            d(V.tensor_tensor(arT[:, 1], rT, eL, ALU.mult))
            dve.wait_ge(S("ya_ready"), 1)
            d(V.tensor_tensor(bkT[:, 0], tmp1, cum, ALU.mult))
            d.to(V.tensor_tensor(bkT[:, 1], kT, cum, ALU.mult), "bk_ready")
            for half in range(2):
                dve.wait_ge(S("bonus_sums"), half + 1)
                d.to(V.tensor_tensor(bonus[:, 2 * half:2 * half + 2, :], bank[5 + half].rearrange("p (m t) -> p m t", m=2),
                                vT[:, 2 * half:2 * half + 2, :], ALU.mult), "bonus_ready")
            for t in range(NT):
                dve.wait_ge(S("tok_turned"), 3 + t)
                d.to(V.tensor_copy(tokb[:, t, :], bank[3 + t][:, :]), "tokb_copied")
            dve.wait_ge(S("bonus_ready"), 2)
            dve.wait_ge(S("mod_done"), 2)
            d.to(V.tensor_tensor(modc[:, 0, 16:48], bank[0][:, 16:48], col("ada_b", 16, 32), ALU.add), "mod_copied")
            dve.wait_ge(S("tok_copied"), 4)
            for i in range(16):
                dve.wait_ge(S("gram_done"), i + 1)
                b = bank[[1, 3, 2, 4, 7, 5][i % 6]]
                d.to(V.tensor_tensor(gram[:, i, :].rearrange("p (q w) -> p q w", q=2), b.rearrange("p (q w) -> p q w", q=2),
                                mask_ar[:, :, :].rearrange("p w t -> p (w t)").unsqueeze(1).broadcast_to([P, 2, 2 * P]),
                                ALU.mult), "gram_copied")
            dve.wait_ge(S("levels_made"), 1)
            d.to(V.memset(Pb, 0.0), "pb_clear")
            b4 = lambda t_: t_.unsqueeze(1).broadcast_to([P, 4, P])
            for T in range(2):
                for l in range(6):
                    for g in range(2):
                        n = T * 12 + l * 2 + g
                        dve.wait_ge(S("ax_done"), n + 1)
                        if n >= 2:
                            dve.wait_ge(S("xt_done"), n - 1)
                        d.to(V.tensor_tensor(Pm[:, g], bank[1 + 3 * g].rearrange("p (j t) -> p j t", j=4),
                                        b4(level[:, l, :]), ALU.mult), "p_ready")
                    for g in range(2):
                        n = T * 12 + l * 2 + g
                        xs = Xi[:, 4 * g:4 * g + 4, :]
                        if l == 0:
                            dve.wait_ge(S("p_ready"), n + 1)
                            d.to(V.tensor_tensor(xs, Pm[:, g], b4(ident[:, :]), ALU.add), "x_ready")
                        elif l < 5:
                            dve.wait_ge(S("xp_done"), T * 8 + (l - 1) * 2 + g + 1)
                            dve.wait_ge(S("x_ready"), T * 10 + (l - 1) * 2 + g + 1)
                            d.to(V.tensor_tensor(xs, xs, bank[2 + 3 * g].rearrange("p (j t) -> p j t", j=4),
                                            ALU.add), "x_ready")
            dve.wait_ge(S("pb_clear"), 1)
            for c in range(4):
                T, ps = c // 2, slice(64 * (c % 2), 64 * (c % 2) + 64)
                if c < 3:
                    if c > 0:
                        dve.wait_ge(S("state_ready"), c)
                    for m in range(NM):
                        d(V.tensor_scalar(DCm[:, m, :], bones[:, :], dend[:, m, c:c + 1], None, ALU.mult))
                if c > 0:
                    dve.wait_ge(S("p_state"), c)
                else:
                    dve.wait_ge(S("pv_done"), 1)
                d.to(V.tensor_copy(Pb[ps, :], bank[7][ps, :]), "pb_ready")
                dve.wait_ge(S("u_done"), c + 1)
                d.to(V.tensor_copy(U[ps, T, :], bank[1][ps, :]), "u_ready")
                if c < 3:
                    dve.wait_ge(S("ds_done"), c + 1)
                    ds = bank[2].rearrange("p (m v) -> p m v", m=NM)
                    if c > 0:
                        d(V.tensor_tensor(Mst, Mst, ds, ALU.add))
                        ds = Mst
                    d.to(V.tensor_tensor(Mst, ds, DCm, ALU.mult), "state_ready")
                if c % 2:
                    dve.wait_ge(S("y_done"), T + 1)
                    d.to(V.tensor_copy(yv[:, :, T * P:(T + 1) * P], bank[5 + T].rearrange("p (m t) -> p m t", m=NM)), "yv_ready")
            dve.wait_ge(S("yv_ready"), 2)
            for half in range(2):
                hs = slice(2 * half, 2 * half + 2)
                dve.wait_ge(S("gn_mean"), half + 1)
                d(V.scalar_tensor_tensor(out=yd[:, hs], in0=bank[1 + half].rearrange("p (m t) -> p m t", m=2),
                                         scalar=-1.0 / HD, in1=yv[:, hs], op0=ALU.mult, op1=ALU.add))
                d.to(V.tensor_tensor(ysq[:, hs], yd[:, hs], yd[:, hs], ALU.mult), "ysq_ready")
            dve.wait_ge(S("gn_std"), 2)
            d(V.reciprocal(yv, yv))
            d(V.tensor_tensor(yd, yd, yv, ALU.mult))
            for m in range(NM):
                d(V.tensor_scalar(yd[:, m, :], yd[:, m, :], col("gn_w", m), col("gn_b", m), ALU.mult, ALU.add))
            d(V.tensor_tensor(yd, yd, bonus, ALU.add))
            d.to(V.tensor_tensor(ybT, yd, gT, ALU.mult), "yb_ready")

            n_diag = [0]

            def make_diag(dst, vec):
                if n_diag[0]:
                    dve.wait_ge(S("rows_done"), 2 * n_diag[0])
                d.to(V.tensor_tensor(dst, ident[:, :].unsqueeze(1).broadcast_to([P, DC, P]),
                                vec.unsqueeze(2).broadcast_to([P, DC, P]), ALU.mult), "diag_ready")
                n_diag[0] += 1

            dve.wait_ge(S("mod_copied"), 2)
            make_diag(diag, modc[:, 0, 16:24])
            gain(0, 32, col("norm2_g", 0, 8))
            make_diag(diag, fcol)
            dve.wait_ge(S("mix_done"), 1)
            dve.wait_ge(S("rows_copied"), 2)
            for t in range(NT):
                y = psum[:, 1 + 4 * t:3 + 4 * t, :].rearrange("p b n -> p (b n)")
                d(V.tensor_tensor(h2[:, t, :], y, gate1b, ALU.mult))
                d.to(V.tensor_tensor(x[:, t, :], x[:, t, :], h2[:, t, :], ALU.add), "x1_ready")
            make_diag(diag, modc[:, 0, 24:32])
            make_diag(diag, modc[:, 0, 40:48])
            dve.wait_ge(S("x1_ready"), 2)
            mean_square(x, h2)
            dve.wait_ge(S("rstd_ready"), 3)
            dve.wait_ge(S("rows_copied"), 6)
            for t in range(NT):
                d(V.scalar_tensor_tensor(out=h2[:, t, :], in0=x[:, t, :], scalar=stat[:, 2 + t:3 + t], in1=sc2b,
                                         op0=ALU.mult, op1=ALU.mult))
                d.to(V.tensor_tensor(h2[:, t, :], h2[:, t, :], sh2b, ALU.add), "h2_ready")
            dve.wait_ge(S("logits_done"), 1)
            dve.wait_ge(S("router_in"), 48)
            dve.wait_ge(S("iota_made"), 1)
            f1 = lambda o: rt[:, o:o + 1]
            for t in range(NT):
                o = 128 * t
                L, G8, m8 = rt[:, o:o + 36], rt[:, o + 40:o + 48], rt[:, o + 48:o + 56]
                i8 = rt[:, o + 56:o + 64].bitcast(U32)
                sel, s8, si = rt[:, o + 64:o + 72], rt[:, o + 72:o + 80], rt[:, o + 80:o + 88].bitcast(U32)
                ohg = rt[:, o + 88:o + 92]
                gf, gs, dd, i1, i2 = f1(o + 92), f1(o + 93), f1(o + 94), f1(o + 95), f1(o + 96)
                e1, e2, w1, w2, ng = f1(o + 97), f1(o + 98), f1(o + 99), f1(o + 100), f1(o + 101)
                p1 = f1(o + 102)
                d(V.tensor_tensor(L, bank[5][:, t * 64:t * 64 + 36], rb, ALU.add))
                d(V.memset(G8, NEG))
                d(V.tensor_copy(G8[:, 0:4], L[:, 0:4]))
                d(V.max(m8, G8))
                d(V.max_index(i8, m8, G8))
                d(V.tensor_copy(gf, i8[:, 0:1]))
                d.to(V.tensor_scalar(ng, m8[:, 0:1], -1.0, None, ALU.mult), "g_max")
                d(V.tensor_scalar(ohg, iota[:, 0:4], gf, None, ALU.is_equal))
                d(V.tensor_scalar(sel, L[:, 4:12], ohg[:, 0:1], None, ALU.mult))
                for g in range(1, NG):
                    d(V.scalar_tensor_tensor(out=sel, in0=L[:, 4 + 8 * g:12 + 8 * g], scalar=ohg[:, g:g + 1], in1=sel,
                                             op0=ALU.mult, op1=ALU.add))
                d(V.max(s8, sel))
                d(V.max_index(si, s8, sel))
                d.to(V.tensor_tensor(dd, s8[:, 1:2], s8[:, 0:1], ALU.subtract), "e_gap")
                d(V.tensor_copy(i1, si[:, 0:1]))
                d(V.tensor_copy(i2, si[:, 1:2]))
                d(V.scalar_tensor_tensor(out=e1, in0=gf, scalar=float(EPG), in1=i1, op0=ALU.mult, op1=ALU.add))
                d(V.scalar_tensor_tensor(out=e2, in0=gf, scalar=float(EPG), in1=i2, op0=ALU.mult, op1=ALU.add))
                oh1, oh2 = rt[:, 256 + 64 * t:288 + 64 * t], rt[:, 288 + 64 * t:320 + 64 * t]
                d(V.tensor_scalar(oh1, iota[:, 0:NE], e1, None, ALU.is_equal))
                d(V.tensor_scalar(oh2, iota[:, 0:NE], e2, None, ALU.is_equal))
                d.to(V.tensor_tensor(rt[:, 768 + NE * t:768 + NE * (t + 1)], oh1, oh2, ALU.add), "onehot_ready")
                dve.wait_ge(S("g_sum"), t + 1)
                d(V.reciprocal(gs, gs))
                dve.wait_ge(S("e_exp"), t + 1)
                d(V.tensor_scalar(p1, dd, 1.0, None, ALU.add))
                d(V.reciprocal(p1, p1))
                d(V.tensor_tensor(w1, gs, p1, ALU.mult))
                d(V.tensor_tensor(w2, w1, dd, ALU.mult))
            cnt, inc_, st = rt[:, 400:432], rt[:, 432:464], rt[:, 464:496]
            dve.wait_ge(S("pos_done"), 1)
            d(V.tensor_copy(cnt, bank[6][:, 2 * NE:3 * NE]))
            d(V.tensor_tensor_scan(out=inc_, data0=ones[:, 0:NE], data1=cnt, initial=0.0, op0=ALU.mult, op1=ALU.add))
            d(V.tensor_tensor(st, inc_, cnt, ALU.subtract))
            for t in range(NT):
                o = 128 * t
                base, tr = rt[:, 496 + 32 * t:528 + 32 * t], rt[:, 560:592]
                d(V.tensor_tensor(base, bank[6][:, t * NE:(t + 1) * NE], st, ALU.add))
                for k in range(2):
                    d(V.tensor_tensor_reduce(out=tr, in0=rt[:, 256 + 64 * t + 32 * k:288 + 64 * t + 32 * k], in1=base,
                                             scale=1.0, scalar=0.0, op0=ALU.mult, op1=ALU.add, accum_out=f1(o + 104 + k)))
                d(V.tensor_scalar(perm[:, t, :], iota, f1(o + 104), None, ALU.is_equal))
                d.to(V.scalar_tensor_tensor(out=perm[:, t, :], in0=iota, scalar=f1(o + 105), in1=perm[:, t, :],
                                       op0=ALU.is_equal, op1=ALU.add), "perm_ready")
            ex, pa = rt[:, 592:624], rt[:, 624:656]
            d(V.tensor_scalar(ex, cnt, float(WIN), None, ALU.is_gt))
            for k in (2, 3):
                d(V.scalar_tensor_tensor(out=ex, in0=cnt, scalar=float(k * WIN), in1=ex, op0=ALU.is_gt, op1=ALU.add))
            d(V.tensor_scalar(inc_, ex, 1.0, None, ALU.add))
            d(V.tensor_tensor_scan(out=pa, data0=ones[:, 0:NE], data1=inc_, initial=0.0, op0=ALU.mult, op1=ALU.add))
            d(V.tensor_scalar(mtab[0:1, 3 * NE:3 * NE + 1], pa[0:1, NE - 1:NE], 1.0, None, ALU.add))
            d(V.tensor_tensor(pa, pa, inc_, ALU.subtract))
            d(V.tensor_scalar(pa, pa, 1.0, None, ALU.add))
            dve.nop().then_inc(S("act_done"), 1)
            d(V.tensor_copy(mtab[0:1, 0:NE], st[0:1, :]))
            d(V.tensor_copy(mtab[0:1, NE:2 * NE], ex[0:1, :]))
            d.to(V.tensor_copy(mtab[0:1, 2 * NE:3 * NE], pa[0:1, :]), "mtab_ready")
            for t in range(NT):
                o = 128 * t
                d(V.tensor_scalar(pw[:, t, :], iota, f1(o + 104), f1(o + 99), ALU.is_equal, ALU.mult))
                d(V.tensor_scalar(diag[:, 0:4, :].rearrange("p a b -> p (a b)"), iota, f1(o + 105), f1(o + 100),
                                  ALU.is_equal, ALU.mult))
                d.to(V.tensor_tensor(pw[:, t, :], pw[:, t, :], diag[:, 0:4, :].rearrange("p a b -> p (a b)"), ALU.add), "pw_ready")
            for c in range(DC):
                dve.wait_ge(S("xs_done"), c + 1)
                d.to(V.tensor_copy(xsT[:, c, 0:SLOTS], bank[1 + c % 4][:, :]), "xs_copied")
            dve.nop().then_inc(S("actT_ready"), 1)
            dve.wait_ge(S("mtab_ready"), 1)
            dve.wait_ge(S("xs_copied"), 8)
            dve.wait_ge(S("iota_made"), 2)

            def act_pass(start, done):
                dve.wait_ge(S("up_done"), done)
                V.tensor_copy(xw, xsT[:, :, bass.ds(start, WIN)]).then_inc(S("xw_ready"), 1)
                dve.wait_ge(S("silu_done"), done + 1)
                dve.wait_ge(S("up_done"), done + 1)
                dve.wait_ge(S("act_turned"), done)
                V.tensor_tensor(actm, bank[2][:, 0:4 * WIN], sg, ALU.mult).then_inc(S("act_done"), 1)
                dve.wait_ge(S("act_turned"), done + 1)
                dve.wait_ge(S("down_done"), done)
                V.tensor_copy(actT.rearrange("p a b -> p (a b)"), bank[4][:, 0:4 * WIN]).then_inc(S("actT_ready"), 1)

            within = "the passes of an expert begin within its slots"
            with dve.Fori(0, NE, 1) as i:
                start = dve.value_load(mtab[0:1, bass.ds(i, 1)], min_val=0, max_val=SLOTS)
                extra = dve.value_load(mtab[0:1, bass.ds(i + NE, 1)], min_val=0, max_val=3)
                before = dve.value_load(mtab[0:1, bass.ds(i + 2 * NE, 1)], min_val=1, max_val=4 * NE)
                with dve.If(extra > 0):
                    with dve.Fori(0, extra, 1) as w:
                        act_pass(nc.s_assert_within(start + w * WIN, 0, SLOTS, skip_runtime_bounds_check_because=within),
                                 before + w)
                act_pass(nc.s_assert_within(start + extra * WIN, 0, SLOTS, skip_runtime_bounds_check_because=within),
                         before + extra)
            for s in range(4):
                dve.wait_ge(S("ys_turned"), 2 * s + 1)
                d.to(V.tensor_copy(ys[:, s, 0:512], bank[1 + (2 * s) % 6][:, :]), "yst_copied0")
            for t in range(NT):
                dve.wait_ge(S("moe_done"), t + 1)
                y = psum[:, 1 + 2 * t:3 + 2 * t, :].rearrange("p b n -> p (b n)")
                if t == 0:
                    dve.wait_ge(S("moe_done"), 2)
                d(V.tensor_tensor(ys[:, t, :], y, gate2b, ALU.mult))
                d.to(V.tensor_tensor(x[:, t, :], x[:, t, :], ys[:, t, :], ALU.add), "x2_sum")
            dve.wait_ge(S("x2_sum"), 2)
            mean_square(x, ys[:, 0:2, :])
            dve.wait_ge(S("rstd_ready"), 4)
            for t in range(NT):
                d.to(V.scalar_tensor_tensor(out=x[:, t, :], in0=x[:, t, :], scalar=stat[:, 2 + t:3 + t], in1=fgb,
                                       op0=ALU.mult, op1=ALU.mult), "x2_ready")

            rn = 5
            for layer in range(2):
                lm = 1 + layer
                dve.wait_ge(S("x2_ready") if layer == 0 else S("x4_ready"), 2)
                dve.wait_ge(S("mod_done"), 4 + 2 * layer)
                d.to(V.tensor_tensor(modc[:, lm, :], bank[0][:, 64 * lm:64 * lm + 48], col(f"b_mod{layer}", 0, 48),
                                ALU.add), "mod_copied")
                dve.wait_ge(S("mod_copied"), 3 + layer)
                for k, (nm, dst) in enumerate((("g_mix_post", 16), ("g_ffn_post", 40))):
                    if n_diag[0]:
                        dve.wait_ge(S("rows_done"), 2 * n_diag[0])
                    d(V.tensor_tensor(spare, modc[:, lm, dst:dst + 8], col(nm, 8 * layer, 8), ALU.mult))
                    make_diag(diagd, spare)
                mean_square(x, yt)
                scaled(yt, rn)
                rn += 1
                gain(lm, 8, col("g_mix_pre", 8 * layer, 8))
                d.to(V.tensor_copy(stat[:, 15:16], fcol[:, 0:1]), "fcol_ready")
                evac_h(hTd, lm, 0, 8 + 8 * layer)
                for u in range(4):
                    dve.wait_ge(S("qk_done"), 8 * layer + 5 + u)
                    d.to(V.tensor_copy(KT[:, 2 * u:2 * u + 2, :], bank[1 + (4 + u) % 6].rearrange("p (m t) -> p m t", m=2)), "k_copied")
                if layer == 1:
                    dve.wait_ge(S("fg_done"), 1)
                    H_ = slice(0, NHA)
                    u_, v_ = ncumf[H_, :], cumf[H_, :]
                    d(V.tensor_scalar(u_, bank[7][H_, 0:TOK], col("b_fg")[H_, :], -1.0, ALU.add, ALU.mult))
                    d(V.tensor_scalar(v_, u_, 0.0, None, ALU.max))
                    d.to(V.scalar_tensor_tensor(out=v_, in0=v_, scalar=-2.0, in1=u_, op0=ALU.mult, op1=ALU.add), "fg_abs")
                    dve.wait_ge(S("fg_log"), 1)
                    d(V.scalar_tensor_tensor(out=v_, in0=u_, scalar=0.0, in1=v_, op0=ALU.max, op1=ALU.add))
                    d(V.tensor_tensor_scan(out=u_, data0=keep1[:, :], data1=v_, initial=0.0, op0=ALU.mult, op1=ALU.add))
                    d.to(V.tensor_scalar(v_, u_, -1.0, None, ALU.mult), "cum_ready")
                A8 = 8 * layer
                for m in range(8 + 2):
                    if m < 8:
                        dve.wait_ge(S("z_done"), A8 + m + 1)
                        z = psum[:, 1 + 2 * (m % 2):3 + 2 * (m % 2), 0:384]
                        if layer == 0:
                            if m >= 2:
                                dve.wait_ge(S("sums_done"), m - 1)
                            d(V.tensor_scalar(sp_[:, m % 2], z, 0.0, None, ALU.max))
                            d.to(V.scalar_tensor_tensor(out=t1[:, m % 2], in0=sp_[:, m % 2], scalar=-2.0, in1=z,
                                                        op0=ALU.mult, op1=ALU.add), "abs_done")
                        else:
                            ng = stat[:, 4 + 4 * (m % 2):8 + 4 * (m % 2)].rearrange("p (h t) -> p h t", h=2)
                            if m >= 2:
                                dve.wait_ge(S("exp_done"), m - 1)
                            d(V.tensor_reduce(ng[:, :, 0:1], z[:, :, 0:128], AX.X, ALU.max))
                            d(V.tensor_reduce(ng[:, :, 1:2], z[:, :, 128:384], AX.X, ALU.max))
                            d.to(V.tensor_scalar(ng, ng, -1.0, None, ALU.mult), "neg_max")
                    if m < 8 and layer == 0:
                        dve.wait_ge(S("log_done"), m + 1)
                        d.to(V.tensor_tensor(sp_[:, m % 2], sp_[:, m % 2], t1[:, m % 2], ALU.add), "sp_ready")
                    if layer == 1 and 1 <= m <= 8:
                        k = m - 1
                        dve.wait_ge(S("exp_done"), k + 1)
                        sm = small[:, 80 + 4 * (k % 2):84 + 4 * (k % 2)].rearrange("p (h t) -> p h t", h=2)
                        d(V.reciprocal(sm, sm))
                        d(V.tensor_tensor(pr[:, k % 2, :, 0:128], pr[:, k % 2, :, 0:128],
                                          sm[:, :, 0:1].broadcast_to([P, 2, 128]), ALU.mult))
                        d.to(V.tensor_tensor(pr[:, k % 2, :, 128:384], pr[:, k % 2, :, 128:384],
                                        sm[:, :, 1:2].broadcast_to([P, 2, 256]), ALU.mult), "prob_ready")
                    if m >= 2:
                        dve.wait_ge(S("o_done"), A8 + m - 1)
                        d.to(V.tensor_copy(oT[:, m - 2, :], bank[5 + m % 2][:, 0:TOK]), "o_copied")
                dve.wait_ge(S("proj_copied"), 4 + 4 * layer)

                def post(rowsb, n):
                    for t in range(NT):
                        d(V.tensor_tensor_reduce(out=hTd[:, 4 * t:4 * t + 4, :].rearrange("p a b -> p (a b)"),
                                                 in0=yt[:, t, :], in1=yt[:, t, :], scale=1.0 / D, scalar=RMS_EPS,
                                                 op0=ALU.mult, op1=ALU.add, accum_out=stat[:, t:t + 1]))
                    d.to(V.tensor_copy(stat[:, 0:2], stat[:, 0:2]), "ms_ready")
                    dve.wait_ge(S("rstd_ready"), n)
                    for t in range(NT):
                        d(V.scalar_tensor_tensor(out=yt[:, t, :], in0=yt[:, t, :], scalar=stat[:, 2 + t:3 + t],
                                                 in1=rowsb, op0=ALU.mult, op1=ALU.mult))
                        ins = V.tensor_tensor(x[:, t, :], x[:, t, :], yt[:, t, :], ALU.add)
                        if rowsb is gmixb:
                            d(ins)
                        else:
                            d.to(ins, "x4_ready" if layer == 0 else "out_ready")

                post(gmixb, rn)
                rn += 1
                mean_square(x, yt)
                gain(lm, 32, col("g_ffn_pre", 8 * layer, 8))
                scaled(yt, rn)
                rn += 1
                d.to(V.tensor_copy(stat[:, 15:16], fcol[:, 0:1]), "fcol_ready")
                evac_h(hTd, lm, 24, 12 + 8 * layer)

                F0 = NFT * layer
                cb, ww = COLS["b_conv"][0] + NFT * layer, COLS["w_conv"][0] + 66 * layer

                def conv(f, r):
                    z = bank[5 + r]
                    dve.wait_ge(S("silu_f"), f + (F0 + 1))
                    dve.wait_ge(S("gu_done"), f + (F0 + 1))
                    c = cv[:, r, :]
                    w = lambda k: cols[:, bass.ds(f + (ww + NFT * k), 1)]
                    V.tensor_scalar(c, z[:, 0:TOK], w(2), cols[:, bass.ds(f + cb, 1)], ALU.mult, ALU.add)\
                        .then_inc(S("conv_step"), 1)
                    dve.wait_ge(S("conv_step"), f * 2 + (2 * F0 + 1))
                    V.scalar_tensor_tensor(out=c[:, 1:TOK], in0=z[:, 0:TOK - 1], scalar=w(1), in1=c[:, 1:TOK],
                                           op0=ALU.mult, op1=ALU.add).then_inc(S("conv_step"), 1)
                    dve.wait_ge(S("conv_step"), f * 2 + (2 * F0 + 2))
                    V.scalar_tensor_tensor(out=c[:, 2:TOK], in0=z[:, 0:TOK - 2], scalar=w(0), in1=c[:, 2:TOK],
                                           op0=ALU.mult, op1=ALU.add).then_inc(S("conv_done"), 1)

                def gated(f, r):
                    dve.wait_ge(S("silu_f"), f + (F0 + 3))
                    V.tensor_tensor(actF[:, 0, r, :], sv[:, r, :], bank[5 + r][:, TOK:2 * TOK], ALU.mult)\
                        .then_inc(S("act_f"), 1)

                with dve.Fori(0, NFT // 2, 1) as i:
                    for r in range(2):
                        conv(i * 2 + r, r)
                        gated(i * 2 + r, r)
                dve.wait_ge(S("down_copied"), 4 + 4 * layer)
                post(gffnb, rn)
                rn += 1

        @block.scalar
        def _(act):
            A = nc.scalar.activation
            a_ = Chain(act, S, "scalar_step")
            act.wait_ge(S("cols_in"), 16)
            a_.to(A(silc, col("c2", 0, 8), ACT.Silu), "silu_c")
            act.nop().then_inc(S("silu_f"), 2)
            act.nop().then_inc(S("silu_done"), 1)
            act.nop().then_inc(S("ys_copied"), 1)

            def evac_h(dst, lm, sh0, n, fc):
                act.wait_ge(S("fcol_ready"), fc)
                for c in (2, 3, 6, 7):
                    act.wait_ge(S("turned"), n + c // 2 + 1)
                    o = (c % 2) * TOK
                    a_.to(A(dst[:, c, :], bank[1 + c // 2][:, o:o + TOK], ACT.Identity, bias=modc[:, lm, sh0 + c:sh0 + c + 1],
                      scale=fcol[:, c:c + 1]), "h_ready_s")

            evac_h(hT, 0, 0, 0, 1)
            UB = [1, 2, 3, 4, 5, 6]
            for u in range(7):
                b = bank[UB[u % 6]]
                act.wait_ge(S("unit_ready"), u + 1)
                for mi in range(2):
                    if u < 6:
                        m = 2 * (u % 2) + mi
                        dst, k, rows_ = (rT, kT, vT)[u // 2][:, m, :], (u // 2) * 4 + m, P
                    else:
                        dst, k, rows_ = (xwa, xg)[mi], 12 + mi, (64, 96)[mi]
                    a_.to(A(dst[0:rows_, :], b[0:rows_, mi * TOK:(mi + 1) * TOK], ACT.Copy,
                      scale=omm[0:rows_, k:k + 1]), "shift_ready")
            act.wait_ge(S("unit_free"), 7)
            a_.to(A(xwa[0:32, :], xwa[0:32, :], ACT.Tanh), "lowrank_ready")
            a_.to(A(xg[0:96, :], xg[0:96, :], ACT.Sigmoid), "lowrank_ready")
            for u in range(7, 11):
                act.wait_ge(S("unit_ready"), u + 1)
                b = bank[UB[u % 6]]
                if u < 9:
                    a_.to(A(gv[:, u - 7, :], b[:, :], ACT.Gelu_apprx_tanh, accum_out=stat[:, 4 + u - 7:5 + u - 7]), "gelu_done")
                else:
                    h_ = 2 * (u - 9)
                    a_.to(A(yaT[:, h_:h_ + 2, :], b.rearrange("p (m t) -> p m t", m=2), ACT.Gelu_apprx_tanh), "gelu_done")
            act.wait_ge(S("lora_done"), 2)
            for nm, dst, b0, bias in (("sw_ready", sw, 1, "w0"), ("a_ready", aT, 3, "a0")):
                for m in range(NM):
                    A(dst[:, m, :], bank[b0 + m // 2][:, (m % 2) * TOK:(m % 2 + 1) * TOK], ACT.Sigmoid,
                      bias=col(bias, m)).then_inc(S(nm), 1)
            for k in range(2):
                a_.to(A(gT[:, 2 * k:2 * k + 2, :], bank[5 + k].rearrange("p (m t) -> p m t", m=2), ACT.Copy), "g_ready")
            for k in range(2):
                act.wait_ge(S("kk_sums"), k + 1)
                if k == 0:
                    act.wait_ge(S("kk_sums"), 2)
                a_.to(A(tmp1[:, 2 * k:2 * k + 2, :], (bank[7] if k else bank[1]).rearrange("p (m t) -> p m t", m=2), ACT.Sqrt), "kk_norm")
            act.wait_ge(S("cum_done"), 1)
            a_.to(A(eL, cum, ACT.Exp, scale=-DECAY), "exps_done")
            act.wait_ge(S("exps_done"), 1)
            a_.to(A(cum, cum, ACT.Exp, scale=DECAY), "exps_done")
            a_.to(A(sw, sw, ACT.Exp, scale=-DECAY), "exps_done")
            for q, dst in ((0, tokv), (2, tokk)):
                for t in range(NT):
                    act.wait_ge(S("tok_turned"), 2 * q + t + 1)
                    a_.to(A(dst[:, t, :], bank[1 + 2 * q + t][:, :], ACT.Copy), "tok_copied")
            for n in range(24):
                T, l, g = n // 12, (n % 12) // 2, n % 2
                act.wait_ge(S("xt_done"), n + 1)
                a_.to(A(XT[:, T * 8 + 4 * g:T * 8 + 4 * g + 4, :], bank[3 + 3 * g].rearrange("p (j t) -> p j t", j=4),
                  ACT.Copy), "xt_ready")
            for k in range(2):
                act.wait_ge(S("gn_var"), k + 1)
                act.wait_ge(S("ysq_ready"), 2)
                a_.to(A(yv[:, 2 * k:2 * k + 2, :], bank[3 + k].rearrange("p (m t) -> p m t", m=2), ACT.Sqrt, bias=gneps,
                  scale=1.0 / HD), "gn_std")

            def row_copies(dst, n, b0):
                for k in range(2):
                    act.wait_ge(S("rows_done"), 2 * (n - 1) + k + 1)
                    a_.to(A(dst[:, 512 * k:512 * (k + 1)], bank[b0 + k][:, :], ACT.Copy), "rows_copied")

            act.wait_ge(S("mix_done"), 1)
            row_copies(gate1b, 1, 3)
            row_copies(sc2b, 2, 3)
            row_copies(sh2b, 3, 1)
            row_copies(gate2b, 4, 5)
            for u in range(4):
                act.wait_ge(S("turned"), 4 + u + 1)
                a_.to(A(h2T[:, 2 * u:2 * u + 2, :], bank[1 + u].rearrange("p (m t) -> p m t", m=2), ACT.Copy), "h2T_ready")
            for t in range(NT):
                o = 128 * t
                act.wait_ge(S("g_max"), t + 1)
                a_.to(A(rt[:, o + 40:o + 44], rt[:, o:o + 4], ACT.Exp, bias=rt[:, o + 101:o + 102],
                  accum_out=rt[:, o + 93:o + 94]), "g_sum")
                act.wait_ge(S("e_gap"), t + 1)
                a_.to(A(rt[:, o + 94:o + 95], rt[:, o + 94:o + 95], ACT.Exp), "e_exp")
            for k in range(2):
                act.wait_ge(S("pwt_done"), k + 1)
                a_.to(A(pwT[:, 2 * k:2 * k + 2, :], bank[5 + k].rearrange("p (m t) -> p m t", m=2), ACT.Copy), "pwt_copied")
            act.wait_ge(S("mtab_ready"), 1)
            act.wait_ge(S("iota_made"), 2)
            act.nop().then_inc(S("ym_ready"), 1)

            def pass_(start, done):
                act.wait_ge(S("gate_done"), done)
                act.wait_ge(S("act_done"), done)
                A(sg, bank[1][:, 0:4 * WIN], ACT.Silu).then_inc(S("silu_done"), 1)
                act.wait_ge(S("down_done"), done + 1)
                act.wait_ge(S("y_turned"), done)
                A(ym, bank[3][:, :], ACT.Copy).then_inc(S("ym_ready"), 1)
                act.wait_ge(S("y_turned"), done + 1)
                act.wait_ge(S("ys_copied"), done)
                A(ysT[:, :, bass.ds(start, WIN)].rearrange("p (h j) w -> p j h w", h=2),
                  bank[5].rearrange("p (j h w) -> p j h w", j=4, h=2), ACT.Copy).then_inc(S("ys_copied"), 1)

            within = "the passes of an expert begin within its slots"
            with act.Fori(0, NE, 1) as i:
                start = act.value_load(mtab[0:1, bass.ds(i, 1)], min_val=0, max_val=SLOTS)
                extra = act.value_load(mtab[0:1, bass.ds(i + NE, 1)], min_val=0, max_val=3)
                before = act.value_load(mtab[0:1, bass.ds(i + 2 * NE, 1)], min_val=1, max_val=4 * NE)
                with act.If(extra > 0):
                    with act.Fori(0, extra, 1) as w:
                        pass_(nc.s_assert_within(start + w * WIN, 0, SLOTS, skip_runtime_bounds_check_because=within),
                              before + w)
                pass_(nc.s_assert_within(start + extra * WIN, 0, SLOTS, skip_runtime_bounds_check_because=within),
                      before + extra)
            for s in range(4):
                act.wait_ge(S("ys_turned"), 2 * s + 2)
                a_.to(A(ys[:, s, 512:1024], bank[1 + (2 * s + 1) % 6][:, :], ACT.Copy), "yst_copied1")
            for layer in range(2):
                lm = 1 + layer
                row_copies(gmixb, 5 + 2 * layer, 5)
                row_copies(gffnb, 6 + 2 * layer, 5)
                evac_h(hTd, lm, 0, 8 + 8 * layer, 2 + 2 * layer)
                for u in range(4):
                    act.wait_ge(S("qk_done"), 8 * layer + 1 + u)
                    a_.to(A(QT[:, 2 * u:2 * u + 2, :], bank[1 + u].rearrange("p (m t) -> p m t", m=2), ACT.Copy,
                      scale=HD ** -0.5), "q_copied")
                for u in range(4):
                    act.wait_ge(S("v_done"), 4 * layer + 1 + u)
                    a_.to(A(Vd[:, u % 2, 512 * (u // 2):512 * (u // 2 + 1)], bank[1 + (8 + u) % 6][:, :], ACT.Copy), "v_copied")
                A8 = 8 * layer
                if layer == 1:
                    H_ = slice(0, NHA)
                    act.wait_ge(S("fg_abs"), 1)
                    a_(A(cumf[H_, :], cumf[H_, :], ACT.Exp))
                    a_.to(A(cumf[H_, :], cumf[H_, :], ACT.Ln, bias=onecol[H_, :]), "fg_log")
                for m in range(8 + 2):
                    if layer == 0:
                        if m < 8:
                            act.wait_ge(S("abs_done"), m + 1)
                            a_(A(t1[:, m % 2], t1[:, m % 2], ACT.Exp))
                            a_.to(A(t1[:, m % 2], t1[:, m % 2], ACT.Ln, bias=onecol), "log_done")
                        if 1 <= m <= 8:
                            k = m - 1
                            act.wait_ge(S("sums_done"), k + 1)
                            if k >= 2:
                                act.wait_ge(S("o_done"), A8 + k - 1)
                            z = psum[:, 1 + 2 * (k % 2):3 + 2 * (k % 2), 0:384]
                            a_.to(A(pr[:, k % 2], z, ACT.Exp), "prob_ready")
                    else:
                        if m < 8:
                            act.wait_ge(S("neg_max"), m + 1)
                            if m >= 2:
                                act.wait_ge(S("pt_done"), m - 1)
                            for hh in range(2):
                                z = bank[1 + 2 * (m % 2) + hh]
                                for t in range(NT):
                                    zs = slice(128, 384) if t else slice(0, 128)
                                    k = 2 * hh + t
                                    ins = A(pr[:, m % 2, hh, zs], z[:, zs], ACT.Exp,
                                            bias=stat[:, 4 + 4 * (m % 2) + k:5 + 4 * (m % 2) + k],
                                            accum_out=small[:, 80 + 4 * (m % 2) + k:81 + 4 * (m % 2) + k])
                                    a_(ins) if k < 3 else a_.to(ins, "exp_done")
                        if 1 <= m <= 8:
                            k = m - 1
                            act.wait_ge(S("pt_done"), k + 1)
                            if k >= 2:
                                act.wait_ge(S("o_done"), A8 + k - 1)
                            a_(A(t1[:, k % 2, 0], bank[0][:, 0:384], ACT.Copy))
                            a_.to(A(t1[:, k % 2, 1], bank[7][:, 0:384], ACT.Copy), "pt_copied")
                for u in range(4):
                    act.wait_ge(S("proj_done"), 4 * layer + 1 + (2 * (u % 2) + u // 2 if False else u))
                    t, n = u % 2, u // 2
                    a_.to(A(yt[:, t, 512 * n:512 * (n + 1)], bank[1 + 2 * t + n][:, :], ACT.Copy), "proj_copied")
                evac_h(hTd, lm, 24, 12 + 8 * layer, 3 + 2 * layer)
                F0 = NFT * layer
                with act.Fori(0, NFT // 2, 1) as i:
                    for r in range(2):
                        act.wait_ge(S("conv_done"), i * 2 + (F0 + r + 1))
                        A(sv[:, r, :], cv[:, r, :], ACT.Silu).then_inc(S("silu_f"), 1)
                act.wait_ge(S("ffn_done"), layer + 1)
                for u in range(4):
                    t, n = u // 2, u % 2
                    a_.to(A(yt[:, t, 512 * n:512 * (n + 1)], bank[1 + u][:, :], ACT.Copy), "down_copied")


def column_pack(v):
    out = np.zeros((P, NCOL), np.float32)

    def put(name, w):
        o, n = COLS[name]
        out[:w.shape[0], o:o + w.shape[1]] = w

    full = lambda w: np.reshape(w, (-1, P)).T
    mu = v["rwkv_mu"][0]
    put("c1", full(v["c"]))
    put("ada_b", full(v["ada_b"]))
    put("norm1_g", full(v["norm1_g"]))
    put("mu_rkv", full(mu[:3 * HALF]))
    put("mu_wa", mu[3 * HALF:3 * HALF + 64][:, None])
    put("mu_g", mu[3 * HALF + 64:][:, None])
    for name in ("w0", "a0", "k_k", "k_a", "r_k", "gn_w", "gn_b"):
        put(name, full(v["rwkv_" + name]))
    put("norm2_g", full(v["norm2_g"]))
    put("c2", full(v["c_2"]))
    for layer in range(2):
        put(f"b_mod{layer}", full(v["b_mod_2"][layer]))
    for name in ("g_mix_pre", "g_mix_post", "g_ffn_pre", "g_ffn_post", "w_conv", "b_conv"):
        put(name, full(v[name + "_2"]))
    put("b_fg", v["b_fg_2"][0][:, None])
    return out


def kernel(**v):
    import concourse.bacc as bacc
    from concourse.bass_utils import run_bass_kernel_spmd

    v = {k: np.asarray(w) for k, w in v.items()}
    cont = np.ascontiguousarray
    arrays = {
        "cols": column_pack(v),
        "x": v["x"][0],
        "ada_w": v["ada_w"][0],
        "w_in": v["w_in"][0],
        "lora": cont(np.concatenate([v["rwkv_w2"][0], v["rwkv_a2"][0]], axis=0)),
        "g2": v["rwkv_g2"][0],
        "ln_w": v["gmlp_ln_w"][0],
        "ln_b": v["gmlp_ln_b"][0],
        "bs": cont(np.reshape(v["gmlp_bs"][0], (NM, 2, P)).transpose(1, 0, 2)),
        "ws": cont(v["gmlp_ws"][0].transpose(2, 0, 1)),
        "w_out": v["w_out"][0],
        "router_w": cont(np.concatenate([v["router_group_w"][0], v["router_expert_w"][0]], axis=1)),
        "router_b": cont(np.concatenate([v["router_group_b"][0], v["router_expert_b"][0]])),
        "moe_gate": v["moe_w_gate"][0],
        "moe_up": v["moe_w_up"][0],
        "moe_down": v["moe_w_down"][0],
        "final_g": v["final_norm_g"],
        "w_fg": v["w_fg_2"][0],
    }
    for layer in range(2):
        arrays[f"w_mod{layer}"] = v["w_mod_2"][layer]
        arrays[f"w_qkv{layer}"] = v["w_qkv_2"][layer]
        arrays[f"w_o{layer}"] = v["w_o_2"][layer]
        for k in ("gate", "up", "down"):
            arrays[f"w_ffn_{k}{layer}"] = v[f"w_ffn_{k}_2"][layer]
    nc = bacc.Bacc("TRN2", target_bir_lowering=False, num_devices=1)
    aps = {k: nc.dram_tensor("in_" + k, w.shape, mybir.dt.from_np(w.dtype), kind="ExternalInput").ap()
           for k, w in arrays.items()}
    aps["out"] = nc.dram_tensor("out", (TOK, D), F32, kind="ExternalOutput").ap()
    build_program(nc, aps)
    r = run_bass_kernel_spmd(nc, [{"in_" + k: w for k, w in arrays.items()}], core_ids=[0])
    return np.reshape(r.results[0]["out"], (1, TOK, D))
```

```python
from contextlib import ExitStack

import numpy as np

import concourse.bass as bass
from concourse import mybir

F32 = mybir.dt.float32
I32 = mybir.dt.int32
U32 = mybir.dt.uint32
ALU = mybir.AluOpType
ACT = mybir.ActivationFunctionType
AX = mybir.AxisListType

P = 128
D = 1024
TOK = 256
NT = TOK // P
DC = D // P
HALF = 512
NM = HALF // P
HD = 64
NHR = HALF // HD
CH = 64
NE, HID = 32, 512
NG, EPG = 4, 8
WIN = 64
SLOTS = 2 * TOK
NHA = 16
FF = 2816
NFT = FF // P
RING = 6
SLOTF = 4096
RMS_EPS, LN_EPS, GN_EPS = 1e-6, 1e-5, 64e-5
DECAY = float(np.exp(-0.5))
NEG = -1e30

COLS = {}
_n = 0
for _name, _w in [("c1", 8), ("ada_b", 48), ("norm1_g", 8), ("mu_rkv", 12), ("mu_wa", 1), ("mu_g", 1),
                  ("w0", 4), ("a0", 4), ("k_k", 4), ("k_a", 4), ("r_k", 4), ("gn_w", 4), ("gn_b", 4),
                  ("norm2_g", 8), ("c2", 8), ("b_mod0", 48), ("b_mod1", 48), ("g_mix_pre", 16),
                  ("g_mix_post", 16), ("g_ffn_pre", 16), ("g_ffn_post", 16), ("w_conv", 132),
                  ("b_conv", 44), ("b_fg", 1)]:
    COLS[_name] = (_n, _w)
    _n += _w
NCOL = _n


class Sems:

    def __init__(self, nc, ctx):
        self.nc, self.ctx, self.made = nc, ctx, {}

    def __call__(self, name):
        if name not in self.made:
            self.made[name] = self.ctx.enter_context(self.nc.semaphore(name))
        return self.made[name]


class Chain:

    def __init__(self, eng, named, name):
        self.eng, self.named, self.sem, self.n, self.told = eng, named, named(name), 0, {}

    def __call__(self, ins):
        self.n += 1
        ins.then_inc(self.sem, 1)
        self.eng.wait_ge(self.sem, self.n)

    def to(self, ins, name):
        self.told[name] = self.told.get(name, 0) + 1
        ins.then_inc(self.named(name), 1)
        self.eng.wait_ge(self.named(name), self.told[name])


class Stream:

    def __init__(self):
        self.n = 0

    def take(self):
        n = self.n
        self.n += 1
        return n % RING, n // RING + 1, n


def build_program(nc, a):
    with ExitStack() as ctx:
        S = Sems(nc, ctx)

        def sb(name, shape, dt=F32):
            return ctx.enter_context(nc.sbuf_tensor(name, shape, dt))

        psum = ctx.enter_context(nc.psum_tensor("psum", [P, 8, 512], F32))
        bank = [psum[:, i, :] for i in range(8)]
        ring = sb("ring", [P, RING, SLOTF])
        AR = 23040
        arena = sb("arena", [P, AR])

        def at(off, *shape):
            n = int(np.prod(shape))
            assert off + n <= AR
            v = arena[:, off:off + n]
            if len(shape) == 1:
                return v
            names = "abcd"[:len(shape)]
            return v.rearrange(f"p ({' '.join(names)}) -> p {' '.join(names)}",
                               **{k: s for k, s in zip(names, shape)})

        x = sb("x", [P, NT, D])
        cols = sb("cols", [P, NCOL])
        ident = sb("ident", [P, P])
        ones = sb("ones", [P, P])
        bones = sb("bones", [P, P])
        upper = sb("upper", [P, P])
        upper_inc = sb("upper_inc", [P, P])
        mask_ar = sb("mask_ar", [P, 2, P])
        level = sb("level", [P, 6, P])
        keep1 = level[0:NHA, 1:3, :].rearrange("p a b -> p (a b)")
        modc = sb("modc", [P, 3, 48])
        small = sb("small", [P, 96])
        omm = small[:, 0:14]
        omka = small[:, 14:18]
        stat = small[:, 18:34]
        negone = small[:, 34:35]
        onecol = small[:, 35:36]
        gneps = small[:, 36:37]
        powh = small[:, 38:40]
        fcol = small[:, 40:48]
        dend = small[:, 48:64].rearrange("p (m c) -> p m c", m=NM)
        silc = small[:, 64:72]
        spare = small[:, 72:80]
        mtab = level[0:1, 0, 0:3 * NE + 1].bitcast(I32)

        def col(name, i=0, n=1):
            o = COLS[name][0] + i
            return cols[:, o:o + n]

        hT = at(0, DC, TOK)
        xn = at(2048, NT, D)
        gv = at(2048, NT, HALF)
        wsT = at(3072, NHR, P)
        rT, kT, vT = at(4096, NM, TOK), at(5120, NM, TOK), at(6144, NM, TOK)
        xwa, xg = at(7168, TOK), at(7424, TOK)
        sw, cum = at(7680, NM, TOK), at(8704, NM, TOK)
        aT, eL = at(9728, NM, TOK), at(10752, NM, TOK)
        kkn, tmp1, tmp2 = at(11776, NM, TOK), at(12800, NM, TOK), at(13824, NM, TOK)
        tokv, tokb, tokk = at(0, NT, HALF), at(1024, NT, HALF), at(2048, NT, HALF)
        gram = at(3072, 16, 512)
        Xi = at(11264, 8, P)
        XT = at(12288, 16, P)
        Pm = at(14336, 2, 4, P)
        Pb = at(15360, 512)
        arT = at(15872, 2, NM, TOK)
        bkT = at(17920, 2, NM, TOK)
        lora = at(15872, 512)
        g2s = at(16384, 512)
        lnw, lnb = at(17920, 512), at(18432, 512)
        bsb = at(18944, NM, P)
        keep = at(19456, TOK)
        U = at(17920, NT, 512)
        Mst = at(18944, NM, P)
        DCm = at(19456, NM, P)
        gT, bonus, yaT = at(19968, NM, TOK), at(20992, NM, TOK), at(22016, NM, TOK)
        ybT = at(3072, NM, TOK)
        yv, yd, ysq = at(4096, NM, TOK), at(5120, NM, TOK), at(6144, NM, TOK)

        h2 = at(0, NT, D)
        h2T = at(2048, DC, TOK)
        perm = at(4096, NT, SLOTS)
        pw = at(5120, NT, SLOTS)
        pwT = at(6144, 4, TOK)
        xsT = at(7168, DC, SLOTS + WIN)
        ysT = at(11776, DC, SLOTS + WIN)
        actT = at(16384, 2, P)
        sg = at(16640, 4 * WIN)
        xw = at(17920, DC, WIN)
        ym = at(18432, 512)
        actm = at(18944, 4 * WIN)
        gate2b = at(16896, D)
        sc2b, sh2b = at(17920, D), at(18944, D)
        gate1b = at(19968, D)
        fgb = at(20992, D)
        rt = at(22016, 1024)
        iota = at(11776, SLOTS)
        diag = at(7680, 4, DC, P)
        pw_second = at(12288, SLOTS)
        rw = at(13312, DC, 36)
        rb = at(13600, 36)
        ys = at(0, 4, D)

        hTd = at(0, DC, TOK)
        QT, KT, Vd = at(2048, DC, TOK), at(4096, DC, TOK), at(6144, NT, D)
        oT = at(8192, DC, TOK)
        yt = at(10240, NT, D)
        gmixb, gffnb = at(12288, D), at(13312, D)
        diagd = at(14336, DC, P)
        t1 = at(15360, 2, 2, 384)
        sp_ = at(16896, 2, 2, 384)
        pr = at(18432, 2, 2, 384)
        cumf = at(19968, TOK)
        ncumf = at(20224, TOK)
        wfg = at(20480, DC, NHA)
        neg_lower = at(20608, P)
        neg_ones = at(20736, P)
        neg_ge = at(20864, P)
        neg_gt = at(20992, P)
        actF = at(15360, 2, 2, TOK)
        cv = at(16896, 2, TOK)
        sv = at(17920, 2, TOK)

        macc = sb("macc", [P, 2, 256])
        maccv = at(13824, 2, 512)
        part = bank[0][:, 256:512]
        mod_at = []

        st_sp = Stream()
        st_pe = Stream()

        def w_cols(w, c0, n=512):
            return w[:, c0:c0 + n].rearrange("(c p) n -> p c n", p=P)

        block = ctx.enter_context(nc.Block())

        @block.sync
        def _(sp):
            def load(src, n):
                s, _, i = st_sp.take()
                if i >= RING:
                    sp.wait_ge(S("slot_freed"), i - RING + 1)
                sp.dma_start(ring[:, s, 0:n].rearrange("p (c n) -> p c n", c=src.shape[1]), src)\
                    .then_inc(S(f"slot{s}_loaded"), 16)

            sp.dma_start(cols[:, :], a["cols"]).then_inc(S("cols_in"), 16)
            sp.dma_start(x[:, :, :], a["x"].rearrange("(t p) d -> p t d", p=P)).then_inc(S("x_in"), 16)
            def load_mod(w, i):
                mod_at.append(st_sp.n)
                load(w_cols(a[w], 512 * i), 4096)

            for i in range(4):
                load_mod("ada_w", i)
            sp.dma_start(lora[0:64, :], a["lora"]).then_inc(S("lora_in"), 16)
            sp.dma_start(g2s[0:96, :], a["g2"]).then_inc(S("lora_in"), 16)
            sp.dma_start(lnw, a["ln_w"].partition_broadcast(P)).then_inc(S("ln_in"), 16)
            sp.dma_start(lnb, a["ln_b"].partition_broadcast(P)).then_inc(S("ln_in"), 16)
            for half in range(2):
                sp.dma_start(bsb[64 * half:64 * half + 64, :, :],
                             a["bs"][half].partition_broadcast(64)).then_inc(S("ln_in"), 16)
            for i in range(3):
                load(w_cols(a["w_in"], D + 512 * i), 4096)
            load(w_cols(a["w_in"], D + 3 * HALF, 160), 1280)
            load(w_cols(a["w_in"], HALF), 4096)
            load(w_cols(a["w_in"], 0), 4096)
            sp.wait_ge(S("turned"), 4)
            sp.dma_start(wsT, a["ws"]).then_inc(S("ws_in"), 16)
            for i in range(4, 12):
                load_mod("ada_w", i)
            for i in range(12):
                load_mod("w_mod0", i)
            for i in range(2):
                load(w_cols(a["w_out"], 512 * i), 4096)
            sp.wait_ge(S("x1_ready"), 2)
            sp.dma_start(fgb, a["final_g"].partition_broadcast(P)).then_inc(S("router_in"), 16)
            sp.dma_start(rw, a["router_w"].rearrange("(c p) n -> p c n", p=P)).then_inc(S("router_in"), 16)
            sp.dma_start(rb, a["router_b"].partition_broadcast(P)).then_inc(S("router_in"), 16)
            moe_n0 = st_sp.n
            with sp.Fori(0, NE // 2, 1) as i:
                for e in range(2):
                    for k, w in enumerate(("moe_gate", "moe_up", "moe_down")):
                        n = moe_n0 + 3 * e + k
                        s = n % RING
                        sp.wait_ge(S("slot_freed"), i * RING + (n - RING + 1))
                        src = a[w][bass.ds(i * 2 + e, 1), :, :].rearrange("o (c p) n -> p (o c) n", p=P)
                        sp.dma_start(ring[:, s, :].rearrange("p (c n) -> p c n", c=src.shape[1]), src)\
                            .then_inc(S(f"slot{s}_loaded"), 16)
            st_sp.n += 3 * NE
            for layer in range(2):
                if layer == 0:
                    for i in range(2):
                        load_mod("w_mod1", i)
                for i in range(6):
                    load(w_cols(a[f"w_qkv{layer}"], 512 * i), 4096)
                if layer == 0:
                    sp.wait_ge(S("x2_ready"), 2)
                    sp.dma_start(wfg, a["w_fg"].rearrange("(c p) n -> p c n", p=P)).then_inc(S("fg_in"), 16)
                    for i in range(2, 10):
                        load_mod("w_mod1", i)
                for i in range(2):
                    load(w_cols(a[f"w_o{layer}"], 512 * i), 4096)
                if layer == 0:
                    for i in range(10, 12):
                        load_mod("w_mod1", i)
                n0 = st_sp.n
                wg, wu, wd = (a[f"w_ffn_{k}{layer}"] for k in ("gate", "up", "down"))

                def ffn_group(g, w, n, i):
                    wide = bass.ds(g * 512, w)
                    for k, src in enumerate((wg[:, wide].rearrange("(c p) n -> p c n", p=P),
                                             wu[:, wide].rearrange("(c p) n -> p c n", p=P),
                                             wd[wide, :].rearrange("(c p) n -> p c n", p=P))):
                        s = (n + k) % RING
                        sp.wait_ge(S("slot_freed"), i * RING + (n + k - RING + 1))
                        sp.dma_start(ring[:, s, 0:8 * w].rearrange("p (c n) -> p c n", c=src.shape[1]), src)\
                            .then_inc(S(f"slot{s}_loaded"), 16)

                ffn_group(0, 512, n0, 0)
                with sp.Fori(0, 2, 1) as i:
                    for k in range(2):
                        ffn_group(i * 2 + (1 + k), 512, n0 + 3 + 3 * k, i)
                ffn_group(5, 256, n0 + 15, 0)
                st_sp.n += 18
            for t in range(NT):
                sp.wait_ge(S("out_ready"), t + 1)
                sp.dma_start(a["out"][t * P:(t + 1) * P, :], x[:, t, :]).then_inc(S("out_stored"), 16)
            sp.wait_ge(S("out_stored"), 16 * NT)

        @block.gpsimd
        def _(pool):
            g = Chain(pool, S, "pool_step")
            nc.gpsimd.memset(small[:, 34:35], -1.0)
            nc.gpsimd.memset(onecol, 1.0)
            nc.gpsimd.memset(gneps, GN_EPS)
            g(nc.gpsimd.memset(powh, -0.5))
            nc.gpsimd.memset(ones[:, :], 1.0).then_inc(S("consts"), 1)
            g(nc.gpsimd.memset(ident[:, :], 0.0))
            nc.gpsimd.affine_select(out=ident[:, :], in_=ident[:, :], compare_op=ALU.not_equal, fill=1.0, base=0,
                                    pattern=[[-1, P]], channel_multiplier=1).then_inc(S("consts"), 1)

            def rsqrt_of(n, ts=slice(0, 2)):
                pool.wait_ge(S("ms_ready"), n)
                nc.gpsimd.tensor_tensor(stat[:, 2:4][:, ts], stat[:, 0:2][:, ts], powh[:, ts], ALU.pow).then_inc(S("rstd_ready"), 1)

            rsqrt_of(1)
            pool.wait_ge(S("consts"), 2)
            g(nc.gpsimd.affine_select(out=bones[:, 0:64], in_=ones[:, 0:64], compare_op=ALU.is_ge, fill=0.0, base=63,
                                      pattern=[[0, 64]], channel_multiplier=-1))
            nc.gpsimd.affine_select(out=bones[:, 64:128], in_=ones[:, 64:128], compare_op=ALU.is_ge, fill=0.0,
                                    base=-64, pattern=[[0, 64]], channel_multiplier=1).then_inc(S("upper_made"), 1)
            for t_, cmp in ((upper[:, :], ALU.is_gt), (upper_inc[:, :], ALU.is_ge)):
                nc.gpsimd.affine_select(out=t_, in_=ones[:, :], compare_op=cmp, fill=0.0, base=0,
                                        pattern=[[1, P]], channel_multiplier=-1).then_inc(S("upper_made"), 1)
            pool.wait_ge(S("upper_made"), 3)
            nc.gpsimd.tensor_tensor(mask_ar[:, 0, :], bones[:, :], upper[:, :], ALU.mult).then_inc(S("masks_made"), 1)
            nc.gpsimd.tensor_tensor(mask_ar[:, 1, :], bones[:, :], upper_inc[:, :], ALU.mult).then_inc(S("masks_made"), 1)
            g(nc.gpsimd.memset(keep[:, :], 1.0))
            nc.gpsimd.memset(keep[:, :].rearrange("p (c t) -> p c t", t=CH)[:, :, 0:1], 0.0)\
                .then_inc(S("masks_made"), 1)
            g(nc.gpsimd.memset(level[:, :, :], 0.0))
            for l in range(6):
                b = 1 << l
                v = level[:, l, :].rearrange("p (q u b) -> p q u b", u=2, b=b)[:, :, 0, :]
                n = P // (2 * b)
                g(nc.gpsimd.memset(v, 1.0))
                g(nc.gpsimd.affine_select(out=v, in_=v, compare_op=ALU.is_ge, fill=0.0, base=-b,
                                          pattern=[[-2 * b, n], [0, b]], channel_multiplier=1))
                g(nc.gpsimd.affine_select(out=v, in_=v, compare_op=ALU.is_ge, fill=0.0, base=2 * b - 1,
                                          pattern=[[2 * b, n], [0, b]], channel_multiplier=-1))
            pool.nop().then_inc(S("levels_made"), 1)
            pool.wait_ge(S("ws_in"), 16)
            nc.gpsimd.affine_select(out=wsT, in_=wsT, compare_op=ALU.is_ge, fill=0.0, base=0,
                                    pattern=[[0, NHR], [1, P]], channel_multiplier=-1).then_inc(S("ws_masked"), 1)
            rsqrt_of(2)
            rsqrt_of(3)
            pool.wait_ge(S("x1_ready"), 2)
            nc.gpsimd.iota(iota, pattern=[[1, SLOTS]], base=0, channel_multiplier=0,
                           allow_small_or_imprecise_dtypes=True).then_inc(S("iota_made"), 1)
            pool.wait_ge(S("rows_done"), 8)
            g(nc.gpsimd.memset(xsT[:, :, SLOTS:SLOTS + WIN], 0.0))
            pool.nop().then_inc(S("iota_made"), 1)
            rsqrt_of(4)
            pool.wait_ge(S("x2_ready"), 2)
            g(nc.gpsimd.memset(neg_lower, -1.0))
            g(nc.gpsimd.memset(keep1, 1.0))
            nc.gpsimd.memset(neg_ones, -1.0)
            nc.gpsimd.memset(neg_ge, NEG)
            g(nc.gpsimd.memset(neg_gt, NEG))
            nc.gpsimd.affine_select(out=neg_lower, in_=neg_lower, compare_op=ALU.is_ge, fill=0.0, base=0,
                                    pattern=[[-1, P]], channel_multiplier=1).then_inc(S("neg_made"), 1)
            nc.gpsimd.affine_select(out=neg_ge, in_=neg_ge, compare_op=ALU.is_ge, fill=0.0, base=0,
                                    pattern=[[-1, P]], channel_multiplier=1).then_inc(S("neg_made"), 1)
            nc.gpsimd.affine_select(out=neg_gt, in_=neg_gt, compare_op=ALU.is_gt, fill=0.0, base=0,
                                    pattern=[[1, P]], channel_multiplier=-1).then_inc(S("neg_made"), 1)
            for layer in range(2):
                rsqrt_of(5 + 6 * layer)
                for t in range(NT):
                    for k in range(2):
                        rsqrt_of(6 + 6 * layer + 2 * t + k, slice(t, t + 1))
                rsqrt_of(10 + 6 * layer)

        @block.tensor
        def _(pe):
            mm = nc.tensor.matmul

            def take():
                s, use, n = st_pe.take()
                pe.wait_ge(S(f"slot{s}_loaded"), 16 * use)
                fresh[0] = n > 0 and not ahead[0]
                ahead[0] = False
                return ring[:, s, :]

            fresh = [False]
            ahead = [False]

            def opened(ins):
                if fresh[0]:
                    fresh[0] = False
                    ins.then_inc(S("slot_freed"), 1)

            def first_slice(k):
                take()
                pe.wait_ge(S("mod_sums"), k + 1)
                for q in range(4):
                    last = mm(bank[0][:, 4 * k + q:4 * k + q + 1], maccv[:, k % 2, q * P:(q + 1) * P], ones[:, 0:1],
                              start=True, stop=True)
                    opened(last)
                last.then_inc(S("mod_cols"), 1)

            halves = [0, None]

            def flush():
                if halves[1] is None:
                    return
                pe.wait_ge(S("part_copied"), halves[0])
                for q in range(2):
                    last = mm(bank[0][:, halves[1] + q:halves[1] + q + 1],
                              macc[:, (halves[0] - 1) % 2, q * P:(q + 1) * P], ones[:, 0:1], start=True, stop=True)
                last.then_inc(S("mod_cols"), 1)
                halves[1] = None

            def half_slice(k, half, vec, o):
                if half == 0:
                    half_slice.w = take()[:, 0:4096].rearrange("p (c n) -> p c n", c=DC)
                w = half_slice.w
                flush()
                if (k, half) in ((4, 0), (12, 0), (24, 0)):
                    pe.wait_ge(S("mod_copied"), {4: 1, 12: 2, 24: 3}[k])
                    pe.wait_ge(S("silu_c"), 1)
                for c in range(DC):
                    g = 32 * (c % 4)
                    last = mm(part[g:g + 1, :], vec[:, c:c + 1], w[:, c, half * 256:(half + 1) * 256],
                              start=(c < 4), stop=(c >= 4), tile_position=(0, g))
                    opened(last)
                last.then_inc(S("part_done"), 1)
                halves[0] += 1
                halves[1] = o

            def h_chunk(n, c):
                pe.wait_ge(S("h_ready_s" if c % 4 >= 2 else "h_ready_v"), 4 * (n - 1) + c % 2 + 1 + 2 * (c // 4))

            pe.wait_ge(S("cols_in"), 16)
            pe.wait_ge(S("consts"), 2)
            pe.wait_ge(S("xn_ready"), 1)
            pe.wait_ge(S("xn_ready_s"), 1)
            for u in range(4):
                for cc in range(2):
                    for t in range(NT):
                        last = nc.tensor.transpose(bank[1 + u][:, (2 * cc + t) * P:(2 * cc + t + 1) * P],
                                                   xn[:, t, (2 * u + cc) * P:(2 * u + cc + 1) * P], ident[:, :])
                last.then_inc(S("turned"), 1)
            for k in range(4):
                first_slice(k)
            unit = 0
            UB = [1, 2, 3, 4, 5, 6]
            for q in range(3):
                w = take()[:, 0:4096].rearrange("p (c n) -> p c n", c=DC)
                for half in range(2):
                    if unit >= 6:
                        pe.wait_ge(S("unit_free"), unit - 5)
                    b = bank[UB[unit % 6]]
                    for mi in range(2):
                        m = 2 * half + mi
                        for c in range(DC):
                            if unit == 0 and mi == 0:
                                h_chunk(1, max(c, 1))
                            last = mm(b[:, mi * TOK:(mi + 1) * TOK], w[:, c, m * P:(m + 1) * P], hT[:, c, :],
                                      start=(c == 0), stop=(c == DC - 1))
                            opened(last)
                    last.then_inc(S("unit_ready"), 1)
                    unit += 1
            w = take()[:, 0:1280].rearrange("p (c n) -> p c n", c=DC)
            pe.wait_ge(S("unit_free"), unit - 5)
            b = bank[UB[unit % 6]]
            for c in range(DC):
                opened(mm(b[0:64, 0:TOK], w[:, c, 0:64], hT[:, c, :], start=(c == 0), stop=(c == DC - 1)))
            for c in range(DC):
                last = mm(b[0:96, TOK:2 * TOK], w[:, c, 64:160], hT[:, c, :], start=(c == 0), stop=(c == DC - 1))
            last.then_inc(S("unit_ready"), 1)
            unit += 1
            w = take()[:, 0:4096].rearrange("p (c n) -> p c n", c=DC)
            for t in range(NT):
                pe.wait_ge(S("unit_free"), unit - 5)
                b = bank[UB[unit % 6]]
                for c in range(DC):
                    last = mm(b[:, :], hT[:, c, t * P:(t + 1) * P], w[:, c, :], start=(c == 0), stop=(c == DC - 1))
                    opened(last)
                last.then_inc(S("unit_ready"), 1)
                unit += 1
            w = take()[:, 0:4096].rearrange("p (c n) -> p c n", c=DC)
            for half in range(2):
                pe.wait_ge(S("unit_free"), unit - 5)
                b = bank[UB[unit % 6]]
                for mi in range(2):
                    m = 2 * half + mi
                    for c in range(DC):
                        last = mm(b[:, mi * TOK:(mi + 1) * TOK], w[:, c, m * P:(m + 1) * P], hT[:, c, :],
                                  start=(c == 0), stop=(c == DC - 1))
                        opened(last)
                last.then_inc(S("unit_ready"), 1)
                unit += 1

            mods = iter([(k, half) for k in range(4, 24) for half in range(2)])

            def fill(n):
                for _ in range(n):
                    k, half = next(mods, (None, None))
                    if k is not None:
                        vec, o = (col("c1", 0, 8), 4 * k) if k < 12 else (silc, 64 + 4 * (k - 12))
                        half_slice(k, half, vec, o + 2 * half)

            pe.wait_ge(S("unit_free"), 7)
            pe.wait_ge(S("gelu_done"), 4)
            pe.wait_ge(S("lora_in"), 32)
            pe.wait_ge(S("lowrank_ready"), 2)
            for half in range(2):
                for mi in range(2):
                    m = 2 * half + mi
                    ms = slice(m * P, (m + 1) * P)
                    o = slice(mi * TOK, (mi + 1) * TOK)
                    mm(bank[1 + half][:, o], lora[0:32, ms], xwa[0:32, :], start=True, stop=True)
                for mi in range(2):
                    m = 2 * half + mi
                    ms = slice(m * P, (m + 1) * P)
                    o = slice(mi * TOK, (mi + 1) * TOK)
                    mm(bank[3 + half][:, o], lora[32:64, ms], xwa[32:64, :], start=True, stop=True)
                for mi in range(2):
                    m = 2 * half + mi
                    ms = slice(m * P, (m + 1) * P)
                    o = slice(mi * TOK, (mi + 1) * TOK)
                    last = mm(bank[5 + half][:, o], g2s[0:96, ms], xg[0:96, :], start=True, stop=True)
                last.then_inc(S("lora_done"), 1)
            fill(4)
            pe.wait_ge(S("upper_made"), 3)
            pe.wait_ge(S("kk_sq"), 1)
            pe.wait_ge(S("sw_ready"), 4)
            for half in range(2):
                mm(bank[7][:, 0:512] if half else bank[1][:, 0:512], bones[:, :],
                   tmp1[:, 2 * half:2 * half + 2, :], start=True, stop=True).then_inc(S("kk_sums"), 1)
            fill(2)
            pe.wait_ge(S("ws_masked"), 1)
            pe.wait_ge(S("gv_ready"), 2)
            pe.wait_ge(S("a_ready"), 4)
            for m in range(NM):
                for hh in range(2):
                    for t in range(NT):
                        last = mm(bank[3 + m // 2][64 * hh:64 * hh + 64, ((m % 2) * 2 + t) * P:((m % 2) * 2 + t + 1) * P],
                                  gv[:, t, (2 * m + hh) * HD:(2 * m + hh + 1) * HD], wsT[:, 2 * m + hh, :],
                                  start=True, stop=True)
                if m % 2:
                    last.then_inc(S("mixed"), 1)
            fill(2)
            pe.wait_ge(S("bonus_in"), 1)
            pe.wait_ge(S("g_ready"), 2)
            for half in range(2):
                mm(bank[5 + half][:, 0:512], bones[:, :], tmp2[:, 2 * half:2 * half + 2, :],
                   start=True, stop=True).then_inc(S("bonus_sums"), 1)
            fill(2)
            pe.wait_ge(S("bk_ready"), 1)
            for q in range(3):
                for t in range(NT):
                    b = bank[1 + 2 * q + t]
                    if q == 1 and t == 0:
                        pe.wait_ge(S("ya_ready"), 1)
                    if q == 2 and t == 0:
                        pe.wait_ge(S("bonus_ready"), 2)
                    for m in range(NM):
                        src = vT if q == 0 else bkT[:, q - 1]
                        last = nc.tensor.transpose(b[:, m * P:(m + 1) * P], src[:, m, t * P:(t + 1) * P], ident[:, :])
                    last.then_inc(S("tok_turned"), 1)
            fill(2)
            pe.wait_ge(S("tok_copied"), 4)
            pe.wait_ge(S("tokb_copied"), 2)
            for i in range(16):
                T, h = i // 8, i % 8
                m, pb = h // 2, 64 * (h % 2)
                if i >= 6:
                    pe.wait_ge(S("gram_copied"), i - 5)
                b = bank[[1, 3, 2, 4, 7, 5][i % 6]]
                for q in range(2):
                    last = mm(b[:, q * 256:(q + 1) * 256].rearrange("p (w t) -> p w t", w=2),
                              bkT[pb:pb + 64, q, m, T * P:(T + 1) * P],
                              arT[pb:pb + 64, :, m, T * P:(T + 1) * P], start=True, stop=True)
                last.then_inc(S("gram_done"), 1)
                if i % 4 == 3:
                    fill(1)
            flush()
            pe.wait_ge(S("gram_copied"), 16)

            def inverse(T, between=()):
                for l in range(6):
                    for g in range(2):
                        n = T * 12 + l * 2 + g
                        pe.wait_ge(S("levels_made"), 1)
                        if l == 0 and T > 0:
                            pe.wait_ge(S("xt_ready"), T * 12 - 1 + g)
                        if l > 0:
                            pe.wait_ge(S("x_ready"), T * 10 + (l - 1) * 2 + g + 1)
                            pe.wait_ge(S("xt_ready"), T * 12 + (l - 1) * 2 + g + 1)
                        for j in range(4):
                            i = T * 8 + 4 * g + j
                            last = mm(bank[1 + 3 * g][:, j * P:(j + 1) * P], gram[:, i, 0:P],
                                      Xi[:, 4 * g + j, :] if l else ident[:, :], start=True, stop=True)
                        last.then_inc(S("ax_done"), 1)
                    fill(1)
                    for g in range(2):
                        n = T * 12 + l * 2 + g
                        pe.wait_ge(S("p_ready"), n + 1)
                        if 0 < l < 5:
                            for j in range(4):
                                last = mm(bank[1 + 3 * g][:, j * P:(j + 1) * P], XT[:, T * 8 + 4 * g + j, :],
                                          Pm[:, g, j, :], start=True, stop=True)
                            last.then_inc(S("xp_done"), 1)
                        for j in range(4):
                            o = bank[3 + 3 * g][:, j * P:(j + 1) * P]
                            old = XT[:, T * 8 + 4 * g + j, :] if l else ident[:, :]
                            last = mm(o, Pm[:, g, j, :], old, start=True, stop=True)
                        last.then_inc(S("xt_done"), 1)
                    fill(1)
                    if l < len(between):
                        for step in between[l]:
                            step()

            def v_terms(T):
                for h in range(8):
                    last = mm(bank[7][:, h * HD:(h + 1) * HD], gram[:, T * 8 + h, 256:384],
                              tokv[:, T, h * HD:(h + 1) * HD], start=(h == 0), stop=False, skip_group_check=True)
                last.then_inc(S("pv_done"), 1)

            def p_state(c):
                ps = slice(64 * (c % 2), 64 * (c % 2) + 64)
                pe.wait_ge(S("state_ready"), c)
                for m in range(NM):
                    last = mm(bank[7][ps, m * P:(m + 1) * P], arT[:, 0, m, c * CH:(c + 1) * CH],
                              Mst[:, m, :], start=False, stop=False, skip_group_check=True)
                last.then_inc(S("p_state"), 1)

            def u_of(c):
                T, ps = c // 2, slice(64 * (c % 2), 64 * (c % 2) + 64)
                pe.wait_ge(S("pb_ready"), c + 1)
                pe.wait_ge(S("xt_ready"), 12 * (T + 1))
                for h in range(8):
                    last = mm(bank[2][ps, h * HD:(h + 1) * HD], XT[:, T * 8 + h, ps], Pb[:, h * HD:(h + 1) * HD],
                              start=True, stop=True)
                last.then_inc(S("u_done"), 1)

            def d_state(c):
                T, ps = c // 2, slice(64 * (c % 2), 64 * (c % 2) + 64)
                pe.wait_ge(S("u_ready"), c + 1)
                for m in range(NM):
                    fs = slice(m * P, (m + 1) * P)
                    mm(bank[2][:, fs], tokb[ps, T, fs], U[ps, T, fs], start=True, stop=False)
                    last = mm(bank[2][:, fs], tokk[ps, T, fs], tokv[ps, T, fs], start=False, stop=True)
                last.then_inc(S("ds_done"), 1)

            def y_v(T):
                b = bank[5 + T]
                for hh in range(2):
                    for m in range(NM):
                        h = 2 * m + hh
                        mm(b[64 * hh:64 * hh + 64, m * P:(m + 1) * P], tokv[:, T, h * HD:(h + 1) * HD],
                           gram[:, T * 8 + h, 384:512], start=(m == 0), stop=False, skip_group_check=True)

            def y_state(c):
                T = c // 2
                for m in range(NM):
                    o = m * P + (c % 2) * CH
                    last = mm(bank[5 + T][:, o:o + CH], Mst[:, m, :], arT[:, 1, m, c * CH:(c + 1) * CH],
                              start=False, stop=False, skip_group_check=True)
                last.then_inc(S("y_state"), 1)

            def y_u(T):
                pe.wait_ge(S("u_ready"), 2 * T + 2)
                for hh in range(2):
                    for m in range(NM):
                        h = 2 * m + hh
                        last = mm(bank[5 + T][64 * hh:64 * hh + 64, m * P:(m + 1) * P], U[:, T, h * HD:(h + 1) * HD],
                                  gram[:, T * 8 + h, 128:256], start=False, stop=True, skip_group_check=True)
                last.then_inc(S("y_done"), 1)

            inverse(0)
            v_terms(0)
            y_v(0)
            inverse(1, ((lambda: u_of(0),), (lambda: d_state(0),),
                        (lambda: p_state(1), lambda: y_state(1)), (lambda: u_of(1),),
                        (lambda: d_state(1), lambda: y_u(0))))
            flush()
            pe.wait_ge(S("xt_ready"), 24)
            pe.wait_ge(S("pb_ready"), 2)
            v_terms(1)
            y_v(1)
            p_state(2)
            y_state(2)
            u_of(2)
            d_state(2)
            p_state(3)
            y_state(3)
            u_of(3)
            y_u(1)
            pe.wait_ge(S("yv_ready"), 2)
            for half in range(2):
                mm(bank[1 + half][:, :], bones[:, :], yv[:, 2 * half:2 * half + 2, :], start=True, stop=True)\
                    .then_inc(S("gn_mean"), 1)
            pe.wait_ge(S("ysq_ready"), 2)
            for half in range(2):
                mm(bank[3 + half][:, :], bones[:, :], ysq[:, 2 * half:2 * half + 2, :], start=True, stop=True)\
                    .then_inc(S("gn_var"), 1)
            def rows(src, n, b0, freed=None):
                pe.wait_ge(S("diag_ready"), n)
                if freed:
                    pe.wait_ge(S(freed[0]), freed[1])
                for k in range(2):
                    mm(bank[b0 + k][:, :], ones[:, :], src[:, 4 * k:4 * k + 4, :], start=True, stop=True)\
                        .then_inc(S("rows_done"), 1)

            ws = []
            for n in range(2):
                ws.append(take()[:, 0:4096].rearrange("p (c n) -> p c n", c=DC))
                if n == 0:
                    before = fresh[0]
            for n in range(2):
                for t in range(NT):
                    for c in range(4):
                        last = mm(bank[[1, 5][t] + n][:, :], yaT[:, c, t * P:(t + 1) * P], ws[n][:, c, :],
                                  start=(c == 0), stop=False)
                        if before and c == 0 and n == 0 and t == 0:
                            last.then_inc(S("slot_freed"), 1)
            pe.wait_ge(S("yb_ready"), 1)
            for t in range(NT):
                for n in range(2):
                    for c in range(4, 8):
                        last = mm(bank[[1, 5][t] + n][:, :], ybT[:, c - 4, t * P:(t + 1) * P], ws[n][:, c, :],
                                  start=False, stop=(c == 7))
                        if t == 1 and n == 1 and c == 4:
                            last.then_inc(S("slot_freed"), 1)
                last.then_inc(S("mix_done"), 1)
                if t == 0:
                    rows(diag[:, 0], 1, 3)
            fresh[0] = True
            rows(diag[:, 1], 2, 3, ("rows_copied", 2))
            rows(diag[:, 2], 3, 1, ("x1_ready", 2))
            rows(diag[:, 3], 4, 5)

            pe.wait_ge(S("h2_ready"), 2)
            for u in range(4):
                if u == 0:
                    pe.wait_ge(S("rows_copied"), 8)
                for cc in range(2):
                    for t in range(NT):
                        last = nc.tensor.transpose(bank[1 + u][:, (2 * cc + t) * P:(2 * cc + t + 1) * P],
                                                   h2[:, t, (2 * u + cc) * P:(2 * u + cc + 1) * P], ident[:, :])
                last.then_inc(S("turned"), 1)
            pe.wait_ge(S("h2T_ready"), 4)
            pe.wait_ge(S("router_in"), 48)
            for t in range(NT):
                for c in range(DC):
                    last = mm(bank[5][:, t * 64:t * 64 + 36], h2T[:, c, t * P:(t + 1) * P], rw[:, c, :],
                              start=(c == 0), stop=(c == DC - 1))
            last.then_inc(S("logits_done"), 1)
            pe.wait_ge(S("onehot_ready"), 2)
            oh = rt[:, 768:832].rearrange("p (t e) -> p t e", t=NT)
            mm(bank[6][:, 0:NE], upper[:, :], oh[:, 0], start=True, stop=True)
            mm(bank[6][:, NE:2 * NE], ones[:, :], oh[:, 0], start=True, stop=False)
            mm(bank[6][:, NE:2 * NE], upper[:, :], oh[:, 1], start=False, stop=True)
            mm(bank[6][:, 2 * NE:3 * NE], ones[:, :], oh[:, 0], start=True, stop=False)
            mm(bank[6][:, 2 * NE:3 * NE], ones[:, :], oh[:, 1], start=False, stop=True).then_inc(S("pos_done"), 1)
            pe.wait_ge(S("perm_ready"), 2)
            for c in range(DC):
                b = [1, 2, 3, 4][c % 4]
                if c >= 4:
                    pe.wait_ge(S("xs_copied"), c - 3)
                for t in range(NT):
                    last = mm(bank[b][:, :], h2[:, t, c * P:(c + 1) * P], perm[:, t, :], start=(t == 0), stop=(t == 1))
                last.then_inc(S("xs_done"), 1)
            pe.wait_ge(S("pw_ready"), 2)
            for s in range(4):
                for t in range(NT):
                    last = nc.tensor.transpose(bank[5 + s // 2][:, ((s % 2) * 2 + t) * P:((s % 2) * 2 + t + 1) * P],
                                               pw[:, t, s * P:(s + 1) * P], ident[:, :])
                if s % 2:
                    last.then_inc(S("pwt_done"), 1)
            pe.wait_ge(S("xs_copied"), 8)

            moe_n0 = st_pe.n
            for name in ("up_done", "down_done", "act_turned", "y_turned"):
                pe.nop().then_inc(S(name), 1)
            pe.wait_ge(S("pwt_copied"), 2)
            pe.wait_ge(S("mtab_ready"), 1)

            def window(slots, done, frees):
                def product(b, lhsT, w, n, first, last):
                    for half in range(2):
                        o = slice(64 * half, 64 * half + 64)
                        ins = mm(bank[b][o, 0:n], lhsT, w[:, half * n:(half + 1) * n], start=first, stop=last,
                                 tile_position=(0, 64 * half))
                    return ins

                for k, (name, free_sem) in enumerate((("gate_done", "silu_done"), ("up_done", "act_done"))):
                    w = slots(k, DC)
                    if k == 0:
                        pe.wait_ge(S("xw_ready"), done)
                    pe.wait_ge(S(free_sem), done)
                    for c in range(DC):
                        last = product(1 + k, xw[:, c, :], w[:, c, :], 256, c == 0, c == DC - 1)
                        if frees and c == 0:
                            last.then_inc(S("slot_freed"), 1)
                    last.then_inc(S(name), 1)
                pe.wait_ge(S("act_done"), done + 1)
                pe.wait_ge(S("actT_ready"), done)
                for j in range(2):
                    last = nc.tensor.transpose(bank[4][:, j * P:(j + 1) * P], actm[:, j * P:(j + 1) * P], ident[:, :])
                last.then_inc(S("act_turned"), 1)
                w = slots(2, 4)
                pe.wait_ge(S("actT_ready"), done + 1)
                pe.wait_ge(S("ym_ready"), done)
                for k in range(4):
                    last = product(3, actT[:, k % 2, 64 * (k // 2):64 * (k // 2) + 64], w[:, k, :], 512, k == 0, k == 3)
                    if frees and k == 0:
                        last.then_inc(S("slot_freed"), 1)
                last.then_inc(S("down_done"), 1)
                pe.wait_ge(S("ym_ready"), done + 1)
                pe.wait_ge(S("ys_copied"), done)
                for j in range(4):
                    last = nc.tensor.transpose(bank[5][:, j * P:(j + 1) * P], ym[:, j * P:(j + 1) * P], ident[:, :])
                last.then_inc(S("y_turned"), 1)

            with pe.Fori(0, NE // 2, 1) as i:
                for e in range(2):
                    extra = pe.value_load(mtab[0:1, bass.ds(i * 2 + (NE + e), 1)], min_val=0, max_val=3)
                    before = pe.value_load(mtab[0:1, bass.ds(i * 2 + (2 * NE + e), 1)], min_val=1, max_val=4 * NE)

                    def slots(k, chunks):
                        n = moe_n0 + 3 * e + k
                        pe.wait_ge(S(f"slot{n % RING}_loaded"), i * 16 + 16 * (n // RING + 1))
                        return ring[:, n % RING, :].rearrange("p (c n) -> p c n", c=chunks)

                    with pe.If(extra > 0):
                        with pe.Fori(0, extra, 1) as w:
                            window(slots, before + w, False)
                    window(slots, before + extra, True)
            st_pe.n += 3 * NE

            total = pe.value_load(mtab[0:1, 3 * NE:3 * NE + 1], min_val=1, max_val=4 * NE)
            pe.wait_ge(S("ys_copied"), total)
            for s in range(4):
                for k in range(2):
                    u = 2 * s + k
                    if u >= 6:
                        pe.wait_ge(S(f"yst_copied{k}"), s - 2)
                    for c in range(4):
                        last = nc.tensor.transpose(bank[1 + u % 6][:, c * P:(c + 1) * P],
                                                   ysT[:, 4 * k + c, s * P:(s + 1) * P], ident[:, :])
                    last.then_inc(S("ys_turned"), 1)
            pe.wait_ge(S("yst_copied0"), 4)
            pe.wait_ge(S("yst_copied1"), 4)
            for t in range(NT):
                for n in range(2):
                    for s in range(4):
                        last = mm(bank[1 + 2 * t + n][:, :], pwT[:, s, t * P:(t + 1) * P], ys[:, s, n * 512:(n + 1) * 512],
                                  start=(s == 0), stop=(s == 3))
                last.then_inc(S("moe_done"), 1)

            turns = [1]

            def turn_again(x3=None):
                turns[0] += 1
                n = turns[0]
                pe.wait_ge(S("xn_ready"), n)
                for t in range(NT):
                    if t == 1:
                        pe.wait_ge(S("xn_ready_s"), n)
                    for u in range(4):
                        if t == 0 and u == 2 and x3:
                            pe.wait_ge(S("x3_ready"), x3)
                        for cc in range(2):
                            last = nc.tensor.transpose(bank[1 + u][:, (2 * cc + t) * P:(2 * cc + t + 1) * P],
                                                       yt[:, t, (2 * u + cc) * P:(2 * u + cc + 1) * P], ident[:, :])
                        if t == 1:
                            last.then_inc(S("turned"), 1)
                return n

            mods1 = iter([(j, half) for j in range(12) for half in range(2)])

            def fill1(n):
                for _ in range(n):
                    j, half = next(mods1)
                    half_slice(24 + j, half, silc, 128 + 4 * j + 2 * half)

            fill1(4)
            for layer in range(2):
                h_n = turn_again()
                L8 = 4 * layer
                for q in range(4):
                    w = take()[:, 0:4096].rearrange("p (c n) -> p c n", c=DC)
                    for half in range(2):
                        u = 2 * q + half
                        if u >= 6:
                            pe.wait_ge(S("q_copied"), L8 + u - 5)
                        for mi in range(2):
                            m = 2 * half + mi
                            for c in range(DC):
                                if u == 0 and mi == 0:
                                    h_chunk(h_n, max(c, 1))
                                last = mm(bank[1 + u % 6][:, mi * TOK:(mi + 1) * TOK], w[:, c, m * P:(m + 1) * P],
                                          hTd[:, c, :], start=(c == 0), stop=(c == DC - 1))
                                opened(last)
                        last.then_inc(S("qk_done"), 1)
                for n in range(2):
                    w = take()[:, 0:4096].rearrange("p (c n) -> p c n", c=DC)
                    for t in range(NT):
                        u = 8 + 2 * n + t
                        if u < 10:
                            pe.wait_ge(S("q_copied"), L8 + u - 5)
                        else:
                            pe.wait_ge(S("k_copied"), L8 + u - 9)
                        for c in range(DC):
                            last = mm(bank[1 + u % 6][:, :], hTd[:, c, t * P:(t + 1) * P], w[:, c, :],
                                      start=(c == 0), stop=(c == DC - 1))
                            opened(last)
                        last.then_inc(S("v_done"), 1)
                if layer == 1:
                    pe.wait_ge(S("fg_in"), 16)
                    for c in range(DC):
                        last = mm(bank[7][0:NHA, 0:TOK], wfg[:, c, :], hTd[:, c, :], start=(c == 0), stop=(c == DC - 1))
                    last.then_inc(S("fg_done"), 1)
                pe.wait_ge(S("q_copied"), L8 + 4)
                pe.wait_ge(S("k_copied"), L8 + 4)
                pe.wait_ge(S("v_copied"), L8 + 4)
                rows(diagd, 5 + 2 * layer, 5)
                rows(diagd, 6 + 2 * layer, 5, ("rows_copied", 10 + 4 * layer))
                pe.wait_ge(S("neg_made"), 3)
                if layer == 1:
                    pe.wait_ge(S("cum_ready"), 1)
                A8 = 8 * layer

                def scores(m):
                    if m >= 2:
                        pe.wait_ge(S("prob_ready"), A8 + m - 1)
                    for hh in range(2):
                        h, pb = 2 * m + hh, 64 * hh
                        z = bank[1 + 2 * (m % 2) + hh]
                        hs = slice(pb, pb + 64)
                        if layer == 0:
                            mm(z[:, 0:256], KT[hs, m, 0:P], QT[hs, m, :], start=True, stop=False, skip_group_check=True)
                            last = mm(z[:, 256:384], KT[hs, m, P:TOK], QT[hs, m, P:TOK], start=False, stop=False,
                                      skip_group_check=True)
                        else:
                            mm(z[:, 0:128], QT[hs, m, 0:P], KT[hs, m, 0:P], start=True, stop=False, skip_group_check=True)
                            mm(z[:, 128:384], QT[hs, m, P:TOK], KT[hs, m, :], start=False, stop=False,
                               skip_group_check=True)
                            one = ident[0:NHA, h:h + 1]
                            last = mm(z[:, 0:128], one.broadcast_to([NHA, P]), ncumf[0:NHA, 0:P], start=False,
                                      stop=False, skip_group_check=True)
                            last = mm(z[:, 128:384], one.broadcast_to([NHA, P]), ncumf[0:NHA, :], start=False,
                                      stop=True, skip_group_check=True)
                    last.then_inc(S("z_done"), 1)

                def middle(m):
                    if layer == 0:
                        pe.wait_ge(S("sp_ready"), m + 1)
                        for hh in range(2):
                            z = bank[1 + 2 * (m % 2) + hh]
                            s_ = sp_[:, m % 2, hh, :]
                            mm(z[:, 0:384], neg_lower, s_, start=False, stop=False, skip_group_check=True)
                            last = mm(z[:, 128:256], neg_ones, s_[:, 256:384], start=False, stop=True,
                                      skip_group_check=True)
                        last.then_inc(S("sums_done"), 1)
                    else:
                        pe.wait_ge(S("prob_ready"), A8 + m + 1)
                        if m >= 1:
                            pe.wait_ge(S("pt_copied"), m)
                        for hh in range(2):
                            for k in range(3):
                                last = nc.tensor.transpose(bank[7 if hh else 0][:, k * P:(k + 1) * P],
                                                           pr[:, m % 2, hh, k * P:(k + 1) * P], ident[:, :])
                        last.then_inc(S("pt_done"), 1)

                def output(m):
                    if layer == 0:
                        pe.wait_ge(S("prob_ready"), A8 + m + 1)
                    else:
                        pe.wait_ge(S("pt_copied"), m + 1)
                    if m >= 2:
                        pe.wait_ge(S("o_copied"), A8 + m - 1)
                    else:
                        pe.wait_ge(S("rows_copied"), 12 + 4 * layer)
                    pt = (t1 if layer else pr)[:, m % 2]
                    for hh in range(2):
                        h = 2 * m + hh
                        o = bank[5 + m % 2][64 * hh:64 * hh + 64, 0:TOK]
                        mm(o, Vd[:, 0, h * HD:(h + 1) * HD], pt[:, hh, 0:256], start=True, stop=False,
                           skip_group_check=True)
                        last = mm(o[:, P:TOK], Vd[:, 1, h * HD:(h + 1) * HD], pt[:, hh, 256:384], start=False, stop=True,
                                  skip_group_check=True)
                    last.then_inc(S("o_done"), 1)

                for m in range(8 + 2):
                    if m < 8:
                        scores(m)
                        fill1(layer == 0)
                    if 1 <= m <= 8:
                        middle(m - 1)
                    if m < 8:
                        fill1(layer == 0)
                    if m >= 2:
                        output(m - 2)
                pe.wait_ge(S("o_copied"), A8 + 8)
                pe.wait_ge(S("prob_ready"), A8 + 8)
                w, before = [], None
                for n in range(2):
                    w.append(take()[:, 0:4096].rearrange("p (c n) -> p c n", c=DC))
                    if n == 0:
                        before = fresh[0]
                for t in range(NT):
                    for n in range(2):
                        for c in range(DC):
                            last = mm(bank[1 + 2 * t + n][:, :], oT[:, c, t * P:(t + 1) * P], w[n][:, c, :],
                                      start=(c == 0), stop=(c == DC - 1))
                            if c == 0 and ((t == 0 and n == 0 and before) or (t == 1 and n == 1)):
                                last.then_inc(S("slot_freed"), 1)
                    last.then_inc(S("proj_done"), 1)
                fresh[0] = True
                if layer == 0:
                    fill1(4)
                    flush()
                h_n = turn_again(2 + 2 * layer)

                n0 = st_pe.n
                F0 = NFT * layer

                def group_slots(n, i, w):
                    out = []
                    for k in range(3):
                        s = (n + k) % RING
                        out.append((S(f"slot{s}_loaded"), i * 16 + 16 * ((n + k) // RING + 1),
                                    ring[:, s, 0:8 * w].rearrange("p (c n) -> p c n", c=(DC, DC, w // P)[k])))
                    return out

                def gate_up(sl, j, f):
                    b = bank[5 + j % 2]
                    if j == 0:
                        pe.wait_ge(*sl[0][0:2])
                        pe.wait_ge(*sl[1][0:2])
                    if not isinstance(f, int) or f >= 2:
                        pe.wait_ge(S("act_f"), f - 1)
                    for k in range(2):
                        for c in range(DC):
                            if k == 0 and isinstance(f, int) and f == F0:
                                h_chunk(h_n, c)
                            last = mm(b[:, k * TOK:(k + 1) * TOK], sl[k][2][:, c, j * P:(j + 1) * P], hTd[:, c, :],
                                      start=(c == 0), stop=(c == DC - 1))
                            opened(last)
                    last.then_inc(S("gu_done"), 1)

                def down(sl, j, f, first=False, last_of=None, final=False):
                    if j == 0:
                        pe.wait_ge(*sl[2][0:2])
                    pe.wait_ge(S("act_f"), f + 1)
                    i = 0
                    for t in range(NT):
                        for n in range(2):
                            ins = mm(bank[1 + 2 * t + n][:, :], actF[:, 0, j % 2, t * P:(t + 1) * P],
                                     sl[2][2][:, j, n * 512:(n + 1) * 512], start=first, stop=final, skip_group_check=True)
                            if last_of and i in (0, 1, 3):
                                ins.then_inc(S("slot_freed"), 1)
                            i += 1

                fresh[0] = True
                g0 = group_slots(n0, 0, 512)
                gate_up(g0, 0, F0 + 0)
                gate_up(g0, 1, F0 + 1)
                down(g0, 0, F0 + 0, first=True)
                gate_up(g0, 2, F0 + 2)
                down(g0, 1, F0 + 1)
                gate_up(g0, 3, F0 + 3)
                down(g0, 2, F0 + 2)

                def middle_group(prev, n, i, f):
                    cur = group_slots(n, i, 512)
                    gate_up(cur, 0, f)
                    down(prev, 3, f - 1, last_of=True)
                    gate_up(cur, 1, f + 1)
                    down(cur, 0, f)
                    gate_up(cur, 2, f + 2)
                    down(cur, 1, f + 1)
                    gate_up(cur, 3, f + 3)
                    down(cur, 2, f + 2)
                    return cur

                with pe.Fori(0, 2, 1) as i:
                    prev = [(None, None, ring[:, (n0 + k) % RING, :].rearrange("p (c n) -> p c n", c=(DC, DC, 4)[k]))
                            for k in range(3)]
                    prev = middle_group(prev, n0 + 3, i, i * 8 + (F0 + 4))
                    middle_group(prev, n0 + 6, i, i * 8 + (F0 + 8))
                prev = [(None, None, ring[:, (n0 + 12 + k) % RING, :].rearrange("p (c n) -> p c n", c=(DC, DC, 4)[k]))
                        for k in range(3)]
                g5 = group_slots(n0 + 15, 0, 256)
                gate_up(g5, 0, F0 + 20)
                down(prev, 3, F0 + 19, last_of=True)
                gate_up(g5, 1, F0 + 21)
                down(g5, 0, F0 + 20)
                down(g5, 1, F0 + 21, last_of=True, final=True)
                st_pe.n += 18
                ahead[0] = True
                pe.wait_ge(S("slot_freed"), st_pe.n)
                pe.nop().then_inc(S("ffn_done"), 1)

        @block.vector
        def _(dve):
            V = nc.vector
            d = Chain(dve, S, "vector_step")

            squares = [0]

            def mean_square(src=None, dst=None):
                if src is None:
                    squares[0] += 1
                else:
                    d(V.tensor_tensor_reduce(out=dst, in0=src, in1=src, scale=1.0 / D, scalar=0.0, op0=ALU.mult,
                                             op1=ALU.add, accum_out=stat[:, 0:1]))
                squares[0] += 1
                dve.wait_ge(S("sq_done"), squares[0])
                d.to(V.tensor_scalar(stat[:, 0:2], stat[:, 0:2], RMS_EPS, None, ALU.add), "ms_ready")

            def scaled(dst, n):
                dve.wait_ge(S("rstd_ready"), n)
                d.to(V.tensor_scalar(dst[:, 0, :], x[:, 0, :], stat[:, 2:3], None, ALU.mult), "xn_ready")

            def gain(lm, sc0, g):
                d(V.scalar_tensor_tensor(out=fcol, in0=modc[:, lm, sc0:sc0 + 8], scalar=1.0, in1=g,
                                         op0=ALU.add, op1=ALU.mult))

            def evac_h(dst, lm, sh0, n):
                for c in (0, 1, 4, 5):
                    dve.wait_ge(S("turned"), n + c // 2 + 1)
                    o = (c % 2) * TOK
                    d.to(V.tensor_scalar(dst[:, c, :], bank[1 + c // 2][:, o:o + TOK], fcol[:, c:c + 1],
                                    modc[:, lm, sh0 + c:sh0 + c + 1], ALU.mult, ALU.add), "h_ready_v")

            d(V.memset(part, 0.0))
            dve.wait_ge(S("x_in"), 16)
            mean_square(x[:, 0, :], xn[:, 0, :])
            scaled(xn, 1)
            dve.wait_ge(S("cols_in"), 16)
            d(V.tensor_scalar(small[:, 0:14], cols[:, COLS["mu_rkv"][0]:COLS["mu_rkv"][0] + 14], -1.0, 1.0,
                              ALU.mult, ALU.add))
            d(V.tensor_scalar(omka, col("k_a", 0, 4), -1.0, 1.0, ALU.mult, ALU.add))
            for k in range(4):
                n = mod_at[k]
                dve.wait_ge(S(f"slot{n % RING}_loaded"), 16 * (n // RING + 1))
                if k >= 2:
                    dve.wait_ge(S("mod_cols"), k - 1)
                w = ring[:, n % RING, :].rearrange("p (c n) -> p c n", c=DC)
                out, vec = maccv[:, k % 2, :], col("c1", 0, 8)
                d(V.tensor_scalar(out, w[:, 0, :], vec[:, 0:1], None, ALU.mult))
                for c in range(1, DC):
                    ins = V.scalar_tensor_tensor(out=out, in0=w[:, c, :], scalar=vec[:, c:c + 1], in1=out,
                                                 op0=ALU.mult, op1=ALU.add)
                    d(ins) if c < DC - 1 else d.to(ins, "mod_sums")
            dve.wait_ge(S("mod_cols"), 4)
            d.to(V.tensor_tensor(modc[:, 0, 0:16], bank[0][:, 0:16], col("ada_b", 0, 16), ALU.add), "mod_copied")
            dve.wait_ge(S("mod_copied"), 1)
            gain(0, 8, col("norm1_g", 0, 8))
            d.to(V.tensor_copy(stat[:, 15:16], fcol[:, 0:1]), "fcol_ready")
            evac_h(hT, 0, 0, 0)

            UB = [1, 2, 3, 4, 5, 6]
            for u in range(7):
                b = bank[UB[u % 6]]
                dve.wait_ge(S("shift_ready"), 2 * u + 2)
                for mi in range(2):
                    if u < 6:
                        m = 2 * (u % 2) + mi
                        dst, mu = (rT, kT, vT)[u // 2][:, m, :], col("mu_rkv", (u // 2) * 4 + m)
                        rows_ = P
                    else:
                        dst, rows_ = (xwa, xg)[mi], (64, 96)[mi]
                        mu = col(("mu_wa", "mu_g")[mi])
                    o = mi * TOK
                    ins = V.scalar_tensor_tensor(out=dst[0:rows_, 1:TOK], in0=b[0:rows_, o:o + TOK - 1],
                                                 scalar=mu[0:rows_, :], in1=dst[0:rows_, 1:TOK],
                                                 op0=ALU.mult, op1=ALU.add)
                    if mi == 0:
                        d(ins)
                    else:
                        d.to(ins, "unit_free")
            dve.wait_ge(S("unit_free"), 7)
            for m in range(NM):
                d(V.tensor_scalar(kkn[:, m, :], kT[:, m, :], col("k_k", m), None, ALU.mult))
            d.to(V.tensor_tensor(tmp1, kkn, kkn, ALU.mult), "kk_sq")
            dve.wait_ge(S("masks_made"), 3)
            dve.wait_ge(S("sw_ready"), 4)
            for m in range(NM):
                d(V.tensor_tensor_scan(out=cum[:, m, :], data0=keep[:, :], data1=sw[:, m, :], initial=0.0,
                                       op0=ALU.mult, op1=ALU.add))
            d.to(V.tensor_tensor(sw, cum, sw, ALU.subtract), "cum_done")
            dve.wait_ge(S("a_ready"), 4)
            for m in range(NM):
                d(V.tensor_scalar(tmp2[:, m, :], aT[:, m, :], col("k_a", m), omka[:, m:m + 1], ALU.mult, ALU.add))
            d(V.tensor_tensor(kT, kT, tmp2, ALU.mult))
            for k in range(2):
                dve.wait_ge(S("kk_sums"), 2)
                d.to(V.tensor_scalar(tmp1[:, 2 * k:2 * k + 2, :], (bank[7] if k else bank[1]).rearrange("p (m t) -> p m t", m=2),
                                     1e-24, None, ALU.max), "kk_max")
            dve.wait_ge(S("gelu_done"), 4)
            d(V.tensor_scalar(stat[:, 6:8], stat[:, 4:6], 1.0 / HALF, None, ALU.mult))
            for t in range(NT):
                d(V.tensor_scalar(gv[:, t, :], gv[:, t, :], stat[:, 6 + t:7 + t], None, ALU.subtract))
                d(V.tensor_tensor_reduce(out=tmp2[:, 0:2, :].rearrange("p a b -> p (a b)"), in0=gv[:, t, :],
                                         in1=gv[:, t, :], scale=1.0 / HALF, scalar=LN_EPS, op0=ALU.mult, op1=ALU.add,
                                         accum_out=stat[:, t:t + 1]))
            d.to(V.tensor_copy(stat[:, 0:2], stat[:, 0:2]), "ms_ready")
            dve.wait_ge(S("kk_norm"), 1)
            d(V.tensor_tensor(kkn, kkn, tmp1, ALU.mult))
            dve.wait_ge(S("ln_in"), 64)
            dve.wait_ge(S("rstd_ready"), 2)
            for t in range(NT):
                d(V.scalar_tensor_tensor(out=gv[:, t, :], in0=gv[:, t, :], scalar=stat[:, 2 + t:3 + t], in1=lnw,
                                         op0=ALU.mult, op1=ALU.mult))
                d.to(V.tensor_tensor(gv[:, t, :], gv[:, t, :], lnb, ALU.add), "gv_ready")
            for m in range(NM):
                ins = V.scalar_tensor_tensor(out=tmp2[:, m, :], in0=rT[:, m, :], scalar=col("r_k", m), in1=kT[:, m, :],
                                             op0=ALU.mult, op1=ALU.mult)
                d(ins) if m < NM - 1 else d.to(ins, "bonus_in")
            dve.wait_ge(S("exps_done"), 3)
            d(V.tensor_copy(dend, eL.rearrange("p m (c t) -> p m c t", t=CH)[:, :, :, CH - 1:CH].squeeze(3)))
            for k in range(2):
                dve.wait_ge(S("mixed"), k + 1)
                v = bank[3 + k].rearrange("p (m t s) -> p m t s", m=2, t=NT)
                for mi in range(2):
                    m = 2 * k + mi
                    d(V.tensor_tensor(tmp1[:, m, :].rearrange("p (t s) -> p t s", t=NT), v[:, mi],
                                      bsb[:, m:m + 1, :].broadcast_to([P, NT, P]), ALU.add))
            d.to(V.tensor_tensor(yaT, yaT, tmp1, ALU.mult), "ya_ready")
            d(V.tensor_tensor(tmp1, kkn, aT, ALU.mult))
            d(V.scalar_tensor_tensor(out=arT[:, 0], in0=kkn, scalar=-1.0, in1=sw, op0=ALU.mult, op1=ALU.mult))
            d(V.tensor_tensor(arT[:, 1], rT, eL, ALU.mult))
            dve.wait_ge(S("ya_ready"), 1)
            d(V.tensor_tensor(bkT[:, 0], tmp1, cum, ALU.mult))
            d.to(V.tensor_tensor(bkT[:, 1], kT, cum, ALU.mult), "bk_ready")
            for half in range(2):
                dve.wait_ge(S("bonus_sums"), half + 1)
                d.to(V.tensor_tensor(bonus[:, 2 * half:2 * half + 2, :], bank[5 + half].rearrange("p (m t) -> p m t", m=2),
                                vT[:, 2 * half:2 * half + 2, :], ALU.mult), "bonus_ready")
            for t in range(NT):
                dve.wait_ge(S("tok_turned"), 3 + t)
                d.to(V.tensor_copy(tokb[:, t, :], bank[3 + t][:, :]), "tokb_copied")
            dve.wait_ge(S("bonus_ready"), 2)
            dve.wait_ge(S("tok_copied"), 4)
            for i in range(16):
                dve.wait_ge(S("gram_done"), i + 1)
                b = bank[[1, 3, 2, 4, 7, 5][i % 6]]
                d.to(V.tensor_tensor(gram[:, i, :].rearrange("p (q w) -> p q w", q=2), b.rearrange("p (q w) -> p q w", q=2),
                                mask_ar[:, :, :].rearrange("p w t -> p (w t)").unsqueeze(1).broadcast_to([P, 2, 2 * P]),
                                ALU.mult), "gram_copied")
            dve.wait_ge(S("levels_made"), 1)
            dve.wait_ge(S("mod_cols"), 20)
            d.to(V.tensor_tensor(modc[:, 0, 16:48], bank[0][:, 16:48], col("ada_b", 16, 32), ALU.add), "mod_copied")
            d(V.memset(Pb, 0.0))
            b4 = lambda t_: t_.unsqueeze(1).broadcast_to([P, 4, P])

            def pb_of(c):
                ps = slice(64 * (c % 2), 64 * (c % 2) + 64)
                dve.wait_ge(S("p_state") if c else S("pv_done"), c or 1)
                d.to(V.tensor_copy(Pb[ps, :], bank[7][ps, :]), "pb_ready")

            def u_of(c):
                ps = slice(64 * (c % 2), 64 * (c % 2) + 64)
                dve.wait_ge(S("u_done"), c + 1)
                d.to(V.tensor_copy(U[ps, c // 2, :], bank[2][ps, :]), "u_ready")

            def state_of(c):
                for m in range(NM):
                    d(V.tensor_scalar(DCm[:, m, :], bones[:, :], dend[:, m, c:c + 1], None, ALU.mult))
                dve.wait_ge(S("ds_done"), c + 1)
                ds = bank[2].rearrange("p (m v) -> p m v", m=NM)
                if c > 0:
                    d(V.tensor_tensor(Mst, Mst, ds, ALU.add))
                    ds = Mst
                d.to(V.tensor_tensor(Mst, ds, DCm, ALU.mult), "state_ready")

            def y_of(T):
                dve.wait_ge(S("y_done"), T + 1)
                d.to(V.tensor_copy(yv[:, :, T * P:(T + 1) * P], bank[5 + T].rearrange("p (m t) -> p m t", m=NM)), "yv_ready")

            def inverse(T, between=()):
                for l in range(6):
                    for g in range(2):
                        n = T * 12 + l * 2 + g
                        dve.wait_ge(S("ax_done"), n + 1)
                        if n >= 2:
                            dve.wait_ge(S("xt_done"), n - 1)
                        d.to(V.tensor_tensor(Pm[:, g], bank[1 + 3 * g].rearrange("p (j t) -> p j t", j=4),
                                        b4(level[:, l, :]), ALU.mult), "p_ready")
                    for g in range(2):
                        n = T * 12 + l * 2 + g
                        xs = Xi[:, 4 * g:4 * g + 4, :]
                        if l == 0:
                            dve.wait_ge(S("p_ready"), n + 1)
                            d.to(V.tensor_tensor(xs, Pm[:, g], b4(ident[:, :]), ALU.add), "x_ready")
                        elif l < 5:
                            dve.wait_ge(S("xp_done"), T * 8 + (l - 1) * 2 + g + 1)
                            d.to(V.tensor_tensor(xs, xs, bank[1 + 3 * g].rearrange("p (j t) -> p j t", j=4),
                                            ALU.add), "x_ready")
                    for g in range(2):
                        n = T * 12 + l * 2 + g
                        xt = XT[:, T * 8 + 4 * g:T * 8 + 4 * g + 4, :]
                        dve.wait_ge(S("xt_done"), n + 1)
                        d.to(V.tensor_tensor(xt, xt if l else b4(ident[:, :]),
                                             bank[3 + 3 * g].rearrange("p (j t) -> p j t", j=4), ALU.add), "xt_ready")
                    if l < len(between):
                        for step in between[l]:
                            step()

            inverse(0)
            pb_of(0)
            inverse(1, ((lambda: u_of(0),), (lambda: state_of(0),), (lambda: pb_of(1),), (lambda: u_of(1),),
                        (lambda: state_of(1), lambda: y_of(0))))
            pb_of(2)
            u_of(2)
            state_of(2)
            pb_of(3)
            u_of(3)
            y_of(1)
            dve.wait_ge(S("yv_ready"), 2)
            for half in range(2):
                hs = slice(2 * half, 2 * half + 2)
                dve.wait_ge(S("gn_mean"), half + 1)
                d(V.scalar_tensor_tensor(out=yd[:, hs], in0=bank[1 + half].rearrange("p (m t) -> p m t", m=2),
                                         scalar=-1.0 / HD, in1=yv[:, hs], op0=ALU.mult, op1=ALU.add))
                d.to(V.tensor_tensor(ysq[:, hs], yd[:, hs], yd[:, hs], ALU.mult), "ysq_ready")
            dve.wait_ge(S("gn_std"), 1)
            d(V.tensor_tensor(yd, yd, yv, ALU.mult))
            for m in range(NM):
                d(V.tensor_scalar(yd[:, m, :], yd[:, m, :], col("gn_w", m), col("gn_b", m), ALU.mult, ALU.add))
            d(V.tensor_tensor(yd, yd, bonus, ALU.add))
            d.to(V.tensor_tensor(ybT, yd, gT, ALU.mult), "yb_ready")

            def mod_columns(layer):
                dve.wait_ge(S("mod_cols"), 44 + 24 * layer)
                d.to(V.tensor_tensor(modc[:, 1 + layer, :], bank[0][:, 64 * (1 + layer):64 * (1 + layer) + 48],
                                     col(f"b_mod{layer}", 0, 48), ALU.add), "mod_copied")

            mod_columns(0)
            n_diag = [0]

            def make_diag(dst, vec):
                d.to(V.tensor_tensor(dst, ident[:, :].unsqueeze(1).broadcast_to([P, DC, P]),
                                vec.unsqueeze(2).broadcast_to([P, DC, P]), ALU.mult), "diag_ready")
                n_diag[0] += 1

            dve.wait_ge(S("mod_copied"), 2)
            gain(0, 32, col("norm2_g", 0, 8))
            for k, vec in enumerate((modc[:, 0, 16:24], fcol, modc[:, 0, 24:32], modc[:, 0, 40:48])):
                make_diag(diag[:, k], vec)
            dve.wait_ge(S("rows_copied"), 2)
            for t in range(NT):
                dve.wait_ge(S("mix_done"), t + 1)
                y = psum[:, 1 + 4 * t:3 + 4 * t, :].rearrange("p b n -> p (b n)")
                d(V.tensor_tensor(h2[:, t, :], y, gate1b, ALU.mult))
                d.to(V.tensor_tensor(x[:, t, :], x[:, t, :], h2[:, t, :], ALU.add), "x1_ready")
            dve.wait_ge(S("x1_ready"), 2)
            mean_square(x[:, 0, :], h2[:, 0, :])
            dve.wait_ge(S("rstd_ready"), 3)
            dve.wait_ge(S("rows_copied"), 6)
            for t in range(NT):
                d(V.scalar_tensor_tensor(out=h2[:, t, :], in0=x[:, t, :], scalar=stat[:, 2 + t:3 + t], in1=sc2b,
                                         op0=ALU.mult, op1=ALU.mult))
                d.to(V.tensor_tensor(h2[:, t, :], h2[:, t, :], sh2b, ALU.add), "h2_ready")
            dve.wait_ge(S("logits_done"), 1)
            dve.wait_ge(S("router_in"), 48)
            dve.wait_ge(S("iota_made"), 1)
            f1 = lambda o: rt[:, o:o + 1]
            for t in range(NT):
                o = 128 * t
                L, G8, m8 = rt[:, o:o + 36], rt[:, o + 40:o + 48], rt[:, o + 48:o + 56]
                i8 = rt[:, o + 56:o + 64].bitcast(U32)
                sel, s8, si = rt[:, o + 64:o + 72], rt[:, o + 72:o + 80], rt[:, o + 80:o + 88].bitcast(U32)
                ohg = rt[:, o + 88:o + 92]
                gf, gs, dd, i1, i2 = f1(o + 92), f1(o + 93), f1(o + 94), f1(o + 95), f1(o + 96)
                e1, e2, w1, w2, ng = f1(o + 97), f1(o + 98), f1(o + 99), f1(o + 100), f1(o + 101)
                p1 = f1(o + 102)
                d(V.tensor_tensor(L, bank[5][:, t * 64:t * 64 + 36], rb, ALU.add))
                d(V.memset(G8, NEG))
                d(V.tensor_copy(G8[:, 0:4], L[:, 0:4]))
                d(V.max(m8, G8))
                d(V.max_index(i8, m8, G8))
                d(V.tensor_copy(gf, i8[:, 0:1]))
                d.to(V.tensor_scalar(ng, m8[:, 0:1], -1.0, None, ALU.mult), "g_max")
                d(V.tensor_scalar(ohg, iota[:, 0:4], gf, None, ALU.is_equal))
                d(V.tensor_scalar(sel, L[:, 4:12], ohg[:, 0:1], None, ALU.mult))
                for g in range(1, NG):
                    d(V.scalar_tensor_tensor(out=sel, in0=L[:, 4 + 8 * g:12 + 8 * g], scalar=ohg[:, g:g + 1], in1=sel,
                                             op0=ALU.mult, op1=ALU.add))
                d(V.max(s8, sel))
                d(V.max_index(si, s8, sel))
                d.to(V.tensor_tensor(dd, s8[:, 1:2], s8[:, 0:1], ALU.subtract), "e_gap")
                d(V.tensor_copy(i1, si[:, 0:1]))
                d(V.tensor_copy(i2, si[:, 1:2]))
                d(V.scalar_tensor_tensor(out=e1, in0=gf, scalar=float(EPG), in1=i1, op0=ALU.mult, op1=ALU.add))
                d(V.scalar_tensor_tensor(out=e2, in0=gf, scalar=float(EPG), in1=i2, op0=ALU.mult, op1=ALU.add))
                oh1, oh2 = rt[:, 256 + 64 * t:288 + 64 * t], rt[:, 288 + 64 * t:320 + 64 * t]
                d(V.tensor_scalar(oh1, iota[:, 0:NE], e1, None, ALU.is_equal))
                d(V.tensor_scalar(oh2, iota[:, 0:NE], e2, None, ALU.is_equal))
                d.to(V.tensor_tensor(rt[:, 768 + NE * t:768 + NE * (t + 1)], oh1, oh2, ALU.add), "onehot_ready")
                dve.wait_ge(S("g_sum"), t + 1)
                d(V.reciprocal(gs, gs))
                dve.wait_ge(S("e_exp"), t + 1)
                d(V.tensor_scalar(p1, dd, 1.0, None, ALU.add))
                d(V.reciprocal(p1, p1))
                d(V.tensor_tensor(w1, gs, p1, ALU.mult))
                d(V.tensor_tensor(w2, w1, dd, ALU.mult))
            cnt, inc_, st = rt[:, 400:432], rt[:, 432:464], rt[:, 464:496]
            dve.wait_ge(S("pos_done"), 1)
            d(V.tensor_copy(cnt, bank[6][:, 2 * NE:3 * NE]))
            d(V.tensor_tensor_scan(out=inc_, data0=ones[:, 0:NE], data1=cnt, initial=0.0, op0=ALU.mult, op1=ALU.add))
            d(V.tensor_tensor(st, inc_, cnt, ALU.subtract))
            for t in range(NT):
                o = 128 * t
                base, tr = rt[:, 496 + 32 * t:528 + 32 * t], rt[:, 560:592]
                d(V.tensor_tensor(base, bank[6][:, t * NE:(t + 1) * NE], st, ALU.add))
                for k in range(2):
                    d(V.tensor_tensor_reduce(out=tr, in0=rt[:, 256 + 64 * t + 32 * k:288 + 64 * t + 32 * k], in1=base,
                                             scale=1.0, scalar=0.0, op0=ALU.mult, op1=ALU.add, accum_out=f1(o + 104 + k)))
                d(V.tensor_scalar(perm[:, t, :], iota, f1(o + 104), None, ALU.is_equal))
                d.to(V.scalar_tensor_tensor(out=perm[:, t, :], in0=iota, scalar=f1(o + 105), in1=perm[:, t, :],
                                       op0=ALU.is_equal, op1=ALU.add), "perm_ready")
            ex, pa = rt[:, 592:624], rt[:, 624:656]
            d(V.tensor_scalar(ex, cnt, float(WIN), None, ALU.is_gt))
            for k in (2, 3):
                d(V.scalar_tensor_tensor(out=ex, in0=cnt, scalar=float(k * WIN), in1=ex, op0=ALU.is_gt, op1=ALU.add))
            d(V.tensor_scalar(inc_, ex, 1.0, None, ALU.add))
            d(V.tensor_tensor_scan(out=pa, data0=ones[:, 0:NE], data1=inc_, initial=0.0, op0=ALU.mult, op1=ALU.add))
            d(V.tensor_scalar(mtab[0:1, 3 * NE:3 * NE + 1], pa[0:1, NE - 1:NE], 1.0, None, ALU.add))
            d(V.tensor_tensor(pa, pa, inc_, ALU.subtract))
            d(V.tensor_scalar(pa, pa, 1.0, None, ALU.add))
            dve.nop().then_inc(S("act_done"), 1)
            d(V.tensor_copy(mtab[0:1, 0:NE], st[0:1, :]))
            d(V.tensor_copy(mtab[0:1, NE:2 * NE], ex[0:1, :]))
            d.to(V.tensor_copy(mtab[0:1, 2 * NE:3 * NE], pa[0:1, :]), "mtab_ready")
            for t in range(NT):
                o = 128 * t
                d(V.tensor_scalar(pw[:, t, :], iota, f1(o + 104), f1(o + 99), ALU.is_equal, ALU.mult))
                d(V.tensor_scalar(pw_second, iota, f1(o + 105), f1(o + 100),
                                  ALU.is_equal, ALU.mult))
                d.to(V.tensor_tensor(pw[:, t, :], pw[:, t, :], pw_second, ALU.add), "pw_ready")
            for c in range(DC):
                dve.wait_ge(S("xs_done"), c + 1)
                d.to(V.tensor_copy(xsT[:, c, 0:SLOTS], bank[1 + c % 4][:, :]), "xs_copied")
            dve.nop().then_inc(S("actT_ready"), 1)
            dve.wait_ge(S("mtab_ready"), 1)
            dve.wait_ge(S("xs_copied"), 8)
            dve.wait_ge(S("iota_made"), 2)

            def act_pass(start, done):
                dve.wait_ge(S("up_done"), done)
                V.tensor_copy(xw, xsT[:, :, bass.ds(start, WIN)]).then_inc(S("xw_ready"), 1)
                dve.wait_ge(S("silu_done"), done + 1)
                dve.wait_ge(S("up_done"), done + 1)
                dve.wait_ge(S("act_turned"), done)
                V.tensor_tensor(actm, bank[2][:, 0:4 * WIN], sg, ALU.mult).then_inc(S("act_done"), 1)
                dve.wait_ge(S("act_turned"), done + 1)
                dve.wait_ge(S("down_done"), done)
                V.tensor_copy(actT.rearrange("p a b -> p (a b)"), bank[4][:, 0:4 * WIN]).then_inc(S("actT_ready"), 1)

            within = "the passes of an expert begin within its slots"
            with dve.Fori(0, NE, 1) as i:
                start = dve.value_load(mtab[0:1, bass.ds(i, 1)], min_val=0, max_val=SLOTS)
                extra = dve.value_load(mtab[0:1, bass.ds(i + NE, 1)], min_val=0, max_val=3)
                before = dve.value_load(mtab[0:1, bass.ds(i + 2 * NE, 1)], min_val=1, max_val=4 * NE)
                with dve.If(extra > 0):
                    with dve.Fori(0, extra, 1) as w:
                        act_pass(nc.s_assert_within(start + w * WIN, 0, SLOTS, skip_runtime_bounds_check_because=within),
                                 before + w)
                act_pass(nc.s_assert_within(start + extra * WIN, 0, SLOTS, skip_runtime_bounds_check_because=within),
                         before + extra)
            for s in range(4):
                dve.wait_ge(S("ys_turned"), 2 * s + 1)
                d.to(V.tensor_copy(ys[:, s, 0:512], bank[1 + (2 * s) % 6][:, :]), "yst_copied0")
            for t in range(NT):
                dve.wait_ge(S("moe_done"), t + 1)
                y = psum[:, 1 + 2 * t:3 + 2 * t, :].rearrange("p b n -> p (b n)")
                if t == 0:
                    dve.wait_ge(S("moe_done"), 2)
                d(V.tensor_tensor(ys[:, t, :], y, gate2b, ALU.mult))
                d.to(V.tensor_tensor(x[:, t, :], x[:, t, :], ys[:, t, :], ALU.add), "x2_sum")
            dve.wait_ge(S("x2_sum"), 2)
            mean_square(x[:, 0, :], ys[:, 0, :])
            dve.wait_ge(S("rstd_ready"), 4)
            for t in range(NT):
                d.to(V.scalar_tensor_tensor(out=x[:, t, :], in0=x[:, t, :], scalar=stat[:, 2 + t:3 + t], in1=fgb,
                                       op0=ALU.mult, op1=ALU.mult), "x2_ready")

            rn = 5
            for layer in range(2):
                lm = 1 + layer
                dve.wait_ge(S("x2_ready") if layer == 0 else S("x4_ready"), 2)
                mean_square(x[:, 0, :], yt[:, 0, :])
                if layer == 1:
                    mod_columns(1)
                gain(lm, 8, col("g_mix_pre", 8 * layer, 8))
                d.to(V.tensor_copy(stat[:, 15:16], fcol[:, 0:1]), "fcol_ready")
                scaled(yt, rn)
                rn += 1
                evac_h(hTd, lm, 0, 8 + 8 * layer)
                for u in range(4):
                    dve.wait_ge(S("qk_done"), 8 * layer + 5 + u)
                    d.to(V.tensor_copy(KT[:, 2 * u:2 * u + 2, :], bank[1 + (4 + u) % 6].rearrange("p (m t) -> p m t", m=2)), "k_copied")
                for k, (nm, dst) in enumerate((("g_mix_post", 16), ("g_ffn_post", 40))):
                    dve.wait_ge(S("rows_done"), 2 * n_diag[0])
                    d(V.tensor_tensor(spare, modc[:, lm, dst:dst + 8], col(nm, 8 * layer, 8), ALU.mult))
                    make_diag(diagd, spare)
                if layer == 1:
                    dve.wait_ge(S("fg_done"), 1)
                    H_ = slice(0, NHA)
                    u_, v_ = ncumf[H_, :], cumf[H_, :]
                    d(V.tensor_scalar(u_, bank[7][H_, 0:TOK], col("b_fg")[H_, :], -1.0, ALU.add, ALU.mult))
                    d(V.tensor_scalar(v_, u_, 0.0, None, ALU.max))
                    d.to(V.scalar_tensor_tensor(out=v_, in0=v_, scalar=-2.0, in1=u_, op0=ALU.mult, op1=ALU.add), "fg_abs")
                    dve.wait_ge(S("fg_log"), 1)
                    d(V.scalar_tensor_tensor(out=v_, in0=u_, scalar=0.0, in1=v_, op0=ALU.max, op1=ALU.add))
                    dve.wait_ge(S("neg_made"), 3)
                    d(V.tensor_tensor_scan(out=u_, data0=keep1, data1=v_, initial=0.0, op0=ALU.mult, op1=ALU.add))
                    d.to(V.tensor_scalar(v_, u_, -1.0, None, ALU.mult), "cum_ready")
                A8 = 8 * layer
                for m in range(8 + 2):
                    if layer == 1 and 1 <= m <= 8:
                        k = m - 1
                        dve.wait_ge(S("exp_done"), k + 1)
                        sm = small[:, 80 + 4 * (k % 2):84 + 4 * (k % 2)].rearrange("p (h t) -> p h t", h=2)
                        d(V.reciprocal(sm, sm))
                        d(V.tensor_tensor(pr[:, k % 2, :, 0:128], pr[:, k % 2, :, 0:128],
                                          sm[:, :, 0:1].broadcast_to([P, 2, 128]), ALU.mult))
                        d.to(V.tensor_tensor(pr[:, k % 2, :, 128:384], pr[:, k % 2, :, 128:384],
                                        sm[:, :, 1:2].broadcast_to([P, 2, 256]), ALU.mult), "prob_ready")
                    if m < 8:
                        dve.wait_ge(S("z_done"), A8 + m + 1)
                        dve.wait_ge(S("neg_made"), 3)
                        z = psum[:, 1 + 2 * (m % 2):3 + 2 * (m % 2), 0:384]
                        for hh in range(2):
                            zd = z[:, hh, :].rearrange("p (b s) -> p b s", b=3)[:, 0:3:2, :]
                            neg = (neg_gt if layer else neg_ge).unsqueeze(1).broadcast_to([P, 2, P])
                            d(V.tensor_tensor(zd, zd, neg, ALU.add))
                        if layer == 0:
                            if m >= 2:
                                dve.wait_ge(S("sums_done"), m - 1)
                            d(V.tensor_scalar(sp_[:, m % 2], z, 0.0, None, ALU.max))
                            d.to(V.scalar_tensor_tensor(out=t1[:, m % 2], in0=sp_[:, m % 2], scalar=-2.0, in1=z,
                                                        op0=ALU.mult, op1=ALU.add), "abs_done")
                            dve.wait_ge(S("log_done"), m + 1)
                            d.to(V.tensor_tensor(sp_[:, m % 2], sp_[:, m % 2], t1[:, m % 2], ALU.add), "sp_ready")
                        else:
                            ng = stat[:, 4 + 4 * (m % 2):8 + 4 * (m % 2)].rearrange("p (h t) -> p h t", h=2)
                            if m >= 2:
                                dve.wait_ge(S("exp_done"), m - 1)
                            d(V.tensor_reduce(ng[:, :, 0:1], z[:, :, 0:128], AX.X, ALU.max))
                            d(V.tensor_reduce(ng[:, :, 1:2], z[:, :, 128:384], AX.X, ALU.max))
                            d.to(V.tensor_scalar(ng, ng, -1.0, None, ALU.mult), "neg_max")
                    if m >= 2:
                        dve.wait_ge(S("o_done"), A8 + m - 1)
                        d.to(V.tensor_copy(oT[:, m - 2, :], bank[5 + m % 2][:, 0:TOK]), "o_copied")

                def post(rowsb, n):
                    y = [psum[:, 1 + 2 * t:3 + 2 * t, :].rearrange("p b n -> p (b n)") for t in range(NT)]
                    mean_square()
                    dve.wait_ge(S("rstd_ready"), n)
                    for t in range(NT):
                        d(V.scalar_tensor_tensor(out=yt[:, t, :], in0=y[t], scalar=stat[:, 2 + t:3 + t],
                                                 in1=rowsb, op0=ALU.mult, op1=ALU.mult))
                        ins = V.tensor_tensor(x[:, t, :], x[:, t, :], yt[:, t, :], ALU.add)
                        d.to(ins, "x3_ready" if rowsb is gmixb else "x4_ready" if layer == 0 else "out_ready")

                gain(lm, 32, col("g_ffn_pre", 8 * layer, 8))
                d.to(V.tensor_copy(stat[:, 15:16], fcol[:, 0:1]), "fcol_ready")
                for t in range(NT):
                    y = psum[:, 1 + 2 * t:3 + 2 * t, :].rearrange("p b n -> p (b n)")
                    mine = stat[:, t:t + 1]
                    squares[0] += 1
                    dve.wait_ge(S("sq_done"), squares[0])
                    d.to(V.tensor_scalar(mine, mine, RMS_EPS, None, ALU.add), "ms_ready")
                    dve.wait_ge(S("rows_copied"), 12 + 4 * layer)
                    dve.wait_ge(S("rstd_ready"), rn)
                    rn += 1
                    d(V.scalar_tensor_tensor(out=yt[:, t, :], in0=y, scalar=stat[:, 2 + t:3 + t],
                                             in1=gmixb, op0=ALU.mult, op1=ALU.mult))
                    d.to(V.tensor_tensor(x[:, t, :], x[:, t, :], yt[:, t, :], ALU.add), "x3_ready")
                    if t == 0:
                        d(V.tensor_tensor_reduce(out=yt[:, 0, :], in0=x[:, 0, :], in1=x[:, 0, :], scale=1.0 / D,
                                                 scalar=0.0, op0=ALU.mult, op1=ALU.add, accum_out=mine))
                    else:
                        squares[0] += 1
                        dve.wait_ge(S("sq_done"), squares[0])
                    d.to(V.tensor_scalar(mine, mine, RMS_EPS, None, ALU.add), "ms_ready")
                    if t == 0:
                        scaled(yt, rn)
                    rn += 1
                evac_h(hTd, lm, 24, 12 + 8 * layer)

                F0 = NFT * layer
                cb, ww = COLS["b_conv"][0] + NFT * layer, COLS["w_conv"][0] + 66 * layer

                def conv(f, r):
                    z = bank[5 + r]
                    dve.wait_ge(S("silu_f"), f + (F0 + 1))
                    dve.wait_ge(S("gu_done"), f + (F0 + 1))
                    c = cv[:, r, :]
                    w = lambda k: cols[:, bass.ds(f + (ww + NFT * k), 1)]
                    V.tensor_scalar(c, z[:, 0:TOK], w(2), cols[:, bass.ds(f + cb, 1)], ALU.mult, ALU.add)\
                        .then_inc(S("conv_step"), 1)
                    dve.wait_ge(S("conv_step"), f * 2 + (2 * F0 + 1))
                    V.scalar_tensor_tensor(out=c[:, 1:TOK], in0=z[:, 0:TOK - 1], scalar=w(1), in1=c[:, 1:TOK],
                                           op0=ALU.mult, op1=ALU.add).then_inc(S("conv_step"), 1)
                    dve.wait_ge(S("conv_step"), f * 2 + (2 * F0 + 2))
                    V.scalar_tensor_tensor(out=c[:, 2:TOK], in0=z[:, 0:TOK - 2], scalar=w(0), in1=c[:, 2:TOK],
                                           op0=ALU.mult, op1=ALU.add).then_inc(S("conv_done"), 1)

                def gated(f, r):
                    dve.wait_ge(S("silu_f"), f + (F0 + 3))
                    V.tensor_tensor(actF[:, 0, r, :], sv[:, r, :], bank[5 + r][:, TOK:2 * TOK], ALU.mult)\
                        .then_inc(S("act_f"), 1)

                with dve.Fori(0, NFT // 2, 1) as i:
                    for r in range(2):
                        conv(i * 2 + r, r)
                        gated(i * 2 + r, r)
                dve.wait_ge(S("ffn_done"), layer + 1)
                post(gffnb, rn)
                rn += 1

        @block.scalar
        def _(act):
            A = nc.scalar.activation
            a_ = Chain(act, S, "scalar_step")
            act.wait_ge(S("cols_in"), 16)
            a_.to(A(silc, col("c2", 0, 8), ACT.Silu), "silu_c")
            act.nop().then_inc(S("silu_f"), 2)
            act.nop().then_inc(S("silu_done"), 1)
            act.nop().then_inc(S("ys_copied"), 1)

            def evac_h(dst, lm, sh0, n, fc):
                act.wait_ge(S("fcol_ready"), fc)
                for c in (2, 3, 6, 7):
                    act.wait_ge(S("turned"), n + c // 2 + 1)
                    o = (c % 2) * TOK
                    a_.to(A(dst[:, c, :], bank[1 + c // 2][:, o:o + TOK], ACT.Identity, bias=modc[:, lm, sh0 + c:sh0 + c + 1],
                      scale=fcol[:, c:c + 1]), "h_ready_s")

            def square(src, dst, t=1):
                flat = lambda v: v if len(v.shape) == 2 else v.rearrange("p a b -> p (a b)")
                a_.to(A(flat(dst), flat(src), ACT.Square, scale=D ** -0.5, accum_out=stat[:, t:t + 1]), "sq_done")

            def scaled(dst, n):
                act.wait_ge(S("rstd_ready"), n)
                a_.to(A(dst[:, 1, :], x[:, 1, :], ACT.Copy, scale=stat[:, 3:4]), "xn_ready_s")

            parts = [0]

            def part_copy(n):
                for _ in range(n):
                    u = parts[0]
                    act.wait_ge(S("part_done"), u + 1)
                    if u >= 2:
                        act.wait_ge(S("mod_cols"), 4 + u - 1)
                    a_.to(A(macc[:, u % 2, :], part, ACT.Copy), "part_copied")
                    parts[0] += 1

            act.wait_ge(S("x_in"), 16)
            square(x[:, 1, :], xn[:, 1, :])
            scaled(xn, 1)
            evac_h(hT, 0, 0, 0, 1)
            UB = [1, 2, 3, 4, 5, 6]
            for u in range(7):
                b = bank[UB[u % 6]]
                act.wait_ge(S("unit_ready"), u + 1)
                for mi in range(2):
                    if u < 6:
                        m = 2 * (u % 2) + mi
                        dst, k, rows_ = (rT, kT, vT)[u // 2][:, m, :], (u // 2) * 4 + m, P
                    else:
                        dst, k, rows_ = (xwa, xg)[mi], 12 + mi, (64, 96)[mi]
                    a_.to(A(dst[0:rows_, :], b[0:rows_, mi * TOK:(mi + 1) * TOK], ACT.Copy,
                      scale=omm[0:rows_, k:k + 1]), "shift_ready")
            act.wait_ge(S("unit_free"), 7)
            a_.to(A(xwa[0:32, :], xwa[0:32, :], ACT.Tanh), "lowrank_ready")
            a_.to(A(xg[0:96, :], xg[0:96, :], ACT.Sigmoid), "lowrank_ready")
            for u in range(7, 11):
                act.wait_ge(S("unit_ready"), u + 1)
                b = bank[UB[u % 6]]
                if u < 9:
                    a_.to(A(gv[:, u - 7, :], b[:, :], ACT.Gelu_apprx_tanh, accum_out=stat[:, 4 + u - 7:5 + u - 7]), "gelu_done")
                else:
                    h_ = 2 * (u - 9)
                    a_.to(A(yaT[:, h_:h_ + 2, :], b.rearrange("p (m t) -> p m t", m=2), ACT.Gelu_apprx_tanh), "gelu_done")
            act.wait_ge(S("lora_done"), 2)
            for nm, dst, b0, bias in (("sw_ready", sw, 1, "w0"), ("a_ready", aT, 3, "a0")):
                for m in range(NM):
                    A(dst[:, m, :], bank[b0 + m // 2][:, (m % 2) * TOK:(m % 2 + 1) * TOK], ACT.Sigmoid,
                      bias=col(bias, m)).then_inc(S(nm), 1)
            for k in range(2):
                a_.to(A(gT[:, 2 * k:2 * k + 2, :], bank[5 + k].rearrange("p (m t) -> p m t", m=2), ACT.Copy), "g_ready")
            part_copy(4)
            act.wait_ge(S("kk_max"), 2)
            a_(A(tmp1, tmp1, ACT.Ln))
            a_.to(A(tmp1, tmp1, ACT.Exp, scale=-0.5), "kk_norm")
            part_copy(2)
            act.wait_ge(S("cum_done"), 1)
            a_.to(A(eL, cum, ACT.Exp, scale=-DECAY), "exps_done")
            act.wait_ge(S("exps_done"), 1)
            a_.to(A(cum, cum, ACT.Exp, scale=DECAY), "exps_done")
            a_.to(A(sw, sw, ACT.Exp, scale=-DECAY), "exps_done")
            part_copy(4)
            for q, dst in ((0, tokv), (2, tokk)):
                for t in range(NT):
                    act.wait_ge(S("tok_turned"), 2 * q + t + 1)
                    a_.to(A(dst[:, t, :], bank[1 + 2 * q + t][:, :], ACT.Copy), "tok_copied")
            part_copy(6)
            part_copy(24)
            act.wait_ge(S("gn_var"), 2)
            act.wait_ge(S("ysq_ready"), 2)
            a_(A(yv, psum[:, 3:5, :].rearrange("p b (m t) -> p (b m) t", m=2), ACT.Ln, bias=gneps, scale=1.0 / HD))
            a_.to(A(yv, yv, ACT.Exp, scale=-0.5), "gn_std")

            def row_copies(dst, n, b0):
                for k in range(2):
                    act.wait_ge(S("rows_done"), 2 * (n - 1) + k + 1)
                    a_.to(A(dst[:, 512 * k:512 * (k + 1)], bank[b0 + k][:, :], ACT.Copy), "rows_copied")

            act.wait_ge(S("mix_done"), 1)
            row_copies(gate1b, 1, 3)
            row_copies(sc2b, 2, 3)
            act.wait_ge(S("x1_ready"), 2)
            square(x[:, 1, :], h2[:, 1, :])
            row_copies(sh2b, 3, 1)
            row_copies(gate2b, 4, 5)
            for u in range(4):
                act.wait_ge(S("turned"), 4 + u + 1)
                a_.to(A(h2T[:, 2 * u:2 * u + 2, :], bank[1 + u].rearrange("p (m t) -> p m t", m=2), ACT.Copy), "h2T_ready")
            for t in range(NT):
                o = 128 * t
                act.wait_ge(S("g_max"), t + 1)
                a_.to(A(rt[:, o + 40:o + 44], rt[:, o:o + 4], ACT.Exp, bias=rt[:, o + 101:o + 102],
                  accum_out=rt[:, o + 93:o + 94]), "g_sum")
                act.wait_ge(S("e_gap"), t + 1)
                a_.to(A(rt[:, o + 94:o + 95], rt[:, o + 94:o + 95], ACT.Exp), "e_exp")
            for k in range(2):
                act.wait_ge(S("pwt_done"), k + 1)
                a_.to(A(pwT[:, 2 * k:2 * k + 2, :], bank[5 + k].rearrange("p (m t) -> p m t", m=2), ACT.Copy), "pwt_copied")
            act.wait_ge(S("mtab_ready"), 1)
            act.wait_ge(S("iota_made"), 2)
            act.nop().then_inc(S("ym_ready"), 1)

            def pass_(start, done):
                act.wait_ge(S("gate_done"), done)
                act.wait_ge(S("act_done"), done)
                A(sg, bank[1][:, 0:4 * WIN], ACT.Silu).then_inc(S("silu_done"), 1)
                act.wait_ge(S("down_done"), done + 1)
                act.wait_ge(S("y_turned"), done)
                A(ym, bank[3][:, :], ACT.Copy).then_inc(S("ym_ready"), 1)
                act.wait_ge(S("y_turned"), done + 1)
                act.wait_ge(S("ys_copied"), done)
                A(ysT[:, :, bass.ds(start, WIN)].rearrange("p (h j) w -> p j h w", h=2),
                  bank[5].rearrange("p (j h w) -> p j h w", j=4, h=2), ACT.Copy).then_inc(S("ys_copied"), 1)

            within = "the passes of an expert begin within its slots"
            with act.Fori(0, NE, 1) as i:
                start = act.value_load(mtab[0:1, bass.ds(i, 1)], min_val=0, max_val=SLOTS)
                extra = act.value_load(mtab[0:1, bass.ds(i + NE, 1)], min_val=0, max_val=3)
                before = act.value_load(mtab[0:1, bass.ds(i + 2 * NE, 1)], min_val=1, max_val=4 * NE)
                with act.If(extra > 0):
                    with act.Fori(0, extra, 1) as w:
                        pass_(nc.s_assert_within(start + w * WIN, 0, SLOTS, skip_runtime_bounds_check_because=within),
                              before + w)
                pass_(nc.s_assert_within(start + extra * WIN, 0, SLOTS, skip_runtime_bounds_check_because=within),
                      before + extra)
            for s in range(4):
                act.wait_ge(S("ys_turned"), 2 * s + 2)
                a_.to(A(ys[:, s, 512:1024], bank[1 + (2 * s + 1) % 6][:, :], ACT.Copy), "yst_copied1")
            part_copy(2)
            act.wait_ge(S("x2_sum"), 2)
            square(x[:, 1, :], ys[:, 1, :])
            part_copy(2)
            for layer in range(2):
                lm = 1 + layer
                act.wait_ge(S("x4_ready" if layer else "x2_ready"), 2)
                square(x[:, 1, :], yt[:, 1, :])
                scaled(yt, 5 + 6 * layer)
                evac_h(hTd, lm, 0, 8 + 8 * layer, 2 + 2 * layer)
                for u in range(4):
                    act.wait_ge(S("qk_done"), 8 * layer + 1 + u)
                    a_.to(A(QT[:, 2 * u:2 * u + 2, :], bank[1 + u].rearrange("p (m t) -> p m t", m=2), ACT.Copy,
                      scale=HD ** -0.5), "q_copied")
                for u in range(4):
                    act.wait_ge(S("v_done"), 4 * layer + 1 + u)
                    a_.to(A(Vd[:, u % 2, 512 * (u // 2):512 * (u // 2 + 1)], bank[1 + (8 + u) % 6][:, :], ACT.Copy), "v_copied")
                row_copies(gmixb, 5 + 2 * layer, 5)
                row_copies(gffnb, 6 + 2 * layer, 5)
                A8 = 8 * layer
                if layer == 1:
                    H_ = slice(0, NHA)
                    act.wait_ge(S("fg_abs"), 1)
                    a_(A(cumf[H_, :], cumf[H_, :], ACT.Exp))
                    a_.to(A(cumf[H_, :], cumf[H_, :], ACT.Ln, bias=onecol[H_, :]), "fg_log")
                for m in range(8 + 2):
                    if layer == 0:
                        if m < 8:
                            part_copy(1)
                            act.wait_ge(S("abs_done"), m + 1)
                            a_(A(t1[:, m % 2], t1[:, m % 2], ACT.Exp))
                            a_.to(A(t1[:, m % 2], t1[:, m % 2], ACT.Ln, bias=onecol), "log_done")
                        if 1 <= m <= 8:
                            k = m - 1
                            act.wait_ge(S("sums_done"), k + 1)
                            if k >= 2:
                                act.wait_ge(S("o_done"), A8 + k - 1)
                            z = psum[:, 1 + 2 * (k % 2):3 + 2 * (k % 2), 0:384]
                            a_.to(A(pr[:, k % 2], z, ACT.Exp), "prob_ready")
                        if m < 8:
                            part_copy(1)
                    else:
                        if m < 8:
                            act.wait_ge(S("neg_max"), m + 1)
                            if m >= 2:
                                act.wait_ge(S("pt_done"), m - 1)
                            for hh in range(2):
                                z = bank[1 + 2 * (m % 2) + hh]
                                for t in range(NT):
                                    zs = slice(128, 384) if t else slice(0, 128)
                                    k = 2 * hh + t
                                    ins = A(pr[:, m % 2, hh, zs], z[:, zs], ACT.Exp,
                                            bias=stat[:, 4 + 4 * (m % 2) + k:5 + 4 * (m % 2) + k],
                                            accum_out=small[:, 80 + 4 * (m % 2) + k:81 + 4 * (m % 2) + k])
                                    a_(ins) if k < 3 else a_.to(ins, "exp_done")
                        if 1 <= m <= 8:
                            k = m - 1
                            act.wait_ge(S("pt_done"), k + 1)
                            if k >= 2:
                                act.wait_ge(S("o_done"), A8 + k - 1)
                            a_(A(t1[:, k % 2, 0], bank[0][:, 0:384], ACT.Copy))
                            a_.to(A(t1[:, k % 2, 1], bank[7][:, 0:384], ACT.Copy), "pt_copied")
                act.wait_ge(S("proj_done"), 1 + 2 * layer)
                square(psum[:, 1:3, :], hTd[:, 0:4, :], 0)
                act.wait_ge(S("proj_done"), 2 + 2 * layer)
                square(psum[:, 3:5, :], hTd[:, 4:8, :])
                if layer == 0:
                    part_copy(4)
                act.wait_ge(S("x3_ready"), 2 + 2 * layer)
                square(x[:, 1, :], yt[:, 1, :])
                scaled(yt, 9 + 6 * layer)
                evac_h(hTd, lm, 24, 12 + 8 * layer, 3 + 2 * layer)
                F0 = NFT * layer
                with act.Fori(0, NFT // 2, 1) as i:
                    for r in range(2):
                        act.wait_ge(S("conv_done"), i * 2 + (F0 + r + 1))
                        A(sv[:, r, :], cv[:, r, :], ACT.Silu).then_inc(S("silu_f"), 1)
                act.wait_ge(S("ffn_done"), layer + 1)
                square(psum[:, 1:3, :], hTd[:, 0:4, :], 0)
                square(psum[:, 3:5, :], hTd[:, 4:8, :])


def column_pack(v):
    out = np.zeros((P, NCOL), np.float32)

    def put(name, w):
        o, n = COLS[name]
        out[:w.shape[0], o:o + w.shape[1]] = w

    full = lambda w: np.reshape(w, (-1, P)).T
    mu = v["rwkv_mu"][0]
    put("c1", full(v["c"]))
    put("ada_b", full(v["ada_b"]))
    put("norm1_g", full(v["norm1_g"]))
    put("mu_rkv", full(mu[:3 * HALF]))
    put("mu_wa", mu[3 * HALF:3 * HALF + 64][:, None])
    put("mu_g", mu[3 * HALF + 64:][:, None])
    for name in ("w0", "a0", "k_k", "k_a", "r_k", "gn_w", "gn_b"):
        put(name, full(v["rwkv_" + name]))
    put("norm2_g", full(v["norm2_g"]))
    put("c2", full(v["c_2"]))
    for layer in range(2):
        put(f"b_mod{layer}", full(v["b_mod_2"][layer]))
    for name in ("g_mix_pre", "g_mix_post", "g_ffn_pre", "g_ffn_post", "w_conv", "b_conv"):
        put(name, full(v[name + "_2"]))
    put("b_fg", v["b_fg_2"][0][:, None])
    return out


def kernel(**v):
    import concourse.bacc as bacc
    from concourse.bass_utils import run_bass_kernel_spmd

    v = {k: np.asarray(w) for k, w in v.items()}
    cont = np.ascontiguousarray
    arrays = {
        "cols": column_pack(v),
        "x": v["x"][0],
        "ada_w": v["ada_w"][0],
        "w_in": v["w_in"][0],
        "lora": cont(np.concatenate([v["rwkv_w2"][0], v["rwkv_a2"][0]], axis=0)),
        "g2": v["rwkv_g2"][0],
        "ln_w": v["gmlp_ln_w"][0],
        "ln_b": v["gmlp_ln_b"][0],
        "bs": cont(np.reshape(v["gmlp_bs"][0], (NM, 2, P)).transpose(1, 0, 2)),
        "ws": cont(v["gmlp_ws"][0].transpose(2, 0, 1)),
        "w_out": v["w_out"][0],
        "router_w": cont(np.concatenate([v["router_group_w"][0], v["router_expert_w"][0]], axis=1)),
        "router_b": cont(np.concatenate([v["router_group_b"][0], v["router_expert_b"][0]])),
        "moe_gate": v["moe_w_gate"][0],
        "moe_up": v["moe_w_up"][0],
        "moe_down": v["moe_w_down"][0],
        "final_g": v["final_norm_g"],
        "w_fg": v["w_fg_2"][0],
    }
    for layer in range(2):
        arrays[f"w_mod{layer}"] = v["w_mod_2"][layer]
        arrays[f"w_qkv{layer}"] = v["w_qkv_2"][layer]
        arrays[f"w_o{layer}"] = v["w_o_2"][layer]
        for k in ("gate", "up", "down"):
            arrays[f"w_ffn_{k}{layer}"] = v[f"w_ffn_{k}_2"][layer]
    nc = bacc.Bacc("TRN2", target_bir_lowering=False, num_devices=1)
    aps = {k: nc.dram_tensor("in_" + k, w.shape, mybir.dt.from_np(w.dtype), kind="ExternalInput").ap()
           for k, w in arrays.items()}
    aps["out"] = nc.dram_tensor("out", (TOK, D), F32, kind="ExternalOutput").ap()
    build_program(nc, aps)
    r = run_bass_kernel_spmd(nc, [{"in_" + k: w for k, w in arrays.items()}], core_ids=[0])
    return np.reshape(r.results[0]["out"], (1, TOK, D))
```
